# Optimizing a Trainium2 kernel written in Bass

```python
import math
import jax, jax.numpy as jnp
from jax import lax
import numpy as np

D_MODEL = 1024
BATCH = 1
SEQ = 128
DEPTH = 1
DEC_BATCH = 1
DEC_SEQ = 256
PAST_LEN = 128

GRID_W = 64
N_HEADS = 8
HEAD_DIM = 64
V_DIM = 2 * HEAD_DIM
AXIS_DIM = HEAD_DIM // 2
ROPE_THETA = 10000.0
N_FOURIER_GROUPS = 4
FOURIER_GROUP = D_MODEL // N_FOURIER_GROUPS
D_FF = 2816
N_EXPERTS = 8
TOP_K = 2
Q_BLOCK = 128
EPS = 1e-6
SUBLN_EPS = 1e-5
N_MOD = 6
LAMBDA_INIT_0 = 0.8 - 0.6 * math.exp(-0.3 * 0)

kernel_name = "hybrid_diffattn_fnet_prefix_diffusion_step"

F32 = jnp.float32

def rmsnorm(x, g, eps=EPS):
    xf = x.astype(F32)
    y = xf * lax.rsqrt(jnp.mean(xf * xf, axis=-1, keepdims=True) + eps)
    return (y * g.astype(F32)).astype(x.dtype)

def adaln(cond, w, b, dtype):
    m = jax.nn.silu(cond.astype(F32)) @ w.astype(F32) + b.astype(F32)
    m = m.reshape(cond.shape[0], 1, N_MOD, D_MODEL).astype(dtype)
    return tuple(m[:, :, i] for i in range(N_MOD))

def modulate(h, shift, scale):
    return h * (1.0 + scale) + shift

def axial_rope_tables(length):
    rows = length // GRID_W
    row = jnp.repeat(jnp.arange(rows), GRID_W).astype(F32)
    col = jnp.tile(jnp.arange(GRID_W), rows).astype(F32)
    inv = 1.0 / (ROPE_THETA ** (jnp.arange(0, AXIS_DIM, 2, dtype=F32) / AXIS_DIM))
    ar = row[:, None] * inv[None, :]
    ac = col[:, None] * inv[None, :]
    ang = jnp.concatenate([ar, ar, ac, ac], axis=-1)
    return jnp.cos(ang), jnp.sin(ang)

def apply_axial_rope(x, cos, sin):
    xf = x.astype(F32)
    hf = AXIS_DIM // 2
    rot = jnp.concatenate([-xf[..., hf:AXIS_DIM], xf[..., :hf],
                           -xf[..., AXIS_DIM + hf:], xf[..., AXIS_DIM:AXIS_DIM + hf]], axis=-1)
    c = cos[:, None, None, :]
    s = sin[:, None, None, :]
    return (xf * c + rot * s).astype(x.dtype)

def diff_lambda(lq1, lk1, lq2, lk2, lambda_init):
    return (jnp.exp(jnp.sum(lq1.astype(F32) * lk1.astype(F32)))
            - jnp.exp(jnp.sum(lq2.astype(F32) * lk2.astype(F32))) + lambda_init)

def diff_project(h, w_qkv):
    b, l, _ = h.shape
    q, k, v = jnp.split(h @ w_qkv, 3, axis=-1)
    return (q.reshape(b, l, N_HEADS, 2, HEAD_DIM),
            k.reshape(b, l, N_HEADS, 2, HEAD_DIM),
            v.reshape(b, l, N_HEADS, V_DIM))

def diff_attend(q, k, v, lam):
    b, lq = q.shape[:2]
    nb = lq // Q_BLOCK
    qb = q.reshape(b, nb, Q_BLOCK, N_HEADS, 2, HEAD_DIM).transpose(1, 0, 2, 3, 4, 5)
    vf = v.astype(F32)
    scale = HEAD_DIM ** -0.5

    def one_block(qblk):
        s = jnp.einsum('bqhmd,bkhmd->bhmqk', qblk, k, preferred_element_type=F32) * scale
        p = jax.nn.softmax(s, axis=-1)
        a = p[:, :, 0] - lam * p[:, :, 1]
        return jnp.einsum('bhqk,bkhe->bqhe', a, vf)

    o = lax.map(one_block, qb)
    return o.transpose(1, 0, 2, 3, 4).reshape(b, lq, N_HEADS, V_DIM).astype(q.dtype)

def diff_out(o, subln_g, w_o, lambda_init):
    b, l = o.shape[:2]
    o = rmsnorm(o, subln_g, SUBLN_EPS) * (1.0 - lambda_init)
    return o.reshape(b, l, N_HEADS * V_DIM) @ w_o

def fourier_mix(h, w_f):
    b, l, d = h.shape
    hg = h.astype(F32).reshape(b, l, N_FOURIER_GROUPS, FOURIER_GROUP)
    f = jnp.fft.fft2(hg, axes=(1, 3), norm='ortho').real
    return f.reshape(b, l, d).astype(h.dtype) @ w_f

def swiglu(h, w_gu, w_down):
    g, u = jnp.split(h @ w_gu, 2, axis=-1)
    return (jax.nn.silu(g) * u) @ w_down

def moe_swiglu(h, w_router, w_gu_e, w_down_e):
    shp = h.shape
    hf = h.reshape(-1, D_MODEL)
    probs = jax.nn.softmax((hf @ w_router).astype(F32), axis=-1)
    topv, topi = lax.top_k(probs, TOP_K)
    topv = topv / jnp.sum(topv, axis=-1, keepdims=True)
    gates = jnp.sum(jax.nn.one_hot(topi, N_EXPERTS, dtype=F32) * topv[..., None], axis=1)
    out = jnp.zeros(hf.shape, F32)
    for e in range(N_EXPERTS):
        out = out + gates[:, e:e + 1] * swiglu(hf, w_gu_e[e], w_down_e[e]).astype(F32)
    return out.reshape(shp).astype(h.dtype)

def setup_inputs(seed: int = 0) -> dict:
    key = jax.random.key(seed)
    ks = iter(jax.random.split(key, 40))
    nrm = lambda shape, s: jax.random.normal(next(ks), shape, F32) * s
    gain = lambda n: 1.0 + 0.02 * jax.random.normal(next(ks), (n,), F32)
    d = D_MODEL
    inv_d = d ** -0.5
    return {
        "x_prompt": nrm((BATCH, SEQ, d), 1.0),
        "x_sample": nrm((DEC_BATCH, DEC_SEQ, d), 1.0),
        "c": nrm((DEC_BATCH, d), 1.0),
        "cache_k_0": nrm((DEC_BATCH, PAST_LEN, N_HEADS, 2 * HEAD_DIM), 1.0),
        "cache_v_0": nrm((DEC_BATCH, PAST_LEN, N_HEADS, V_DIM), 1.0),
        "c_ctx": nrm((d,), 1.0),
        "ada_w_0": nrm((d, N_MOD * d), 0.5 * inv_d),
        "ada_b_0": nrm((N_MOD * d,), 0.02),
        "norm1_g_0": gain(d),
        "norm2_g_0": gain(d),
        "w_qkv_0": nrm((d, 3 * N_HEADS * 2 * HEAD_DIM), inv_d),
        "lambda_q1_0": nrm((HEAD_DIM,), 0.1),
        "lambda_k1_0": nrm((HEAD_DIM,), 0.1),
        "lambda_q2_0": nrm((HEAD_DIM,), 0.1),
        "lambda_k2_0": nrm((HEAD_DIM,), 0.1),
        "subln_g_0": gain(V_DIM),
        "w_o_0": nrm((N_HEADS * V_DIM, d), inv_d),
        "w_gu_0": nrm((d, 2 * D_FF), inv_d),
        "w_down_0": nrm((D_FF, d), D_FF ** -0.5),
        "ada_w_1": nrm((d, N_MOD * d), 0.5 * inv_d),
        "ada_b_1": nrm((N_MOD * d,), 0.02),
        "norm1_g_1": gain(d),
        "norm2_g_1": gain(d),
        "w_fourier_1": nrm((d, d), inv_d),
        "w_router_1": nrm((d, N_EXPERTS), inv_d),
        "w_gu_e_1": nrm((N_EXPERTS, d, 2 * D_FF), inv_d),
        "w_down_e_1": nrm((N_EXPERTS, D_FF, d), D_FF ** -0.5),
        "final_norm_g": gain(d),
    }

def reference(x_prompt, x_sample, c, cache_k_0, cache_v_0, c_ctx,
              ada_w_0, ada_b_0, norm1_g_0, norm2_g_0, w_qkv_0,
              lambda_q1_0, lambda_k1_0, lambda_q2_0, lambda_k2_0, subln_g_0, w_o_0,
              w_gu_0, w_down_0,
              ada_w_1, ada_b_1, norm1_g_1, norm2_g_1, w_fourier_1,
              w_router_1, w_gu_e_1, w_down_e_1,
              final_norm_g):
    lam0 = diff_lambda(lambda_q1_0, lambda_k1_0, lambda_q2_0, lambda_k2_0, LAMBDA_INIT_0)

    x = x_prompt
    bp, lp, _ = x.shape
    s1, sc1, g1, s2, sc2, g2 = adaln(c_ctx[None, :], ada_w_0, ada_b_0, x.dtype)
    h = modulate(rmsnorm(x, norm1_g_0), s1, sc1)
    q, k, v = diff_project(h, w_qkv_0)
    o = diff_attend(q, k, v, lam0)
    x = x + g1 * diff_out(o, subln_g_0, w_o_0, LAMBDA_INIT_0)
    k_ctx_0 = k.reshape(bp, lp, N_HEADS, 2 * HEAD_DIM)
    v_ctx_0 = v
    x = x + g2 * swiglu(modulate(rmsnorm(x, norm2_g_0), s2, sc2), w_gu_0, w_down_0)

    s1, sc1, g1, s2, sc2, g2 = adaln(c_ctx[None, :], ada_w_1, ada_b_1, x.dtype)
    x = x + g1 * fourier_mix(modulate(rmsnorm(x, norm1_g_1), s1, sc1), w_fourier_1)
    x = x + g2 * moe_swiglu(modulate(rmsnorm(x, norm2_g_1), s2, sc2), w_router_1, w_gu_e_1, w_down_e_1)
    y_prompt = rmsnorm(x, final_norm_g)

    x = x_sample
    bs, ls, _ = x.shape
    cos, sin = axial_rope_tables(ls)
    s1, sc1, g1, s2, sc2, g2 = adaln(c, ada_w_0, ada_b_0, x.dtype)
    h = modulate(rmsnorm(x, norm1_g_0), s1, sc1)
    q, k, v = diff_project(h, w_qkv_0)
    q = apply_axial_rope(q, cos, sin)
    k = apply_axial_rope(k, cos, sin)
    pl = cache_k_0.shape[1]
    k_all = jnp.concatenate([k, cache_k_0.reshape(bs, pl, N_HEADS, 2, HEAD_DIM).astype(k.dtype)], axis=1)
    v_all = jnp.concatenate([v, cache_v_0.astype(v.dtype)], axis=1)
    o = diff_attend(q, k_all, v_all, lam0)
    x = x + g1 * diff_out(o, subln_g_0, w_o_0, LAMBDA_INIT_0)
    x = x + g2 * swiglu(modulate(rmsnorm(x, norm2_g_0), s2, sc2), w_gu_0, w_down_0)

    s1, sc1, g1, s2, sc2, g2 = adaln(c, ada_w_1, ada_b_1, x.dtype)
    x = x + g1 * fourier_mix(modulate(rmsnorm(x, norm1_g_1), s1, sc1), w_fourier_1)
    x = x + g2 * moe_swiglu(modulate(rmsnorm(x, norm2_g_1), s2, sc2), w_router_1, w_gu_e_1, w_down_e_1)
    y_sample = rmsnorm(x, final_norm_g)

    return (y_prompt, y_sample, k_ctx_0, v_ctx_0)


_drawn_inputs = setup_inputs


def setup_inputs(seed=0):
    import zlib

    import numpy as np

    out = dict(_drawn_inputs(seed))
    spreads = {}
    factors = {'norm1_g_0': 3.117,
     'norm2_g_0': 5.082,
     'lambda_k1_0': 3.571,
     'lambda_q2_0': 3.299,
     'lambda_k2_0': 4.447,
     'subln_g_0': 8.0,
     'norm1_g_1': 52.994,
     'norm2_g_1': 8.987,
     'final_norm_g': 9.599,
     'cache_k_0': 8.0,
     'cache_v_0': 8.0}
    for name, (base, spread) in spreads.items():
        noise = np.random.default_rng([zlib.crc32(name.encode()), seed]).standard_normal(out[name].shape)
        drawn = base * np.exp(spread * noise) if base else spread * noise
        out[name] = __import__('jax').numpy.asarray(drawn.astype(out[name].dtype))
    for name, factor in factors.items():
        out[name] = (out[name] * factor).astype(out[name].dtype)
    return out
```

```python
from contextlib import ExitStack

import numpy as np

import concourse.bass as bass
from concourse import mybir

F32 = mybir.dt.float32
F32R = mybir.dt.float32r
I32 = mybir.dt.int32
U32 = mybir.dt.uint32
ALU = mybir.AluOpType
ACT = mybir.ActivationFunctionType
AX = mybir.AxisListType

P = 128
D = 1024
KC = D // P
TILES = 3
TOK = TILES * P
COND = (0, 1, 1)
HEADS = 8
HD = 64
D_FF = 2816
N_EXP = 8
FFC = D_FF // 256
EPS = 1e-6
SUBLN_EPS = 1e-5
LAMBDA_INIT = 0.2
SCALE = HD ** -0.5
HALF = 512

UNIT = 2048
RAW = 6
RING = 3


def ffn_units():
    out = []
    for c in range(FFC):
        out += [("gu", c, 0), ("gu", c, 1)]
        if c:
            out.append(("down", c - 1, 0))
    return out + [("down", FFC - 1, 0)]


FFN_UNITS = ffn_units()
NU = len(FFN_UNITS)


def ada_slots(steps, groups, double):
    todo = [(g, k) for g in groups for k in range(KC)]
    out = []
    for s in range(steps):
        n = 2 if s < double else 1
        out.append(todo[:n])
        todo = todo[n:]
    assert not todo
    return out


QKV_UNITS = [("qkv", n, kh) for n in range(6) for kh in range(2)]
QKV_ADA = ada_slots(len(QKV_UNITS), (1, 2), 4)
FFN_ADA = ada_slots(NU, (3, 4, 5), 0)


def stream_before_experts():
    s = [("ada", 0, k) for k in range(KC)]
    for u, more in zip(QKV_UNITS, QKV_ADA):
        s += [u] + [("ada", g, k) for g, k in more]
    s += [("wo", n, kh) for n in range(2) for kh in range(2)]
    for u, more in zip(FFN_UNITS, FFN_ADA):
        s += [(u[0], u[1], u[2])] + [("ada", g, k) for g, k in more]
    s += [("wf", n, kh) for n in range(2) for kh in range(2)]
    return s


STREAM = stream_before_experts()
SPLIT_AT = [u for u, it in enumerate(STREAM) if it[0] != "ada"]
ADA_AT = [u for u, it in enumerate(STREAM) if it[0] == "ada"]
QKV0, WO0 = 0, len(QKV_UNITS)
FFN0 = WO0 + 4
WF0 = FFN0 + NU
MOE0 = WF0 + 4
MOE_U0 = len(STREAM)
PAIRS = N_EXP // 2
EXTRA = (2 * TOK) // (P + 1)
PER_PAIR = 2 * NU
assert PER_PAIR % RAW == 0 and PER_PAIR % RING == 0 and len(SPLIT_AT) == MOE0


def build(nc, t):
    with ExitStack() as ctx:
        def sb(name, shape, dt=F32, stack=ctx):
            return stack.enter_context(nc.sbuf_tensor(name, shape, dt))

        def sem(name):
            return ctx.enter_context(nc.semaphore(name))

        ps = ctx.enter_context(nc.psum_tensor("ps", [P, 8, HALF], F32))

        raw = sb("raw", [P, RAW, UNIT])
        ring_hi = sb("ring_hi", [P, RING, UNIT], F32R)
        ring_lo = sb("ring_lo", [P, RING, UNIT], F32R)
        x = sb("x", [P, TILES, D])
        mrow = sb("mrow", [P, 3, HALF])
        gbc = sb("gbc", [P, 2, D])
        ident = sb("ident", [P, P])
        iota = sb("iota", [P, P])
        tri = sb("tri", [P, P])
        ones = sb("ones", [P, 1])
        wr = sb("wr", [P, KC, N_EXP])
        vecs = sb("vecs", [49, P])
        vecsT = sb("vecsT", [P, 49])
        cond_t = sb("cond_t", [P, 2, KC])
        cond = sb("cond", [P, KC, 32])
        modv = sb("modv", [P, 6, 2, KC, 2])
        mod_a = sb("mod_a", [P, 4, KC, 2])
        sub_g = sb("sub_g", [P, 1])
        lamv = sb("lamv", [P, 4, HD])
        lams = sb("lams", [P, 4])
        junk = sb("junk", [P, HD])
        lam = sb("lam", [P, 1])
        ssq = sb("ssq", [P, 5, TILES])
        msq = sb("msq", [P, 5, TILES])
        rstd = sb("rstd", [P, 5, TILES])
        mhalf = sb("mhalf", [P, 24])
        o_ssq = sb("o_ssq", [P, TILES, HEADS])
        o_msq = sb("o_msq", [P, TILES, HEADS])
        o_rstd = sb("o_rstd", [P, TILES, HEADS])
        mx = sb("mx", [P, 2, 2])
        nmx = sb("nmx", [P, 2, 2])
        sums = sb("sums", [P, 2, 2])
        rs = sb("rs", [P, 2, 2])
        l1 = sb("l1", [P, 2])
        lg = sb("lg", [P, TILES, N_EXP])
        lmax = sb("lmax", [P, TILES])
        pr = sb("pr", [P, TILES, N_EXP])
        psumr = sb("psumr", [P, TILES])
        prec = sb("prec", [P, TILES])
        top = sb("top", [P, TILES, 8])
        topi = sb("topi", [P, TILES, 8], U32)
        topf = sb("topf", [P, TILES, 8])
        tsum = sb("tsum", [P, TILES])
        trec = sb("trec", [P, TILES])
        tg = sb("tg", [P, TILES, 2])
        oh1 = sb("oh1", [P, TILES, N_EXP])
        oh2 = sb("oh2", [P, TILES, N_EXP])
        mask = sb("mask", [P, TILES, N_EXP])
        gate = sb("gate", [P, TILES, N_EXP])
        posm = sb("posm", [P, TILES, N_EXP])
        pos_pair = sb("pos_pair", [P, TILES, 2])
        gate_pair = sb("gate_pair", [P, TILES, 2])
        cnt = sb("cnt", [P, N_EXP])
        ext = sb("ext", [P, 2, N_EXP])
        ones8 = sb("ones8", [P, N_EXP])
        cum = sb("cum", [P, 2, N_EXP])
        pick = sb("pick", [P, EXTRA, 2, N_EXP])
        meta_f = sb("meta_f", [P, 8])
        meta = sb("meta", [P, 8], I32)
        start = sb("start", [P, EXTRA])
        x_place = sb("x_place", [P, EXTRA, TILES])
        x_gate = sb("x_gate", [P, EXTRA, TILES])
        x_tmp = sb("x_tmp", [P, TILES, N_EXP])

        def over(stack_fn):
            with ExitStack() as s:
                return stack_fn(s)

        def phase_h(s):
            return (sb("h_hi", [P, KC, TOK], F32R, s), sb("h_lo", [P, KC, TOK], F32R, s))

        def phase_attn(s):
            return (sb("qT", [P, 2, TOK], F32, s), sb("kT", [P, 2, HALF], F32, s),
                    sb("prob", [P, 2, 2, TOK], F32, s), sb("amap", [P, 2, TOK], F32, s),
                    sb("aT", [P, 2, TOK], F32, s))

        h_hi, h_lo = over(phase_h)
        qT, kT, prob, amap, aT = over(phase_attn)

        def dense(s):
            sb("skip_h", [P, 2, KC, TOK], F32, s)
            h32 = sb("h32", [P, KC, TOK], F32, s)
            xn = sb("xn", [P, TILES, D], F32, s)
            dft_ch = sb("dft_ch", [P, 2, HALF], F32, s)
            dft_p = sb("dft_p", [P, 2, P], F32, s)
            dft_s = sb("dft_s", [P, 2, 2, 256], F32, s)
            with ExitStack() as q:
                v = sb("v", [P, TILES, D], F32, q)
                cos = sb("cos", [P, 2, HD], F32, q)
                sin = sb("sin", [P, 2, HD], F32, q)
                rope_a = sb("rope_a", [P, HALF], F32, q)
                rope_b = sb("rope_b", [P, HALF], F32, q)
            with ExitStack() as q:
                ff_hi = sb("ff_hi", [P, 2, 2, TOK], F32R, q)
                ff_lo = sb("ff_lo", [P, 2, 2, TOK], F32R, q)
                tnh = sb("tnh", [P, 2, TOK], F32, q)
                hb = sb("hb", [P, 2, TOK], F32, q)
            with ExitStack() as q:
                f_sin = sb("f_sin", [P, TILES, D], F32, q)
            return h32, xn, dft_ch, dft_p, dft_s, v, cos, sin, rope_a, rope_b, ff_hi, ff_lo, tnh, hb, f_sin

        (h32, xn, dft_ch, dft_p, dft_s, v, cos, sin, rope_a, rope_b,
         ff_hi, ff_lo, tnh, hb, f_sin) = over(dense)

        def one_or_other(s):
            with ExitStack() as q:
                xe = sb("xe", [P, KC, 2, 256], F32R, q)
            with ExitStack() as q:
                more = (sb("x_tok", [P, KC, P], F32, q), sb("x_hT", [P, 2, P], F32, q), sb("x_y", [P, D], F32, q))
            sb("xe_space", [P, KC, 2, 256], F32, s)
            return xe, more

        def experts(s):
            return (sb("tok_hi", [P, TILES, D], F32R, s), sb("tok_lo", [P, TILES, D], F32R, s),
                    sb("acc", [P, TILES, D], F32, s),
                    one_or_other(s),
                    sb("sel", [P, TILES, 2, P], F32R, s), sb("selT", [P, 2, TOK], F32R, s),
                    sb("y_hi", [P, D], F32R, s), sb("y_lo", [P, D], F32R, s),
                    sb("eh_hi", [P, 2, 2, P], F32R, s), sb("eh_lo", [P, 2, 2, P], F32R, s),
                    sb("et", [P, 2, 256], F32, s), sb("eh", [P, 2, 256], F32, s))

        (tok_hi, tok_lo, acc, (xe, (x_tok, x_hT, x_y)), sel, selT, y_hi, y_lo, eh_hi, eh_lo, et, eh) = over(experts)

        kbuf = h32[:].rearrange("p k m -> p (k m)").rearrange("p (t n) -> p t n", t=TILES)
        qbuf = xn
        obuf = xn
        yacc = xn
        f_cos = xn
        final_g = mrow[:, 0:2, :].rearrange("p a n -> p (a n)")

        raw_loaded = [sem(f"raw_loaded{i}") for i in range(RAW)]
        hi_ready, lo_ready, unit_used, ada_used = map(sem, ("hi_ready", "lo_ready", "unit_used", "ada_used"))
        x_loaded, vecs_loaded, ident_loaded, lam_loaded = map(sem, ("x_loaded", "vecs_loaded", "ident_loaded", "lam_loaded"))
        rope_loaded, cache_loaded, dft_loaded, route_loaded, final_g_loaded = map(
            sem, ("rope_loaded", "cache_loaded", "dft_loaded", "route_loaded", "final_g_loaded"))
        bias_loaded = [sem(f"bias_loaded{g}") for g in range(6)]
        const_ready, vecsT_ps, vecsT_sb, cond_tanh, cond_ready, vch, lam_exp, lam_sum = map(
            sem, ("const_ready", "vecsT_ps", "vecsT_sb", "cond_tanh", "cond_ready", "vch", "lam_exp", "lam_sum"))
        mrow_ready, modT_ps, modv_ready, mod_a_ready = map(
            sem, ("mrow_ready", "modT_ps", "modv_ready", "mod_a_ready"))
        ssq_ready, msq_ready, rstd_ready, xn_ready, xT_ps, h32_ready, hhi_ready, hlo_ready, x_upd = map(
            sem, ("ssq_ready", "msq_ready", "rstd_ready", "xn_ready", "xT_ps", "h32_ready", "hhi_ready", "hlo_ready", "x_upd"))
        qkv_acc, qkv_sb, rope_done, ctx_stored = map(sem, ("qkv_acc", "qkv_sb", "rope_done", "ctx_stored"))
        qkT_ps, qT_sb, kT_sb, score_ps, negmax, exp_done, a_ready, aT_ps, aT_sb, o_ps, o_sb = map(
            sem, ("qkT_ps", "qT_sb", "kT_sb", "score_ps", "negmax", "exp_done", "a_ready", "aT_ps", "aT_sb", "o_ps", "o_sb"))
        o_sq, o_sum, o_ms, o_rs, on_ready = map(sem, ("o_sq", "o_sum", "o_ms", "o_rs", "on_ready"))
        gbc_ps, gbc_sb, proj_acc = map(sem, ("gbc_ps", "gbc_sb", "proj_acc"))
        tanh_ready, ffh_ready, ffhi_ready, fflo_ready, y_ps, y_added = map(
            sem, ("tanh_ready", "ffh_ready", "ffhi_ready", "fflo_ready", "y_ps", "y_added"))
        dft1_ps, dft1_act, dft1_dve, dft2_ps, ft_hi, ft_lo = map(
            sem, ("dft1_ps", "dft1_act", "dft1_dve", "dft2_ps", "ft_hi", "ft_lo"))
        logit_ps, logit_sb, r_neg, r_exp, mask_ready, pos_ps, pos_sb, gate_ready = map(
            sem, ("logit_ps", "logit_sb", "r_neg", "r_exp", "mask_ready", "pos_ps", "pos_sb", "gate_ready"))
        tokT_ps, tok_hi_ready, tok_lo_ready, acc_zero = map(sem, ("tokT_ps", "tok_hi_ready", "tok_lo_ready", "acc_zero"))
        pair_cols, sel_ready, selT_ps, selT_sb, xe_ps, xe_act, xe_dve = map(
            sem, ("pair_cols", "sel_ready", "selT_ps", "selT_sb", "xe_ps", "xe_act", "xe_dve"))
        et_ready, ea_ready, eh_ready, ehT_ps, eh_hi_ready, eh_lo_ready = map(
            sem, ("et_ready", "ea_ready", "eh_ready", "ehT_ps", "eh_hi_ready", "eh_lo_ready"))
        ey_hi_ready, ey_lo_ready, comb_ps, comb_sb, y_ready, y_stored, xt_mul = map(
            sem, ("ey_hi_ready", "ey_lo_ready", "comb_ps", "comb_sb", "y_ready", "y_stored", "xt_mul"))

        meta_ready, x_sel, x_selT_ps, x_tok_ps, x_selT_sb, x_tok_sb, x_used = map(
            sem, ("meta_ready", "x_sel", "x_selT_ps", "x_tok_ps", "x_selT_sb", "x_tok_sb", "x_used"))
        x_tanh, x_h_half, x_h, x_hT_ps, x_hT_sb, x_y_sb, x_comb_ps, x_comb_sb = map(
            sem, ("x_tanh", "x_h_half", "x_h", "x_hT_ps", "x_hT_sb", "x_y_sb", "x_comb_ps", "x_comb_sb"))
        x_loaded_w = [sem(f"x_loaded_w{i}") for i in range(RING)]

        block = ctx.enter_context(nc.Block())

        w_rows = {
            "qkv": t["w_qkv_0"].rearrange("(k p) n -> p k n", p=P),
            "wo": t["w_o_0"].rearrange("(k p) n -> p k n", p=P),
            "wf": t["w_fourier_1"].rearrange("(k p) n -> p k n", p=P),
        }
        ada_rows = [t[f"ada_w_{l}"].rearrange("(k p) n -> p k n", p=P) for l in range(2)]

        def gu_source(w, c, kh):
            return w.rearrange("(k p) (u n) -> p k u n", p=P, u=2)[:, kh * 4:kh * 4 + 4, :, c * 256:c * 256 + 256]

        def down_source(w, c):
            return w.rearrange("(s p) n -> p s n", p=P)[:, 2 * c:2 * c + 2, :]

        def slot_view(slot, kind):
            s = raw[:, slot, :]
            if kind == "gu":
                return s.rearrange("p (k u n) -> p k u n", k=4, u=2)
            if kind == "down":
                return s.rearrange("p (s n) -> p s n", s=2)
            if kind == "ada":
                return s
            return s.rearrange("p (k n) -> p k n", k=4)

        def par(j, c):
            return (FFC * j + c) % 2

        def nth(i, j, c):
            return 2 * FFC * i + FFC * j + c


        def down_used(i, j, c):
            jj, cc = (j, c - 2) if c >= 2 else (j - 1, c - 2 + FFC)
            return MOE0 + NU * jj + FFN_UNITS.index(("down", cc, 0)) + 1 + PER_PAIR * i

        @block.sync
        def _(sp):
            def load(slot, kind, a, b, source=None, loaded=raw_loaded):
                dst = slot_view(slot, kind)
                if kind == "ada":
                    src = ada_rows[a // 3][:, b, (a % 3) * UNIT:(a % 3 + 1) * UNIT]
                elif kind == "gu":
                    src = gu_source(source[0], a, b)
                elif kind == "down":
                    src = down_source(source[1], a)
                else:
                    src = w_rows[kind][:, b * 4:b * 4 + 4, a * HALF:a * HALF + HALF]
                if kind == "gu":
                    for g in range(2):
                        sp.dma_start(dst[:, :, g, :], src[:, :, g, :]).then_inc(loaded[slot], 16)
                else:
                    sp.dma_start(dst, src).then_inc(loaded[slot], 16)

            for u, (kind, a, b) in enumerate(STREAM):
                if u >= RAW:
                    before = u - RAW
                    if STREAM[before][0] == "ada":
                        sp.wait_ge(ada_used, ADA_AT.index(before) + 1)
                    else:
                        sp.wait_ge(lo_ready, SPLIT_AT.index(before) + 1)
                load(u % RAW, kind, a, b, (t["w_gu_0"], t["w_down_0"]))
            with sp.Fori(0, PAIRS) as i:
                for m in range(PER_PAIR):
                    kind, c, kh = FFN_UNITS[m % NU]
                    e = 2 * i + m // NU
                    u = MOE_U0 + m
                    sp.wait_ge(lo_ready, MOE0 + m - RAW + 1 + PER_PAIR * i)
                    load(u % RAW, kind, c, kh, (t["w_gu_e_1"][e], t["w_down_e_1"][e]))
            sp.wait_ge(meta_ready, 1)
            blocks = sp.value_load(meta[0:1, EXTRA:EXTRA + 1], min_val=0, max_val=EXTRA)
            sp.wait_ge(lo_ready, MOE0 + PER_PAIR * PAIRS)
            with sp.If(blocks > 0):
                with sp.Fori(0, EXTRA) as b:
                    e = sp.value_load(meta[0:1, bass.ds(b, 1)], min_val=0, max_val=N_EXP - 1)
                    for m, (kind, c, kh) in enumerate(FFN_UNITS):
                        if m < RING:
                            sp.wait_ge(x_sel, b + 1)
                        else:
                            sp.wait_ge(x_used, NU * b + m - RING + 1)
                        load(m % RING, kind, c, kh, (t["w_gu_e_1"][e], t["w_down_e_1"][e]), x_loaded_w)
            sp.end_ifs()
            sp.wait_ge(ctx_stored, 32)
            sp.wait_ge(y_stored, 48)

        x_unit_loaded, x_slot_total = [], [0] * RING
        for m in range(NU):
            x_slot_total[m % RING] += 32 if FFN_UNITS[m][0] == "gu" else 16
            x_unit_loaded.append(x_slot_total[m % RING])

        per_slot = [0] * RAW
        loaded_at = []
        for u, (kind, a, b) in enumerate(STREAM):
            per_slot[u % RAW] += 32 if kind == "gu" else 16
            loaded_at.append(per_slot[u % RAW])
        moe_loaded, moe_slot_total = [], [0] * RAW
        for m in range(PER_PAIR):
            s = (MOE_U0 + m) % RAW
            moe_slot_total[s] += 32 if FFN_UNITS[m % NU][0] == "gu" else 16
            moe_loaded.append(per_slot[s] + moe_slot_total[s])

        def wait_loaded(eng, u):
            eng.wait_ge(raw_loaded[u % RAW], loaded_at[u])

        def wait_moe_loaded(eng, i, m):
            s = (MOE_U0 + m) % RAW
            eng.wait_ge(raw_loaded[s], moe_loaded[m] + moe_slot_total[s] * i)

        @block.gpsimd
        def _(pool):
            def load_bias(g):
                b = t[f"ada_b_{g // 3}"]
                for j in range(4):
                    src = b[(g % 3) * UNIT + j * HALF:(g % 3) * UNIT + (j + 1) * HALF]
                    pool.dma_start(mrow[32 * j:32 * j + 32, g % 3, :],
                                   src.partition_broadcast(32)).then_inc(bias_loaded[g], 16)

            pool.memset(mhalf[:], -0.5).then_inc(const_ready, 1)
            pool.memset(ones[:], 1.0).then_inc(const_ready, 1)
            load_bias(0)
            for r, name in enumerate(("lambda_q1_0", "lambda_k1_0", "lambda_q2_0", "lambda_k2_0")):
                pool.dma_start(lamv[:, r, :], t[name].partition_broadcast(P)).then_inc(lam_loaded, 16)

            def norm_pool(n):
                for k in range(TILES):
                    pool.wait_ge(ssq_ready, 3 * n + k + 1)
                    pool.tensor_scalar(msq[:, n, k:k + 1], ssq[:, n, k:k + 1], 1.0 / D, EPS,
                                       ALU.mult, ALU.add).then_inc(msq_ready, 1)
                    pool.wait_ge(msq_ready, 3 * n + k + 1)
                    pool.tensor_tensor(rstd[:, n, k:k + 1], msq[:, n, k:k + 1], mhalf[:, 0:1],
                                       ALU.pow).then_inc(rstd_ready, 1)

            pool.wait_ge(const_ready, 2)
            norm_pool(0)
            load_bias(1)
            load_bias(2)
            for c, name in enumerate(("rope_cos", "rope_sin")):
                pool.dma_start((cos, sin)[c][:], t[name].rearrange("(t p) n -> p t n", p=P)).then_inc(rope_loaded, 16)
            for c, name in enumerate(("cache_k_0", "cache_v_0")):
                pool.dma_start(gbc[:, c, :], t[name].rearrange("b p h d -> (b p) (h d)")).then_inc(cache_loaded, 16)
            pool.dma_start(dft_ch[:], t["dft_ch"].rearrange("(k p) n -> p k n", p=P)).then_inc(dft_loaded, 16)
            pool.dma_start(dft_p[:], t["dft_p"].rearrange("p (k n) -> p k n", k=2)).then_inc(dft_loaded, 16)
            pool.dma_start(dft_s[:], t["dft_s"].rearrange("(k p) (c n) -> p k c n", p=P, c=2)).then_inc(dft_loaded, 16)
            pool.dma_start(iota[:], t["iota"]).then_inc(route_loaded, 16)
            pool.dma_start(tri[:], t["tri"]).then_inc(route_loaded, 16)
            pool.dma_start(wr[:], t["w_router_1"].rearrange("(k p) n -> p k n", p=P)).then_inc(route_loaded, 16)
            pool.wait_ge(modv_ready, 1)
            load_bias(3)
            pool.wait_ge(qkv_sb, 3 * 3 + 1)
            pool.dma_start(t["k_ctx"], kbuf[:, 0, :]).then_inc(ctx_stored, 16)
            pool.wait_ge(qkv_sb, 3 * 5 + 1)
            pool.dma_start(t["v_ctx"], v[:, 0, :]).then_inc(ctx_stored, 16)
            for k in range(TILES):
                pool.wait_ge(o_sum, k + 1)
                pool.tensor_scalar(o_msq[:, k, :], o_ssq[:, k, :], 1.0 / P, SUBLN_EPS,
                                   ALU.mult, ALU.add).then_inc(o_ms, 1)
                pool.wait_ge(o_ms, k + 1)
                pool.tensor_tensor(o_rstd[:, k, :], o_msq[:, k, :], mhalf[:, 0:HEADS],
                                   ALU.pow).then_inc(o_rs, 1)
            norm_pool(1)
            pool.wait_ge(gbc_ps, 4)
            load_bias(4)
            pool.wait_ge(gbc_ps, 8)
            load_bias(5)
            norm_pool(2)
            norm_pool(3)
            pool.wait_ge(gbc_ps, 16)
            pool.dma_start(final_g, t["final_norm_g"].partition_broadcast(P)).then_inc(final_g_loaded, 16)
            norm_pool(4)

        @block.scalar
        def _(act):
            act.dma_start(ident[:], t["ident"]).then_inc(ident_loaded, 16)
            row = 0
            for name, n in (("c_ctx", 8), ("c", 8), ("norm1_g_0", 8), ("norm2_g_0", 8),
                            ("norm1_g_1", 8), ("norm2_g_1", 8), ("subln_g_0", 1)):
                src = t[name] if name != "c" else t[name].rearrange("b n -> (b n)")
                act.dma_start(vecs[row:row + n, :], src.rearrange("(k p) -> k p", p=P)).then_inc(vecs_loaded, 16)
                row += n
            act.dma_start(x[:, 0, :], t["x_prompt"].rearrange("b p n -> (b p) n")).then_inc(x_loaded, 16)
            act.dma_start(x[:, 1:3, :], t["x_sample"].rearrange("b (t p) n -> (b p) t n", p=P)).then_inc(x_loaded, 16)

            def split_hi(s):
                u = SPLIT_AT[s]
                wait_loaded(act, u)
                if s >= RING:
                    act.wait_ge(unit_used, s - RING + 1)
                act.activation(ring_hi[:, s % RING, :], raw[:, u % RAW, :], ACT.Copy).then_inc(hi_ready, 1)

            def x_ready(n, k):
                if n == 0:
                    act.wait_ge(x_loaded, 32)
                else:
                    act.wait_ge(x_upd, 6 * n - 3 + k + 1)

            def norm_act(n, turned, split, gate_no):
                for k in range(TILES):
                    x_ready(n, k)
                    act.activation(xn[:, k, :], x[:, k, :], ACT.Square,
                                   accum_out=ssq[:, n, k:k + 1]).then_inc(ssq_ready, 1)
                for k in range(TILES):
                    act.wait_ge(rstd_ready, 3 * n + k + 1)
                    act.activation(xn[:, k, :], x[:, k, :], ACT.Copy, scale=rstd[:, n, k:k + 1]).then_inc(xn_ready, 1)
                if gate_no is not None:
                    spread_gate(gate_no)
                if split is not None:
                    high_parts(turned, split)

            def high_parts(turned, split):
                for k in range(TILES):
                    act.wait_ge(h32_ready, 3 * turned + k + 1)
                    act.activation(h_hi[:, :, k * P:(k + 1) * P], h32[:, :, k * P:(k + 1) * P],
                                   ACT.Copy).then_inc(hhi_ready, 1)

            def spread_gate(q):
                act.wait_ge(x_upd, 6 * q) if q else act.wait_ge(o_sb, 24)
                for j in range(4):
                    act.wait_ge(gbc_ps, 4 * q + j + 1)
                    act.activation(gbc[:, j // 2, (j % 2) * HALF:(j % 2 + 1) * HALF], ps[:, 6, :],
                                   ACT.Copy).then_inc(gbc_sb, 1)

            act.wait_ge(vecsT_sb, 1)
            act.activation(cond_t[:].rearrange("p c k -> p (c k)"), vecsT[:, 0:16], ACT.Tanh,
                           scale=0.5).then_inc(cond_tanh, 1)
            act.wait_ge(lam_sum, 2)
            act.activation(lams[:, 2:4], lams[:, 0:2], ACT.Exp).then_inc(lam_exp, 1)

            norm_act(0, 0, None, None)
            high_parts(0, 0)

            split_hi(QKV0)
            split_hi(QKV0 + 1)
            for s in range(len(QKV_UNITS) + 1):
                if s + 2 < len(QKV_UNITS):
                    split_hi(QKV0 + s + 2)
                if s and QKV_UNITS[s - 1][2] == 1:
                    n = QKV_UNITS[s - 1][1]
                    dst = (qbuf, kbuf, v)[n // 2]
                    for k in range(TILES):
                        if k < 2:
                            act.wait_ge(qkv_acc, 2 * n + k + 1)
                        else:
                            act.wait_ge(unit_used, s)
                        act.activation(dst[:, k, (n % 2) * HALF:(n % 2 + 1) * HALF],
                                       ps[:, (n % 2) * 3 + k, :], ACT.Copy).then_inc(qkv_sb, 1)

            def keys_turned(h):
                act.wait_ge(qkT_ps, h + 1)
                if h >= 2:
                    act.wait_ge(score_ps, 3 * (h - 1))
                act.activation(kT[:, h % 2, :], ps[:, 6, :], ACT.Copy).then_inc(kT_sb, 1)

            def exps(i):
                n = P if i % 3 == 0 else TOK
                act.wait_ge(negmax, i + 1)
                if i >= 2:
                    act.wait_ge(a_ready, i - 1)
                for m in range(2):
                    ins = act.activation(prob[:, i % 2, m, 0:n], ps[:, 2 * (i % 2) + m, 0:n], ACT.Exp,
                                         bias=nmx[:, i % 2, m:m + 1], scale=SCALE,
                                         accum_out=sums[:, i % 2, m:m + 1])
                ins.then_inc(exp_done, 1)

            def map_turned(i):
                n = P if i % 3 == 0 else TOK
                act.wait_ge(aT_ps, i + 1)
                if i >= 2:
                    act.wait_ge(o_ps, i - 1)
                act.activation(aT[:, i % 2, 0:n], ps[:, 4, 0:n], ACT.Copy).then_inc(aT_sb, 1)

            keys_turned(0)
            exps(0)
            for i in range(24):
                if i % 3 == 1 and i // 3 + 1 < HEADS:
                    keys_turned(i // 3 + 1)
                if i + 1 < 24:
                    exps(i + 1)
                map_turned(i)
            act.wait_ge(ctx_stored, 32)
            for k in range(TILES):
                act.wait_ge(o_sb, 24)
                act.activation(kbuf[:, k, :], obuf[:, k, :], ACT.Square).then_inc(o_sq, 1)
            split_hi(WO0)
            split_hi(WO0 + 1)
            spread_gate(0)
            high_parts(1, 1)
            for s in range(2):
                split_hi(WO0 + s + 2)

            norm_act(1, 2, None, 1)
            high_parts(2, 2)
            split_hi(FFN0)
            split_hi(FFN0 + 1)
            for s in range(NU + 1):
                if s + 2 < NU:
                    split_hi(FFN0 + s + 2)
                if s and FFN_UNITS[s - 1][0] == "gu" and FFN_UNITS[s - 1][2] == 1:
                    c = FFN_UNITS[s - 1][1]
                    act.wait_ge(unit_used, FFN0 + s)
                    if c:
                        act.wait_ge(ffh_ready, 2 * c)
                    for j in range(2):
                        act.activation(tnh[:, j, :], ps[:, 2 * j, 0:TOK], ACT.Tanh, scale=0.5).then_inc(tanh_ready, 1)
                    if c >= 2:
                        act.wait_ge(unit_used, FFN0 + FFN_UNITS.index(("down", c - 2, 0)) + 1)
                    for j in range(2):
                        act.wait_ge(ffh_ready, 2 * c + j + 1)
                        act.activation(ff_hi[:, c % 2, j, :], hb[:, j, :], ACT.Copy).then_inc(ffhi_ready, 1)
            norm_act(2, 3, None, 2)

            for n in range(0, 12, 2):
                k, g = n // 4, n % 4
                act.wait_ge(dft1_ps, n + 1)
                act.wait_ge(xT_ps, 3 * 3 + 3)
                act.activation(f_cos[:, k, g * 256:(g + 1) * 256], ps[:, n % 6, 0:256], ACT.Copy)
                act.activation(f_sin[:, k, g * 256:(g + 1) * 256], ps[:, n % 6, 256:512], ACT.Copy).then_inc(dft1_act, 1)
            split_hi(WF0)
            split_hi(WF0 + 1)
            for k in range(KC):
                act.wait_ge(dft2_ps, k + 1)
                act.activation(h_hi[:, k, :], ps[:, k % 6, 0:TOK], ACT.Copy).then_inc(ft_hi, 1)
            for s in range(2):
                split_hi(WF0 + s + 2)

            norm_act(3, 4, None, 3)
            act.wait_ge(r_neg, 1)
            for k in range(TILES):
                act.activation(pr[:, k, :], lg[:, k, :], ACT.Exp, bias=lmax[:, k:k + 1],
                               accum_out=psumr[:, k:k + 1]).then_inc(r_exp, 1)
            for n in range(2 * TILES):
                act.wait_ge(tokT_ps, n + 1)
                act.activation(tok_hi[:, n // 2, (n % 2) * HALF:(n % 2 + 1) * HALF], ps[:, n, :],
                               ACT.Copy).then_inc(tok_hi_ready, 1)

            act.wait_ge(meta_ready, 1)
            blocks = act.value_load(meta[0:1, EXTRA:EXTRA + 1], min_val=0, max_val=EXTRA)

            with act.Fori(0, PAIRS) as i:
                def hi(m):
                    wait_moe_loaded(act, i, m)
                    s = MOE0 + m
                    act.wait_ge(unit_used, s - RING + 1 + PER_PAIR * i)
                    act.activation(ring_hi[:, s % RING, :], raw[:, (MOE_U0 + m) % RAW, :],
                                   ACT.Copy).then_inc(hi_ready, 1)

                hi(0)
                hi(1)
                for j in range(2):
                    act.wait_ge(selT_ps, 2 * i + j + 1)
                    act.activation(selT[:, j, :], ps[:, 4 + j, 0:TOK], ACT.Copy).then_inc(selT_sb, 1)
                for k in range(0, KC, 2):
                    act.wait_ge(xe_ps, 8 * i + k + 1)
                    act.activation(xe[:, k, :, :], ps[:, 6, :].rearrange("p (a n) -> p a n", a=2),
                                   ACT.Copy).then_inc(xe_act, 1)
                def high_eh(j, c):
                    act.wait_ge(ehT_ps, nth(i, j, c) + 1)
                    act.wait_ge(unit_used, down_used(i, j, c))
                    act.activation(eh_hi[:, par(j, c), :, :],
                                   ps[:, 2 + par(j, c), 0:256].rearrange("p (s n) -> p s n", s=2),
                                   ACT.Copy).then_inc(eh_hi_ready, 1)

                for m in range(PER_PAIR + 1):
                    if m + 2 < PER_PAIR:
                        hi(m + 2)
                    if m:
                        j, (kind, c, kh) = (m - 1) // NU, FFN_UNITS[(m - 1) % NU]
                        if kind == "gu" and kh == 1:
                            act.wait_ge(unit_used, MOE0 + m + PER_PAIR * i)
                            act.activation(et[:, par(j, c), :], ps[:, par(j, c), 0:256], ACT.Tanh,
                                           scale=0.5).then_inc(et_ready, 1)
                        if kind == "down" and c == FFC - 1:
                            act.wait_ge(unit_used, MOE0 + m + PER_PAIR * i)
                            if j:
                                act.wait_ge(comb_ps, 12 * i + 6)
                            act.activation(y_hi[:].rearrange("p (a n) -> p a n", a=2), ps[:, 4:6, :],
                                           ACT.Copy).then_inc(ey_hi_ready, 1)
                    if m < PER_PAIR:
                        j, (kind, c, kh) = m // NU, FFN_UNITS[m % NU]
                        if kind == "gu" and kh == 1 and c >= 1:
                            high_eh(j, c - 1)
                        if kind == "down" and c == FFC - 1:
                            high_eh(j, c)

            with act.If(blocks > 0):
                with act.Fori(0, EXTRA) as b:
                    act.wait_ge(x_selT_ps, b + 1)
                    act.activation(selT[:, 0, :], ps[:, 2, 0:TOK], ACT.Copy).then_inc(x_selT_sb, 1)
                    act.wait_ge(x_tok_ps, b + 1)
                    act.activation(x_tok[:].rearrange("p (a k) n -> p a (k n)", a=2), ps[:, 0:2, :],
                                   ACT.Copy).then_inc(x_tok_sb, 1)
                    for m, (kind, c, kh) in enumerate(FFN_UNITS):
                        if (kind == "gu" and kh == 1 and c) or (kind == "down" and c == FFC - 1):
                            cc = c - 1 if kind == "gu" else c
                            act.wait_ge(x_hT_ps, FFC * b + cc + 1)
                            act.activation(x_hT[:], ps[:, 0, 0:256].rearrange("p (s n) -> p s n", s=2),
                                           ACT.Copy).then_inc(x_hT_sb, 1)
                        if kind == "gu" and kh == 1:
                            act.wait_ge(x_used, NU * b + m + 1)
                            act.activation(et[:, 0, :], ps[:, 3, 0:256], ACT.Tanh, scale=0.5).then_inc(x_tanh, 1)
                    act.wait_ge(x_used, NU * b + NU)
                    act.activation(x_y[:].rearrange("p (a n) -> p a n", a=2), ps[:, 4:6, :],
                                   ACT.Copy).then_inc(x_y_sb, 1)
            act.end_ifs()

            for k in range(TILES):
                act.wait_ge(x_upd, 6 * 4 - 3 + k + 1)
                act.activation(acc[:, k, :], x[:, k, :], ACT.Square,
                               accum_out=ssq[:, 4, k:k + 1]).then_inc(ssq_ready, 1)
            yp = t["y_prompt"].rearrange("b p n -> (b p) n")
            ysm = t["y_sample"].rearrange("b (t p) n -> t (b p) n", p=P)
            for k in range(TILES):
                act.wait_ge(y_ready, k + 1)
                act.dma_start(yp if k == 0 else ysm[k - 1], acc[:, k, :]).then_inc(y_stored, 16)

        @block.vector
        def _(dve):
            chain = [0]

            def link(ins):
                chain[0] += 1
                ins.then_inc(vch, 1)
                dve.wait_ge(vch, chain[0])

            def split_lo(s):
                u = SPLIT_AT[s]
                dve.wait_ge(hi_ready, s + 1)
                dve.tensor_tensor(ring_lo[:, s % RING, :], raw[:, u % RAW, :],
                                  ring_hi[:, s % RING, :].bitcast(F32), ALU.subtract).then_inc(lo_ready, 1)

            dve.wait_ge(vecsT_ps, 1)
            dve.tensor_copy(vecsT[:], ps[:, 6, 0:49]).then_inc(vecsT_sb, 1)
            dve.wait_ge(cond_tanh, 1)
            link(dve.scalar_tensor_tensor(cond_t[:].rearrange("p c k -> p (c k)"),
                                          cond_t[:].rearrange("p c k -> p (c k)"), 1.0,
                                          vecsT[:, 0:16], ALU.add, ALU.mult))
            for r in range(16):
                ins = dve.tensor_scalar(cond[:, :, 2 * r:2 * r + 2], cond_t[:].rearrange("p c k -> p k c"),
                                        0.5, None, ALU.mult)
            ins.then_inc(cond_ready, 1)
            dve.tensor_scalar(sub_g[:], vecsT[:, 48:49], 1.0 - LAMBDA_INIT, None, ALU.mult)
            dve.wait_ge(lam_loaded, 64)
            for r in range(2):
                dve.tensor_tensor_reduce(junk[:], lamv[:, 2 * r, :], lamv[:, 2 * r + 1, :], 1.0, 0.0,
                                         ALU.mult, ALU.add, lams[:, r:r + 1]).then_inc(lam_sum, 1)
                dve.wait_ge(lam_sum, r + 1)
            dve.wait_ge(lam_exp, 1)
            link(dve.tensor_scalar(lam[:], lams[:, 2:3], lams[:, 3:4], LAMBDA_INIT, ALU.subtract, ALU.add))

            def ada_rows_out(g):
                dve.wait_ge(ada_used, KC * (g + 1))
                dve.wait_ge(bias_loaded[g], 64)
                dve.tensor_tensor(mrow[:, g % 3, :], ps[:, 7, :], mrow[:, g % 3, :], ALU.add).then_inc(mrow_ready, 1)

            def ada_cols_out(g):
                dve.wait_ge(modT_ps, g + 1)
                src = ps[:, 7, :].rearrange("p (q j r) -> p q j r", q=4, j=4)
                for c in range(2):
                    ins = dve.tensor_copy(
                        modv[:, g, :, :, c].rearrange("p v (h q) -> p (v h) q", h=2).rearrange("p j q -> p q j"),
                        src[:, :, :, c])
                ins.then_inc(modv_ready, 1)

            ada_rows_out(0)
            ada_cols_out(0)

            NORMS = ((0, 0, 0, 1, 16), (1, 1, 2, 0, 24), (3, 0, 3, 1, 32), (4, 1, 5, 0, 40))

            def low_parts(split):
                def low(k):
                    dve.wait_ge(hhi_ready, 3 * split + k + 1)
                    dve.tensor_tensor(h_lo[:, :, k * P:(k + 1) * P], h32[:, :, k * P:(k + 1) * P],
                                      h_hi[:, :, k * P:(k + 1) * P].bitcast(F32), ALU.subtract).then_inc(hlo_ready, 1)
                return low

            def norm_dve(n, turned, split):
                gs, vs, gc, vc, row = NORMS[n]
                dve.wait_ge(modv_ready, max(gs, gc) + 1)
                for c in range(2):
                    ins = dve.scalar_tensor_tensor(mod_a[:, n, :, c], modv[:, gc, vc, :, c], 1.0,
                                                   vecsT[:, row:row + KC], ALU.add, ALU.mult)
                ins.then_inc(mod_a_ready, 1)
                dve.wait_ge(mod_a_ready, n + 1)
                low = low_parts(split) if split is not None else (lambda k: None)
                for k in range(TILES):
                    dve.wait_ge(xT_ps, 3 * turned + k + 1)
                    for q in range(KC):
                        ins = dve.tensor_scalar(h32[:, q, k * P:(k + 1) * P],
                                                ps[:, 2 * k + q // 4, (q % 4) * P:(q % 4 + 1) * P],
                                                mod_a[:, n, q, COND[k]:COND[k] + 1],
                                                modv[:, gs, vs, q, COND[k]:COND[k] + 1], ALU.mult, ALU.add)
                    ins.then_inc(h32_ready, 1)
                    if k:
                        low(k - 1)
                low(TILES - 1)

            norm_dve(0, 0, 0)

            def rope(n):
                buf = (qbuf, kbuf)[n // 2]
                for k in (1, 2):
                    xs = buf[:, k, (n % 2) * HALF:(n % 2 + 1) * HALF]
                    dve.wait_ge(qkv_sb, 3 * n + k + 1)
                    if n == 0 and k == 1:
                        dve.wait_ge(rope_loaded, 32)
                    g8 = lambda a: a.rearrange("p (g d) -> p g d", d=HD)
                    table = lambda a: a[:, k - 1, :].unsqueeze(1).to_broadcast([P, 8, HD])
                    dve.tensor_tensor(g8(rope_a[:]), g8(xs), table(cos), ALU.mult)
                    halves = lambda a: a.rearrange("p g (a f r) -> p g a f r", a=2, f=2)
                    for f in range(2):
                        for a in range(2):
                            ins = dve.tensor_tensor(halves(g8(rope_b[:]))[:, :, a, f, :], halves(g8(xs))[:, :, a, 1 - f, :],
                                                    halves(table(sin))[:, :, a, f, :], ALU.mult)
                    link(ins)
                    dve.tensor_tensor(xs, rope_a[:], rope_b[:], ALU.add).then_inc(rope_done, 1)
                    dve.wait_ge(rope_done, 2 * n + k)

            def ada_events(plan, step):
                return [g for s, more in enumerate(plan) if s == step for g, k in more if k == KC - 1]

            split_lo(QKV0)
            split_lo(QKV0 + 1)
            for s in range(len(QKV_UNITS) + 2):
                for g in ada_events(QKV_ADA, s - 2):
                    ada_cols_out(g)
                if s + 2 < len(QKV_UNITS):
                    split_lo(QKV0 + s + 2)
                if 2 <= s < 10 and s % 2 == 0:
                    rope(s // 2 - 1)
                for g in ada_events(QKV_ADA, s - 1):
                    ada_rows_out(g)

            def queries_turned(h):
                dve.wait_ge(qkT_ps, h + 1)
                if h >= 2:
                    dve.wait_ge(score_ps, 3 * (h - 1))
                dve.tensor_copy(qT[:, h % 2, :], ps[:, 7, 0:TOK]).then_inc(qT_sb, 1)

            def row_max(i):
                n = P if i % 3 == 0 else TOK
                dve.wait_ge(score_ps, i + 1)
                link(dve.tensor_reduce(mx[:, i % 2, :], ps[:, 2 * (i % 2):2 * (i % 2) + 2, 0:n], AX.X, ALU.max))
                dve.tensor_scalar(nmx[:, i % 2, :], mx[:, i % 2, :], -SCALE, None, ALU.mult).then_inc(negmax, 1)

            def difference(i):
                n = P if i % 3 == 0 else TOK
                dve.wait_ge(exp_done, i + 1)
                link(dve.reciprocal(rs[:, i % 2, :], sums[:, i % 2, :]))
                link(dve.tensor_scalar(l1[:, i % 2:i % 2 + 1], rs[:, i % 2, 1:2], lam[:, 0:1], None, ALU.mult))
                link(dve.tensor_scalar(prob[:, i % 2, 1, 0:n], prob[:, i % 2, 1, 0:n], l1[:, i % 2:i % 2 + 1], None, ALU.mult))
                if i >= 2:
                    dve.wait_ge(aT_ps, i - 1)
                dve.scalar_tensor_tensor(amap[:, i % 2, 0:n], prob[:, i % 2, 0, 0:n], rs[:, i % 2, 0:1],
                                         prob[:, i % 2, 1, 0:n], ALU.mult, ALU.subtract).then_inc(a_ready, 1)

            def out_rows(i):
                h, k = i // 3, i % 3
                dve.wait_ge(o_ps, i + 1)
                dve.tensor_copy(obuf[:, k, h * P:(h + 1) * P], ps[:, 5, k * P:(k + 1) * P]).then_inc(o_sb, 1)

            queries_turned(0)
            row_max(0)
            for i in range(24):
                if i % 3 == 1 and i // 3 + 1 < HEADS:
                    queries_turned(i // 3 + 1)
                if i + 1 < 24:
                    row_max(i + 1)
                difference(i)
                if i:
                    out_rows(i - 1)
            out_rows(23)

            split_lo_wo = [WO0, WO0 + 1]
            for k in range(TILES):
                dve.wait_ge(o_sq, k + 1)
                dve.tensor_reduce(o_ssq[:, k, :], kbuf[:, k, :].rearrange("p (h d) -> p h d", d=P), AX.X,
                                  ALU.add).then_inc(o_sum, 1)
            for k in range(TILES):
                dve.wait_ge(o_rs, k + 1)
                dve.tensor_tensor(obuf[:, k, :].rearrange("p (h d) -> p h d", d=P),
                                  obuf[:, k, :].rearrange("p (h d) -> p h d", d=P),
                                  o_rstd[:, k, :].unsqueeze(2).to_broadcast([P, HEADS, P]),
                                  ALU.mult).then_inc(on_ready, 1)
            low = low_parts(1)
            for k in range(TILES):
                dve.wait_ge(xT_ps, 3 + k + 1)
                dve.wait_ge(o_sum, TILES)
                for q in range(2):
                    ins = dve.tensor_scalar(h32[:, 4 * q:4 * q + 4, k * P:(k + 1) * P],
                                            ps[:, 2 * k + q, :].rearrange("p (q n) -> p q n", q=4),
                                            sub_g[:, 0:1], None, ALU.mult)
                ins.then_inc(h32_ready, 1)
            for s in split_lo_wo:
                split_lo(s)
            for k in range(TILES):
                low(k)

            def add_projection(w, n, first):
                for k in range(TILES):
                    if k < 2:
                        dve.wait_ge(proj_acc, 4 * w + 2 * n + k + 1)
                    else:
                        dve.wait_ge(unit_used, first + 2 * n + 2)
                    if n == 0 and k == 0:
                        dve.wait_ge(gbc_sb, 4 * (2 * w + 1))
                    cols = slice(n * HALF, (n + 1) * HALF)
                    link(dve.tensor_tensor(xn[:, k, cols], ps[:, n * 3 + k, :], gbc[:, COND[k], cols], ALU.mult))
                    dve.tensor_tensor(x[:, k, cols], x[:, k, cols], xn[:, k, cols], ALU.add).then_inc(x_upd, 1)

            split_lo(WO0 + 2)
            split_lo(WO0 + 3)
            add_projection(0, 0, WO0)
            add_projection(0, 1, WO0)

            norm_dve(1, 2, 2)
            split_lo(FFN0)
            split_lo(FFN0 + 1)

            def add_y(c, n):
                k, half = n // 2, n % 2
                if n < 5:
                    dve.wait_ge(y_ps, 5 * c + n + 1)
                else:
                    dve.wait_ge(unit_used, FFN0 + FFN_UNITS.index(("down", c, 0)) + 1)
                dst = yacc[:, k, half * HALF:(half + 1) * HALF]
                if c == 0:
                    dve.tensor_copy(dst, ps[:, 4 + n % 3, :]).then_inc(y_added, 1)
                else:
                    dve.wait_ge(y_added, 6 * (c - 1) + n + 1)
                    dve.tensor_tensor(dst, ps[:, 4 + n % 3, :], dst, ALU.add).then_inc(y_added, 1)

            for s in range(NU + 2):
                for g in ada_events(FFN_ADA, s - 2):
                    ada_cols_out(g)
                if s + 2 < NU:
                    split_lo(FFN0 + s + 2)
                prev = FFN_UNITS[s - 1] if 1 <= s <= NU else None
                down = s < NU and FFN_UNITS[s][0] == "down"
                silu = prev is not None and prev[0] == "gu" and prev[2] == 1
                if silu:
                    c = prev[1]
                    for j in range(2):
                        dve.wait_ge(tanh_ready, 2 * c + j + 1)
                        if c:
                            dve.wait_ge(fflo_ready, 2 * (c - 1) + j + 1)
                        link(dve.scalar_tensor_tensor(hb[:, j, :], tnh[:, j, :], 1.0, ps[:, 2 * j, 0:TOK],
                                                      ALU.add, ALU.mult))
                        dve.scalar_tensor_tensor(hb[:, j, :], hb[:, j, :], 0.5, ps[:, 2 * j + 1, 0:TOK],
                                                 ALU.mult, ALU.mult).then_inc(ffh_ready, 1)
                if down:
                    for n in range(3):
                        add_y(FFN_UNITS[s][1], n)
                if silu:
                    for j in range(2):
                        dve.wait_ge(ffhi_ready, 2 * c + j + 1)
                        dve.tensor_tensor(ff_lo[:, c % 2, j, :], hb[:, j, :], ff_hi[:, c % 2, j, :].bitcast(F32),
                                          ALU.subtract).then_inc(fflo_ready, 1)
                if down:
                    for n in range(3, 6):
                        add_y(FFN_UNITS[s][1], n)
                for g in ada_events(FFN_ADA, s - 1):
                    ada_rows_out(g)
            dve.wait_ge(y_added, 6 * FFC)
            dve.wait_ge(gbc_sb, 8)

            def add_gated(buf):
                for n in range(2):
                    for k in range(TILES):
                        cols = slice(n * HALF, (n + 1) * HALF)
                        link(dve.tensor_tensor(buf[:, k, cols], buf[:, k, cols], gbc[:, COND[k], cols], ALU.mult))
                        dve.tensor_tensor(x[:, k, cols], x[:, k, cols], buf[:, k, cols], ALU.add).then_inc(x_upd, 1)

            add_gated(yacc)
            norm_dve(2, 3, None)

            for n in range(1, 12, 2):
                k, g = n // 4, n % 4
                dve.wait_ge(dft1_ps, n + 1)
                dve.tensor_copy(f_cos[:, k, g * 256:(g + 1) * 256], ps[:, n % 6, 0:256])
                dve.tensor_copy(f_sin[:, k, g * 256:(g + 1) * 256], ps[:, n % 6, 256:512]).then_inc(dft1_dve, 1)
            split_lo(WF0)
            split_lo(WF0 + 1)
            for k in range(KC):
                dve.wait_ge(ft_hi, k + 1)
                dve.tensor_tensor(h_lo[:, k, :], ps[:, k % 6, 0:TOK], h_hi[:, k, :].bitcast(F32),
                                  ALU.subtract).then_inc(ft_lo, 1)
            split_lo(WF0 + 2)
            split_lo(WF0 + 3)
            add_projection(1, 0, WF0)
            add_projection(1, 1, WF0)
            norm_dve(3, 4, None)

            dve.wait_ge(logit_ps, 1)
            dve.wait_ge(route_loaded, 48)
            link(dve.tensor_copy(lg[:], ps[:, 6, 0:24].rearrange("p (t e) -> p t e", t=TILES)))
            link(dve.tensor_reduce(lmax[:], lg[:], AX.X, ALU.max))
            dve.tensor_scalar(lmax[:], lmax[:], -1.0, None, ALU.mult).then_inc(r_neg, 1)
            dve.wait_ge(r_exp, TILES)
            link(dve.reciprocal(prec[:], psumr[:]))
            for k in range(TILES):
                link(dve.tensor_scalar(pr[:, k, :], pr[:, k, :], prec[:, k:k + 1], None, ALU.mult))
                link(dve.max(top[:, k, :], pr[:, k, :]))
                link(dve.max_index(topi[:, k, :], top[:, k, :], pr[:, k, :]))
            link(dve.tensor_copy(topf[:], topi[:]))
            link(dve.tensor_tensor(tsum[:], top[:, :, 0], top[:, :, 1], ALU.add))
            link(dve.reciprocal(trec[:], tsum[:]))
            for k in range(TILES):
                dve.tensor_scalar(tg[:, k, :], top[:, k, 0:2], trec[:, k:k + 1], None, ALU.mult)
                dve.tensor_scalar(oh1[:, k, :], iota[:, 0:N_EXP], topf[:, k, 0:1], None, ALU.is_equal)
                link(dve.tensor_scalar(oh2[:, k, :], iota[:, 0:N_EXP], topf[:, k, 1:2], None, ALU.is_equal))
            dve.tensor_tensor(mask[:], oh1[:], oh2[:], ALU.add).then_inc(mask_ready, 1)
            for k in range(TILES):
                link(dve.tensor_scalar(gate[:, k, :], oh1[:, k, :], tg[:, k, 0:1], None, ALU.mult))
                link(dve.scalar_tensor_tensor(gate[:, k, :], oh2[:, k, :], tg[:, k, 1:2], gate[:, k, :],
                                              ALU.mult, ALU.add))
            dve.wait_ge(mask_ready, 1)
            dve.wait_ge(pos_ps, 1)
            link(dve.scalar_tensor_tensor(posm[:], ps[:, 6, 0:24].rearrange("p (t e) -> p t e", t=TILES), 1.0,
                                          mask[:], ALU.add, ALU.mult))
            link(dve.tensor_scalar(posm[:], posm[:], -1.0, None, ALU.add))
            dve.memset(ones8[:], 1.0)
            link(dve.tensor_copy(cnt[:], ps[:, 6, 24:32]))
            dve.tensor_scalar(ext[:, 0, :], cnt[:], float(P), None, ALU.is_gt)
            link(dve.tensor_scalar(ext[:, 1, :], cnt[:], float(2 * P), None, ALU.is_gt))
            link(dve.tensor_tensor(ext[:, 0, :], ext[:, 0, :], ext[:, 1, :], ALU.add))
            link(dve.tensor_tensor_scan(cum[:, 0, :], ones8[:], ext[:, 0, :], 0.0, ALU.mult, ALU.add))
            link(dve.tensor_tensor(cum[:, 1, :], cum[:, 0, :], ext[:, 0, :], ALU.subtract))
            for b in range(EXTRA):
                dve.tensor_scalar(pick[:, b, 0, :], cum[:, 0, :], float(b), None, ALU.is_gt)
                link(dve.tensor_scalar(pick[:, b, 1, :], cum[:, 1, :], float(b), None, ALU.is_le))
                link(dve.tensor_tensor(pick[:, b, 0, :], pick[:, b, 0, :], pick[:, b, 1, :], ALU.mult))
                link(dve.tensor_tensor(pick[:, b, 1, :], pick[:, b, 0, :], iota[:, 0:N_EXP], ALU.mult))
                link(dve.tensor_reduce(meta_f[:, b:b + 1], pick[:, b, 1, :], AX.X, ALU.add))
                link(dve.tensor_scalar(pick[:, b, 1, :], cum[:, 1, :], float(-P), float(P * (b + 1)), ALU.mult, ALU.add))
                link(dve.tensor_tensor(pick[:, b, 1, :], pick[:, b, 0, :], pick[:, b, 1, :], ALU.mult))
                link(dve.tensor_reduce(start[:, b:b + 1], pick[:, b, 1, :], AX.X, ALU.add))
                chosen = pick[:, b, 0, :].unsqueeze(1).to_broadcast([P, TILES, N_EXP])
                link(dve.scalar_tensor_tensor(x_tmp[:], posm[:], 1.0, chosen, ALU.add, ALU.mult))
                link(dve.tensor_reduce(x_place[:, b, :], x_tmp[:], AX.X, ALU.add))
                link(dve.tensor_scalar(x_place[:, b, :], x_place[:, b, :], start[:, b:b + 1], -1.0,
                                       ALU.subtract, ALU.add))
                link(dve.tensor_tensor(x_tmp[:], gate[:], chosen, ALU.mult))
                link(dve.tensor_reduce(x_gate[:, b, :], x_tmp[:], AX.X, ALU.add))
            dve.memset(meta_f[:, EXTRA + 1:8], 0.0)
            link(dve.tensor_copy(meta_f[:, EXTRA:EXTRA + 1], cum[:, 0, N_EXP - 1:N_EXP]))
            dve.tensor_copy(meta[:], meta_f[:]).then_inc(meta_ready, 1)
            dve.wait_ge(meta_ready, 1)
            blocks = dve.value_load(meta[0:1, EXTRA:EXTRA + 1], min_val=0, max_val=EXTRA)
            for n in range(2 * TILES):
                dve.wait_ge(tok_hi_ready, n + 1)
                cols = slice((n % 2) * HALF, (n % 2 + 1) * HALF)
                dve.tensor_tensor(tok_lo[:, n // 2, cols], ps[:, n, :], tok_hi[:, n // 2, cols].bitcast(F32),
                                  ALU.subtract).then_inc(tok_lo_ready, 1)
            dve.memset(acc[:], 0.0).then_inc(acc_zero, 1)
            dve.wait_ge(acc_zero, 1)

            with dve.Fori(0, PAIRS) as i:
                def lo(m):
                    s = MOE0 + m
                    dve.wait_ge(hi_ready, s + 1 + PER_PAIR * i)
                    dve.tensor_tensor(ring_lo[:, s % RING, :], raw[:, (MOE_U0 + m) % RAW, :],
                                      ring_hi[:, s % RING, :].bitcast(F32), ALU.subtract).then_inc(lo_ready, 1)

                def combine(j):
                    for n in range(6):
                        k, half = n // 2, n % 2
                        cols = slice(half * HALF, (half + 1) * HALF)
                        dve.wait_ge(comb_ps, 12 * i + 6 * j + n + 1)
                        if j:
                            dve.wait_ge(comb_sb, 12 * i + n + 1)
                        dve.scalar_tensor_tensor(acc[:, k, cols], ps[:, 6 + n % 2, :], gate_pair[:, k, j:j + 1],
                                                 acc[:, k, cols], ALU.mult, ALU.add).then_inc(comb_sb, 1)

                dve.tensor_copy(pos_pair[:], posm[:, :, bass.ds(2 * i, 2)])
                dve.tensor_copy(gate_pair[:], gate[:, :, bass.ds(2 * i, 2)]).then_inc(pair_cols, 1)
                dve.wait_ge(pair_cols, i + 1)
                for j in range(2):
                    for k in range(TILES):
                        ins = dve.tensor_scalar(sel[:, k, j, :], iota[:], pos_pair[:, k, j:j + 1], None, ALU.is_equal)
                ins.then_inc(sel_ready, 1)
                lo(0)
                lo(1)
                for k in range(1, KC, 2):
                    dve.wait_ge(xe_ps, 8 * i + k + 1)
                    dve.tensor_copy(xe[:, k, :, :], ps[:, 7, :].rearrange("p (a n) -> p a n", a=2)).then_inc(xe_dve, 1)
                def low_eh(j, c):
                    dve.wait_ge(eh_hi_ready, nth(i, j, c) + 1)
                    b = par(j, c)
                    dve.tensor_tensor(eh_lo[:, b, :, :], ps[:, 2 + b, 0:256].rearrange("p (s n) -> p s n", s=2),
                                      eh_hi[:, b, :, :].bitcast(F32), ALU.subtract).then_inc(eh_lo_ready, 1)

                for m in range(PER_PAIR + 1):
                    if m + 2 < PER_PAIR:
                        lo(m + 2)
                    if m:
                        j = (m - 1) // NU
                        kind, c, kh = FFN_UNITS[(m - 1) % NU]
                        n, b = nth(i, j, c), par(j, c)
                        if kind == "gu" and kh == 1:
                            dve.wait_ge(et_ready, n + 1)
                            dve.scalar_tensor_tensor(eh[:, b, :], et[:, b, :], 1.0, ps[:, b, 0:256],
                                                     ALU.add, ALU.mult).then_inc(ea_ready, 1)
                            dve.wait_ge(ea_ready, n + 1)
                            dve.scalar_tensor_tensor(eh[:, b, :], eh[:, b, :], 0.5, ps[:, b, 256:512],
                                                     ALU.mult, ALU.mult).then_inc(eh_ready, 1)
                    if m < PER_PAIR:
                        kind, c, kh = FFN_UNITS[m % NU]
                        if kind == "gu" and kh == 1 and c >= 1:
                            low_eh(m // NU, c - 1)
                        if kind == "down" and c == FFC - 1:
                            low_eh(m // NU, c)
                    if m and FFN_UNITS[(m - 1) % NU] == ("down", FFC - 1, 0):
                        j = (m - 1) // NU
                        dve.wait_ge(ey_hi_ready, 2 * i + j + 1)
                        dve.tensor_tensor(y_lo[:].rearrange("p (a n) -> p a n", a=2), ps[:, 4:6, :],
                                          y_hi[:].rearrange("p (a n) -> p a n", a=2).bitcast(F32),
                                          ALU.subtract).then_inc(ey_lo_ready, 1)
                        combine(j)
                dve.wait_ge(comb_sb, 12 * i + 12)

            dve.wait_ge(comb_sb, 12 * PAIRS)
            with dve.If(blocks > 0):
                with dve.Fori(0, EXTRA) as b:
                    dve.tensor_copy(pos_pair[:, :, 0:1], x_place[:, bass.ds(b, 1), :].rearrange("p b t -> p t b"))
                    dve.tensor_copy(gate_pair[:, :, 0:1],
                                    x_gate[:, bass.ds(b, 1), :].rearrange("p b t -> p t b")).then_inc(pair_cols, 1)
                    dve.wait_ge(pair_cols, PAIRS + b + 1)
                    for k in range(TILES):
                        ins = dve.tensor_scalar(sel[:, k, 0, :], iota[:], pos_pair[:, k, 0:1], None, ALU.is_equal)
                    ins.then_inc(x_sel, 1)
                    for c in range(FFC):
                        dve.wait_ge(x_tanh, FFC * b + c + 1)
                        if c:
                            dve.wait_ge(x_hT_ps, FFC * b + c)
                        dve.scalar_tensor_tensor(eh[:, 0, :], et[:, 0, :], 1.0, ps[:, 3, 0:256],
                                                 ALU.add, ALU.mult).then_inc(x_h_half, 1)
                        dve.wait_ge(x_h_half, FFC * b + c + 1)
                        dve.scalar_tensor_tensor(eh[:, 0, :], eh[:, 0, :], 0.5, ps[:, 3, 256:512],
                                                 ALU.mult, ALU.mult).then_inc(x_h, 1)
                    for n in range(6):
                        k, half = n // 2, n % 2
                        cols = slice(half * HALF, (half + 1) * HALF)
                        dve.wait_ge(x_comb_ps, 6 * b + n + 1)
                        dve.scalar_tensor_tensor(acc[:, k, cols], ps[:, 6 + n % 2, :], gate_pair[:, k, 0:1],
                                                 acc[:, k, cols], ALU.mult, ALU.add).then_inc(x_comb_sb, 1)
                    dve.wait_ge(x_comb_sb, 6 * b + 6)
            dve.end_ifs()
            dve.wait_ge(gbc_sb, 16)
            dve.wait_ge(final_g_loaded, 16)
            add_gated(acc)
            for k in range(TILES):
                dve.wait_ge(rstd_ready, 12 + k + 1)
                dve.scalar_tensor_tensor(acc[:, k, :], x[:, k, :], rstd[:, 4, k:k + 1], final_g,
                                         ALU.mult, ALU.mult).then_inc(y_ready, 1)

        @block.tensor
        def _(pe):
            def mm3(out, l_hi, l_lo, r_hi, r_lo, first, last):
                pe.matmul(out, l_hi, r_hi, start=first, stop=False)
                pe.matmul(out, l_lo, r_hi, start=False, stop=False)
                return pe.matmul(out, l_hi, r_lo, start=False, stop=last)

            def ada_unit(g, k):
                n = KC * g + k
                u = ADA_AT[n]
                wait_loaded(pe, u)
                if k == 0 and g:
                    pe.wait_ge(modv_ready, g)
                for j in range(4):
                    ins = pe.matmul(ps[32 * j:32 * j + 32, 7, :], cond[:, k, :],
                                    raw[:, u % RAW, j * HALF:(j + 1) * HALF], start=(k == 0), stop=(k == KC - 1))
                ins.then_inc(ada_used, 1)

            def ada_turn(g):
                pe.wait_ge(mrow_ready, g + 1)
                for q in range(4):
                    ins = pe.transpose(ps[:, 7, q * P:(q + 1) * P], mrow[:, g % 3, q * P:(q + 1) * P], ident[:])
                ins.then_inc(modT_ps, 1)

            pe.wait_ge(ident_loaded, 16)
            pe.wait_ge(vecs_loaded, 7 * 16)
            pe.transpose(ps[:, 6, 0:49], vecs[:], ident[0:49, 0:49]).then_inc(vecsT_ps, 1)
            pe.wait_ge(cond_ready, 1)
            for k in range(KC):
                ada_unit(0, k)
            ada_turn(0)

            def ada_step(plan, s):
                if 1 <= s <= len(plan):
                    for g, k in plan[s - 1]:
                        if k == KC - 1:
                            ada_turn(g)
                if s < len(plan):
                    for g, k in plan[s]:
                        ada_unit(g, k)

            def turn_rows(ordinal, ready, base):
                for k in range(TILES):
                    pe.wait_ge(ready, base + k + 1)
                    for q in range(KC):
                        ins = pe.transpose(ps[:, 2 * k + q // 4, (q % 4) * P:(q % 4 + 1) * P],
                                           xn[:, k, q * P:(q + 1) * P], ident[:])
                    ins.then_inc(xT_ps, 1)

            def spread_gate(q):
                layer, second = q // 2, q % 2
                g = 3 * layer + 1 + second
                pe.wait_ge(mrow_ready, g + 1)
                for n in range(4):
                    if n or q:
                        pe.wait_ge(gbc_sb, 4 * q + n)
                    c, half = n // 2, n % 2
                    row = 32 * (2 * second + half) + c
                    pe.matmul(ps[:, 6, :], ident[:, row:row + 1].to_broadcast([P, P]), mrow[:, g % 3, :],
                              start=True, stop=True).then_inc(gbc_ps, 1)

            turn_rows(0, xn_ready, 0)

            def project(first, n, kh, s, banks, acc_sem, acc_base, hsem, hbase):
                pe.wait_ge(lo_ready, first + s + 1)
                slot = (first + s) % RING
                for k in range(TILES):
                    if hsem is not None:
                        pe.wait_ge(hsem, hbase + k + 1)
                    for q in range(4):
                        kc = kh * 4 + q
                        cols = slice(k * P, (k + 1) * P)
                        ins = mm3(ps[:, banks + k, :], h_hi[:, kc, cols], h_lo[:, kc, cols],
                                  ring_hi[:, slot, q * HALF:(q + 1) * HALF], ring_lo[:, slot, q * HALF:(q + 1) * HALF],
                                  kh == 0 and q == 0, kh == 1 and q == 3)
                    if kh == 1 and k < 2:
                        ins.then_inc(acc_sem, 1)
                ins.then_inc(unit_used, 1)

            for s, (_, n, kh) in enumerate(QKV_UNITS):
                if kh == 0 and n >= 2:
                    pe.wait_ge(qkv_sb, 3 * (n - 1))
                project(QKV0, n, kh, s, (n % 2) * 3, qkv_acc, 2 * n, hlo_ready if s == 0 else None, 0)
                ada_step(QKV_ADA, s)
            ada_step(QKV_ADA, len(QKV_UNITS))

            def turn_heads(h):
                if h:
                    pe.wait_ge(qT_sb, h)
                    pe.wait_ge(kT_sb, h)
                else:
                    pe.wait_ge(modv_ready, 3)
                    pe.wait_ge(qkv_sb, 18)
                    pe.wait_ge(rope_done, 8)
                    pe.wait_ge(cache_loaded, 32)
                cols = slice(h * P, (h + 1) * P)
                for k in range(TILES):
                    pe.transpose(ps[:, 7, k * P:(k + 1) * P], qbuf[:, k, cols], ident[:])
                    pe.transpose(ps[:, 6, k * P:(k + 1) * P], kbuf[:, k, cols], ident[:])
                pe.transpose(ps[:, 6, TOK:HALF], gbc[:, 0, cols], ident[:]).then_inc(qkT_ps, 1)

            def scores(i):
                h, k = i // 3, i % 3
                pe.wait_ge(qT_sb, h + 1)
                pe.wait_ge(kT_sb, h + 1)
                if i >= 2:
                    pe.wait_ge(exp_done, i - 1)
                keys = slice(0, P) if k == 0 else slice(P, HALF)
                for m in range(2):
                    rows = slice(HD * m, HD * m + HD)
                    ins = pe.matmul(ps[:, 2 * (i % 2) + m, 0:(P if k == 0 else TOK)],
                                    qT[rows, h % 2, k * P:(k + 1) * P], kT[rows, h % 2, keys], start=True, stop=True)
                ins.then_inc(score_ps, 1)

            def turn_map(i):
                pe.wait_ge(a_ready, i + 1)
                if i:
                    pe.wait_ge(aT_sb, i)
                for b in range(1 if i % 3 == 0 else 3):
                    ins = pe.transpose(ps[:, 4, b * P:(b + 1) * P], amap[:, i % 2, b * P:(b + 1) * P], ident[:])
                ins.then_inc(aT_ps, 1)

            def values(i):
                h, k = i // 3, i % 3
                cols = slice(h * P, (h + 1) * P)
                pe.wait_ge(aT_sb, i + 1)
                if i:
                    pe.wait_ge(o_sb, i)
                vs = [v[:, 0, cols]] if k == 0 else [v[:, 1, cols], v[:, 2, cols], gbc[:, 1, cols]]
                for b, vb in enumerate(vs):
                    ins = pe.matmul(ps[:, 5, k * P:(k + 1) * P], aT[:, i % 2, b * P:(b + 1) * P], vb,
                                    start=(b == 0), stop=(b == len(vs) - 1))
                ins.then_inc(o_ps, 1)

            turn_heads(0)
            scores(0)
            for i in range(24):
                if i % 3 == 1 and i // 3 + 1 < HEADS:
                    turn_heads(i // 3 + 1)
                if i + 1 < 24:
                    scores(i + 1)
                turn_map(i)
                values(i)
            pe.wait_ge(o_sb, 24)
            turn_rows(1, on_ready, 0)
            spread_gate(0)

            def projection(first, w, hsem, hbase):
                for s in range(4):
                    n, kh = s // 2, s % 2
                    project(first, n, kh, s, 3 * n, proj_acc, 4 * w + 2 * n, hsem if s == 0 else None, hbase)

            pe.wait_ge(h32_ready, 6)
            projection(WO0, 0, hlo_ready, 3)
            turn_rows(2, xn_ready, 3)
            spread_gate(1)

            pe.wait_ge(hlo_ready, 9)
            for s, (kind, c, kh) in enumerate(FFN_UNITS):
                pe.wait_ge(lo_ready, FFN0 + s + 1)
                slot = (FFN0 + s) % RING
                if kind == "gu":
                    if kh == 0 and c:
                        pe.wait_ge(ffh_ready, 2 * c)
                    for q in range(4):
                        for b in range(4):
                            w = q * HALF + (b % 2) * 256 + (b // 2) * P
                            cols = slice(w, w + P)
                            kc = kh * 4 + q
                            ins = mm3(ps[:, b, 0:TOK], ring_hi[:, slot, cols], ring_lo[:, slot, cols],
                                      h_hi[:, kc, :], h_lo[:, kc, :], kh == 0 and q == 0, kh == 1 and q == 3)
                else:
                    pe.wait_ge(fflo_ready, 2 * c + 2)
                    if c == 0:
                        pe.wait_ge(gbc_sb, 8)
                    for n in range(6):
                        k, half = n // 2, n % 2
                        if 6 * c + n >= 3:
                            pe.wait_ge(y_added, 6 * c + n - 2)
                        for j in range(2):
                            cols = slice(k * P, (k + 1) * P)
                            w = slice(j * D + half * HALF, j * D + (half + 1) * HALF)
                            ins = mm3(ps[:, 4 + n % 3, :], ff_hi[:, c % 2, j, cols], ff_lo[:, c % 2, j, cols],
                                      ring_hi[:, slot, w], ring_lo[:, slot, w], j == 0, j == 1)
                        if n < 5:
                            ins.then_inc(y_ps, 1)
                ins.then_inc(unit_used, 1)
                ada_step(FFN_ADA, s)
            ada_step(FFN_ADA, NU)

            turn_rows(3, xn_ready, 6)
            spread_gate(2)
            pe.wait_ge(h32_ready, 12)
            pe.wait_ge(dft_loaded, 48)
            for n in range(12):
                k, g = n // 4, n % 4
                if n >= 6:
                    pe.wait_ge(dft1_act if n % 2 == 0 else dft1_dve, (n - 6) // 2 + 1)
                for q in range(2):
                    ins = pe.matmul(ps[:, n % 6, :], h32[:, 2 * g + q, k * P:(k + 1) * P], dft_ch[:, q, :],
                                    start=(q == 0), stop=(q == 1))
                ins.then_inc(dft1_ps, 1)
            pe.wait_ge(dft1_act, 6)
            pe.wait_ge(dft1_dve, 6)
            for q in range(KC):
                cols = slice(q * P, (q + 1) * P)
                if q >= 6:
                    pe.wait_ge(ft_lo, q - 5)
                pe.matmul(ps[:, q % 6, 0:P], f_cos[:, 0, cols], dft_p[:, 0, :], start=True, stop=False)
                pe.matmul(ps[:, q % 6, 0:P], f_sin[:, 0, cols], dft_p[:, 1, :], start=False, stop=True)
                for k in range(2):
                    pe.matmul(ps[:, q % 6, P:TOK], f_cos[:, 1 + k, cols], dft_s[:, k, 0, :], start=(k == 0), stop=False)
                    ins = pe.matmul(ps[:, q % 6, P:TOK], f_sin[:, 1 + k, cols], dft_s[:, k, 1, :],
                                    start=False, stop=(k == 1))
                ins.then_inc(dft2_ps, 1)
            pe.wait_ge(ft_lo, KC)
            projection(WF0, 1, None, 0)
            turn_rows(4, xn_ready, 9)
            spread_gate(3)

            pe.wait_ge(h32_ready, 15)
            pe.wait_ge(gbc_sb, 16)
            pe.wait_ge(route_loaded, 48)
            for k in range(TILES):
                for q in range(KC):
                    ins = pe.matmul(ps[:, 6, k * N_EXP:(k + 1) * N_EXP], h32[:, q, k * P:(k + 1) * P], wr[:, q, :],
                                    start=(q == 0), stop=(q == KC - 1))
            ins.then_inc(logit_ps, 1)
            for n in range(2 * TILES):
                for q in range(4):
                    ins = pe.transpose(ps[:, n, q * P:(q + 1) * P],
                                       h32[:, 4 * (n % 2) + q, (n // 2) * P:(n // 2 + 1) * P], ident[:])
                ins.then_inc(tokT_ps, 1)
            pe.wait_ge(mask_ready, 1)
            pe.wait_ge(const_ready, 2)
            for k in range(TILES):
                out = ps[:, 6, k * N_EXP:(k + 1) * N_EXP]
                for b in range(k):
                    pe.matmul(out, ones[:].to_broadcast([P, P]), mask[:, b, :], start=(b == 0), stop=False)
                pe.matmul(out, tri[:], mask[:, k, :], start=(k == 0), stop=True)
            for k in range(TILES):
                ins = pe.matmul(ps[:, 6, 24:32], ones[:].to_broadcast([P, P]), mask[:, k, :],
                                start=(k == 0), stop=(k == TILES - 1))
            ins.then_inc(pos_ps, 1)
            pe.wait_ge(tok_lo_ready, 6)

            pe.wait_ge(meta_ready, 1)
            blocks = pe.value_load(meta[0:1, EXTRA:EXTRA + 1], min_val=0, max_val=EXTRA)

            with pe.Fori(0, PAIRS) as i:
                pe.wait_ge(sel_ready, i + 1)
                for j in range(2):
                    for k in range(TILES):
                        ins = pe.transpose(ps[:, 4 + j, k * P:(k + 1) * P], sel[:, k, j, :].bitcast(F32), ident[:])
                    ins.then_inc(selT_ps, 1)
                for q in range(KC):
                    if q >= 2:
                        pe.wait_ge(xe_act if q % 2 == 0 else xe_dve, 4 * i + (q - 2) // 2 + 1)
                    for b, part in enumerate((tok_hi, tok_lo)):
                        for k in range(TILES):
                            ins = pe.matmul(ps[:, 6 + q % 2, b * 256:(b + 1) * 256], part[:, k, q * P:(q + 1) * P],
                                            sel[:, k, :, :].rearrange("p j n -> p (j n)"),
                                            start=(k == 0), stop=(k == TILES - 1))
                    ins.then_inc(xe_ps, 1)
                pe.wait_ge(xe_act, 4 * i + 4)
                pe.wait_ge(xe_dve, 4 * i + 4)
                pe.wait_ge(selT_sb, 2 * i + 2)

                def turn_hidden(j, c):
                    b = par(j, c)
                    pe.wait_ge(eh_ready, nth(i, j, c) + 1)
                    for s in range(2):
                        ins = pe.transpose(ps[:, 2 + b, s * P:(s + 1) * P], eh[:, b, s * P:(s + 1) * P], ident[:])
                    ins.then_inc(ehT_ps, 1)

                for m in range(PER_PAIR):
                    j = m // NU
                    kind, c, kh = FFN_UNITS[m % NU]
                    n, b = nth(i, j, c), par(j, c)
                    if kind == "gu" and kh == 1 and c >= 1:
                        turn_hidden(j, c - 1)
                    if kind == "down" and c == FFC - 1:
                        turn_hidden(j, c)
                    pe.wait_ge(lo_ready, MOE0 + m + 1 + PER_PAIR * i)
                    slot = (MOE0 + m) % RING
                    if kind == "gu":
                        for q in range(4):
                            kc = kh * 4 + q
                            rows = slice(j * P, (j + 1) * P)
                            ins = mm3(ps[:, b, :], xe[:, kc, 0, rows], xe[:, kc, 1, rows],
                                      ring_hi[:, slot, q * HALF:(q + 1) * HALF], ring_lo[:, slot, q * HALF:(q + 1) * HALF],
                                      kh == 0 and q == 0, kh == 1 and q == 3)
                    else:
                        pe.wait_ge(eh_lo_ready, n + 1)
                        if c == 0 and j:
                            pe.wait_ge(ey_lo_ready, 2 * i + 1)
                        for s in range(2):
                            for half in range(2):
                                w = slice(s * D + half * HALF, s * D + (half + 1) * HALF)
                                ins = mm3(ps[:, 4 + half, :], eh_hi[:, b, s, :], eh_lo[:, b, s, :],
                                          ring_hi[:, slot, w], ring_lo[:, slot, w],
                                          c == 0 and s == 0, c == FFC - 1 and s == 1)
                    ins.then_inc(unit_used, 1)
                    if kind == "down" and c == FFC - 1:
                        pe.wait_ge(ey_lo_ready, 2 * i + j + 1)
                        for o in range(6):
                            k, half = o // 2, o % 2
                            if o >= 2:
                                pe.wait_ge(comb_sb, 12 * i + 6 * j + o - 1)
                            for r, part in enumerate((y_hi, y_lo)):
                                ins = pe.matmul(ps[:, 6 + o % 2, :], selT[:, j, k * P:(k + 1) * P],
                                                part[:, half * HALF:(half + 1) * HALF], start=(r == 0), stop=(r == 1))
                            ins.then_inc(comb_ps, 1)

            pe.wait_ge(comb_sb, 12 * PAIRS)
            with pe.If(blocks > 0):
                with pe.Fori(0, EXTRA) as b:
                    pe.wait_ge(x_sel, b + 1)
                    for k in range(TILES):
                        ins = pe.transpose(ps[:, 2, k * P:(k + 1) * P], sel[:, k, 0, :].bitcast(F32), ident[:])
                    ins.then_inc(x_selT_ps, 1)
                    for q in range(KC):
                        for r, part in enumerate((tok_hi, tok_lo)):
                            for k in range(TILES):
                                ins = pe.matmul(ps[:, q // 4, (q % 4) * P:(q % 4 + 1) * P],
                                                part[:, k, q * P:(q + 1) * P], sel[:, k, 0, :],
                                                start=(r == 0 and k == 0), stop=(r == 1 and k == TILES - 1))
                    ins.then_inc(x_tok_ps, 1)
                    pe.wait_ge(x_tok_sb, b + 1)
                    pe.wait_ge(x_selT_sb, b + 1)

                    def turn_extra(c):
                        pe.wait_ge(x_h, FFC * b + c + 1)
                        for s in range(2):
                            ins = pe.transpose(ps[:, 0, s * P:(s + 1) * P], eh[:, 0, s * P:(s + 1) * P], ident[:])
                        ins.then_inc(x_hT_ps, 1)

                    for m, (kind, c, kh) in enumerate(FFN_UNITS):
                        if kind == "gu" and kh == 0 and c:
                            turn_extra(c - 1)
                        if kind == "down" and c == FFC - 1:
                            turn_extra(c)
                        slot = m % RING
                        pe.wait_ge(x_loaded_w[slot], x_unit_loaded[m] + x_slot_total[slot] * b)
                        if kind == "gu":
                            for q in range(4):
                                ins = pe.matmul(ps[:, 3, :], x_tok[:, kh * 4 + q, :],
                                                raw[:, slot, q * HALF:(q + 1) * HALF],
                                                start=(kh == 0 and q == 0), stop=(kh == 1 and q == 3))
                        else:
                            pe.wait_ge(x_hT_sb, FFC * b + c + 1)
                            for s in range(2):
                                for half in range(2):
                                    w = slice(s * D + half * HALF, s * D + (half + 1) * HALF)
                                    ins = pe.matmul(ps[:, 4 + half, :], x_hT[:, s, :], raw[:, slot, w],
                                                    start=(c == 0 and s == 0), stop=(c == FFC - 1 and s == 1))
                        ins.then_inc(x_used, 1)
                    pe.wait_ge(x_y_sb, b + 1)
                    for n in range(6):
                        k, half = n // 2, n % 2
                        if n >= 2:
                            pe.wait_ge(x_comb_sb, 6 * b + n - 1)
                        pe.matmul(ps[:, 6 + n % 2, :], selT[:, 0, k * P:(k + 1) * P].bitcast(F32),
                                  x_y[:, half * HALF:(half + 1) * HALF], start=True, stop=True).then_inc(x_comb_ps, 1)
            pe.end_ifs()


_INS = ["x_prompt", "x_sample", "c", "cache_k_0", "cache_v_0", "c_ctx",
        "ada_w_0", "ada_b_0", "norm1_g_0", "norm2_g_0", "w_qkv_0",
        "lambda_q1_0", "lambda_k1_0", "lambda_q2_0", "lambda_k2_0", "subln_g_0", "w_o_0",
        "w_gu_0", "w_down_0", "ada_w_1", "ada_b_1", "norm1_g_1", "norm2_g_1", "w_fourier_1",
        "w_router_1", "w_gu_e_1", "w_down_e_1", "final_norm_g"]
_OUTS = [("y_prompt", (1, 128, 1024)), ("y_sample", (1, 256, 1024)),
         ("k_ctx", (1, 128, 8, 128)), ("v_ctx", (1, 128, 8, 128))]


def shape_constants():
    f = np.float32
    rows = 256 // 64
    row = np.repeat(np.arange(rows), 64).astype(f)
    col = np.tile(np.arange(64), rows).astype(f)
    inv = (f(1.0) / (f(10000.0) ** (np.arange(0, 32, 2, dtype=f) / f(32)))).astype(f)
    ar, ac = row[:, None] * inv[None, :], col[:, None] * inv[None, :]
    ang = np.concatenate([ar, ar, ac, ac], axis=-1).astype(np.float64)
    sign = np.tile(np.repeat([-1.0, 1.0], 16), 2)

    def wave(n):
        a = 2 * np.pi * (np.outer(np.arange(n), np.arange(n)) % n) / n
        return np.cos(a), np.sin(a)

    c256, s256 = wave(256)
    c128, s128 = wave(128)
    return {
        "ident": np.eye(128, dtype=f),
        "iota": np.tile(np.arange(128, dtype=f), (128, 1)),
        "tri": np.triu(np.ones((128, 128), f), 1),
        "rope_cos": np.cos(ang).astype(f),
        "rope_sin": (np.sin(ang) * sign).astype(f),
        "dft_ch": (np.concatenate([c256, s256], axis=1) / 16).astype(f),
        "dft_p": (np.concatenate([c128, -s128], axis=1) / np.sqrt(128)).astype(f),
        "dft_s": (np.concatenate([c256, -s256], axis=1) / 16).astype(f),
    }


def kernel(**inputs):
    import concourse.bacc as bacc
    from concourse.bass_utils import run_bass_kernel_spmd

    nc = bacc.Bacc("TRN2", target_bir_lowering=False, num_devices=1)
    arrays, args = {}, {}
    for name, a in list((n, inputs[n]) for n in _INS) + list(shape_constants().items()):
        a = np.ascontiguousarray(a)
        arrays[f"in_{name}"] = a
        args[name] = nc.dram_tensor(f"in_{name}", a.shape, mybir.dt.from_np(a.dtype), kind="ExternalInput").ap()
    for name, shape in _OUTS:
        out = nc.dram_tensor(f"out_{name}", shape, F32, kind="ExternalOutput").ap()
        args[name] = out.rearrange("b p h d -> (b p) (h d)") if len(shape) == 4 else out
    build(nc, args)
    r = run_bass_kernel_spmd(nc, [arrays], core_ids=[0])
    return tuple(np.asarray(r.results[0][f"out_{name}"]) for name, _ in _OUTS)
```

```python
from contextlib import ExitStack

import numpy as np

import concourse.bass as bass
from concourse import mybir

F32 = mybir.dt.float32
F32R = mybir.dt.float32r
I32 = mybir.dt.int32
U32 = mybir.dt.uint32
ALU = mybir.AluOpType
ACT = mybir.ActivationFunctionType
AX = mybir.AxisListType

P = 128
D = 1024
KC = D // P
TILES = 3
TOK = TILES * P
GATE_GROUPS = (1, 2, 4, 5)
COND = (0, 1, 1)
HEADS = 8
HD = 64
D_FF = 2816
N_EXP = 8
FFC = D_FF // 256
EPS = 1e-6
SUBLN_EPS = 1e-5
LAMBDA_INIT = 0.2
SCALE = HD ** -0.5
HALF = 512

UNIT = 2048
RAW = 6
RING = 3


def ffn_units():
    out = []
    for c in range(FFC):
        out += [("gu", c, 0), ("gu", c, 1)]
        if c:
            out.append(("down", c - 1, 0))
    return out + [("down", FFC - 1, 0)]


FFN_UNITS = ffn_units()
NU = len(FFN_UNITS)


QKV_UNITS = [("qkv", n, kh) for n in range(6) for kh in range(2)]
ITEMS = HEADS * TILES


def ada_at(item):
    n = 2 * (item - 1)
    return [(1 + m // KC, m % KC) for m in (n, n + 1)] if 0 <= n < 5 * KC else []


def ada_complete(item):
    before = ada_at(item - 1)
    return before[1][0] if before and before[1][1] == KC - 1 else None


def stream_before_experts():
    s = [("ada", 0, k) for k in range(KC)]
    s += QKV_UNITS
    s += [("ada", g, k) for g in range(1, 6) for k in range(KC)]
    s += [("wo", n, kh) for n in range(2) for kh in range(2)]
    s += FFN_UNITS
    s += [("wf", n, kh) for n in range(2) for kh in range(2)]
    return s


STREAM = stream_before_experts()
SPLIT_AT = [u for u, it in enumerate(STREAM) if it[0] != "ada"]
ADA_AT = [u for u, it in enumerate(STREAM) if it[0] == "ada"]
QKV0, WO0 = 0, len(QKV_UNITS)
FFN0 = WO0 + 4
WF0 = FFN0 + NU
MOE0 = WF0 + 4
MOE_U0 = len(STREAM)
PAIRS = N_EXP // 2
EXTRA = (2 * TOK) // (P + 1)
PER_PAIR = 2 * NU
AHEAD = 2
COMBINE_AT = (2, 3, 4)
NEXT_SEL_AT = 6
ROWS_AT = (8, 12)
TURN_AT = (10, 14)
SELT_AT = 16
assert PER_PAIR % RAW == 0 and PER_PAIR % RING == 0 and len(SPLIT_AT) == MOE0


def build(nc, t):
    with ExitStack() as ctx:
        def sb(name, shape, dt=F32, stack=ctx):
            return stack.enter_context(nc.sbuf_tensor(name, shape, dt))

        def sem(name):
            return ctx.enter_context(nc.semaphore(name))

        ps = ctx.enter_context(nc.psum_tensor("ps", [P, 8, HALF], F32))

        raw = sb("raw", [P, RAW, UNIT])
        ring_hi = sb("ring_hi", [P, RING, UNIT], F32R)
        ring_lo = sb("ring_lo", [P, RING, UNIT], F32R)
        x = sb("x", [P, TILES, D])
        mrow = sb("mrow", [P, 2, HALF])
        gates = sb("gates", [P, HALF])
        lane = sb("lane", [P, 6])
        gbc = sb("gbc", [P, 2, D])
        ident = sb("ident", [P, P])
        iota = sb("iota", [P, P])
        tri = sb("tri", [P, P])
        ones = sb("ones", [P, 1])
        wr = sb("wr", [P, KC, N_EXP])
        vecs = sb("vecs", [49, P])
        vecsT = sb("vecsT", [P, 49])
        cond_t = sb("cond_t", [P, 2, KC])
        cond = sb("cond", [P, KC, 32])
        modv = sb("modv", [P, 6, 2, KC, 2])
        mod_a = sb("mod_a", [P, 4, KC, 2])
        sub_g = sb("sub_g", [P, 1])
        lamv = sb("lamv", [P, 4, HD])
        lams = sb("lams", [P, 4])
        junk = sb("junk", [P, HD])
        lam = sb("lam", [P, 1])
        ssq = sb("ssq", [P, 5, TILES])
        msq = sb("msq", [P, 5, TILES])
        rstd = sb("rstd", [P, 5, TILES])
        mhalf = sb("mhalf", [P, 24])
        o_ssq = sb("o_ssq", [P, TILES, HEADS])
        o_msq = sb("o_msq", [P, TILES, HEADS])
        o_rstd = sb("o_rstd", [P, TILES, HEADS])
        mx = sb("mx", [P, 2, 2])
        nmx = sb("nmx", [P, 2, 2])
        sums = sb("sums", [P, 2, 2])
        rs = sb("rs", [P, 2, 2])
        l1 = sb("l1", [P, 2])
        lg = sb("lg", [P, TILES, N_EXP])
        lmax = sb("lmax", [P, TILES])
        pr = sb("pr", [P, TILES, N_EXP])
        psumr = sb("psumr", [P, TILES])
        prec = sb("prec", [P, TILES])
        top = sb("top", [P, TILES, 8])
        topi = sb("topi", [P, TILES, 8], U32)
        topf = sb("topf", [P, TILES, 8])
        tsum = sb("tsum", [P, TILES])
        trec = sb("trec", [P, TILES])
        tg = sb("tg", [P, TILES, 2])
        oh1 = sb("oh1", [P, TILES, N_EXP])
        oh2 = sb("oh2", [P, TILES, N_EXP])
        mask = sb("mask", [P, TILES, N_EXP])
        gate = sb("gate", [P, TILES, N_EXP])
        posm = sb("posm", [P, TILES, N_EXP + 1])
        pos_col = sb("pos_col", [P, TILES])
        gate_col = sb("gate_col", [P, TILES])
        cnt = sb("cnt", [P, N_EXP])
        ext = sb("ext", [P, 2, N_EXP])
        cum = sb("cum", [P, 2, N_EXP])
        pick = sb("pick", [P, EXTRA, 2, N_EXP])
        meta_f = sb("meta_f", [P, 8])
        meta = sb("meta", [P, 8], I32)
        start = sb("start", [P, EXTRA])
        x_place = sb("x_place", [P, EXTRA, TILES])
        x_gate = sb("x_gate", [P, EXTRA, TILES])
        x_tmp = sb("x_tmp", [P, TILES, N_EXP])

        def over(stack_fn):
            with ExitStack() as s:
                return stack_fn(s)

        def phase_h(s):
            return (sb("h_hi", [P, KC, TOK], F32R, s), sb("h_lo", [P, KC, TOK], F32R, s))

        def phase_attn(s):
            return (sb("qT", [P, 2, TOK], F32, s), sb("kT", [P, 2, HALF], F32, s),
                    sb("prob", [P, 2, 2, TOK], F32, s), sb("amap", [P, 2, TOK], F32, s),
                    sb("aT", [P, 2, TOK], F32, s))

        h_hi, h_lo = over(phase_h)
        qT, kT, prob, amap, aT = over(phase_attn)

        def dense(s):
            sb("skip_h", [P, 2, KC, TOK], F32, s)
            h32 = sb("h32", [P, KC, TOK], F32, s)
            xn = sb("xn", [P, TILES, D], F32, s)
            dft_ch = sb("dft_ch", [P, 2, HALF], F32, s)
            dft_p = sb("dft_p", [P, 2, P], F32, s)
            dft_s = sb("dft_s", [P, 2, 2, 256], F32, s)
            with ExitStack() as q:
                v = sb("v", [P, TILES, D], F32, q)
                cos = sb("cos", [P, 2, HD], F32, q)
                sin = sb("sin", [P, 2, HD], F32, q)
                rope_a = sb("rope_a", [P, HALF], F32, q)
                rope_b = sb("rope_b", [P, HALF], F32, q)
            with ExitStack() as q:
                ff_hi = sb("ff_hi", [P, 2, 2, TOK], F32R, q)
                ff_lo = sb("ff_lo", [P, 2, 2, TOK], F32R, q)
                tnh = sb("tnh", [P, 2, TOK], F32, q)
                hb = sb("hb", [P, 2, TOK], F32, q)
            with ExitStack() as q:
                f_sin = sb("f_sin", [P, TILES, D], F32, q)
            return h32, xn, dft_ch, dft_p, dft_s, v, cos, sin, rope_a, rope_b, ff_hi, ff_lo, tnh, hb, f_sin

        (h32, xn, dft_ch, dft_p, dft_s, v, cos, sin, rope_a, rope_b,
         ff_hi, ff_lo, tnh, hb, f_sin) = over(dense)

        def one_or_other(s):
            with ExitStack() as q:
                xe = sb("xe", [P, 2, 2, KC, P], F32R, q)
            with ExitStack() as q:
                more = (sb("x_tok", [P, KC, P], F32, q), sb("x_hT", [P, 2, P], F32, q), sb("x_y", [P, D], F32, q))
            sb("xe_space", [P, 2, 2, KC, P], F32, s)
            return xe, more

        def experts(s):
            return (sb("tok_hi", [P, TILES, D], F32R, s), sb("tok_lo", [P, TILES, D], F32R, s),
                    sb("acc", [P, TILES, D], F32, s),
                    one_or_other(s),
                    sb("sel", [P, 2, TILES, P], F32R, s), sb("selT", [P, 2, TOK], F32R, s),
                    sb("y_hi", [P, D], F32R, s), sb("y_lo", [P, D], F32R, s),
                    sb("eh_hi", [P, 2, 2, P], F32R, s), sb("eh_lo", [P, 2, 2, P], F32R, s),
                    sb("et", [P, 2, 256], F32, s), sb("eh", [P, 2, 256], F32, s),
                    sb("gathered", [P, HALF], F32, s))

        (tok_hi, tok_lo, acc, (xe, (x_tok, x_hT, x_y)), sel, selT, y_hi, y_lo, eh_hi, eh_lo, et, eh, gathered) = over(experts)

        kbuf = h32[:].rearrange("p k m -> p (k m)").rearrange("p (t n) -> p t n", t=TILES)
        qbuf = xn
        obuf = xn
        yacc = xn
        f_cos = xn
        final_g = mrow[:, 0:2, :].rearrange("p a n -> p (a n)")

        raw_loaded = [sem(f"raw_loaded{i}") for i in range(RAW)]
        hi_ready, lo_ready, unit_used, ada_used = map(sem, ("hi_ready", "lo_ready", "unit_used", "ada_used"))
        x_loaded, vecs_loaded, ident_loaded, lam_loaded = map(sem, ("x_loaded", "vecs_loaded", "ident_loaded", "lam_loaded"))
        rope_loaded, cache_loaded, dft_loaded, route_loaded, final_g_loaded = map(
            sem, ("rope_loaded", "cache_loaded", "dft_loaded", "route_loaded", "final_g_loaded"))
        lane_loaded, gates_ready = map(sem, ("lane_loaded", "gates_ready"))
        bias_loaded = [sem(f"bias_loaded{g}") for g in range(6)]
        const_ready, vecsT_ps, vecsT_sb, cond_tanh, cond_ready, vch, lam_exp, lam_sum = map(
            sem, ("const_ready", "vecsT_ps", "vecsT_sb", "cond_tanh", "cond_ready", "vch", "lam_exp", "lam_sum"))
        mrow_ready, modT_ps, modv_ready, mod_a_ready = map(
            sem, ("mrow_ready", "modT_ps", "modv_ready", "mod_a_ready"))
        ssq_ready, msq_ready, rstd_ready, xn_ready, xT_ps, h32_ready, h32_upper, hhi_ready, hlo_ready, x_upd = map(
            sem, ("ssq_ready", "msq_ready", "rstd_ready", "xn_ready", "xT_ps", "h32_ready", "h32_upper", "hhi_ready", "hlo_ready", "x_upd"))
        qkv_acc, qkv_sb, rope_done, ctx_stored = map(sem, ("qkv_acc", "qkv_sb", "rope_done", "ctx_stored"))
        qkT_ps, qT_sb, kT_sb, score_ps, negmax, exp_done, a_ready, aT_ps, aT_sb, o_ps, o_sb = map(
            sem, ("qkT_ps", "qT_sb", "kT_sb", "score_ps", "negmax", "exp_done", "a_ready", "aT_ps", "aT_sb", "o_ps", "o_sb"))
        o_sq, o_sum, o_ms, o_rs, on_ready = map(sem, ("o_sq", "o_sum", "o_ms", "o_rs", "on_ready"))
        gbc_ps, gbc_sb, proj_acc = map(sem, ("gbc_ps", "gbc_sb", "proj_acc"))
        tanh_ready, ffh_ready, ffhi_ready, fflo_ready, y_ps, y_added = map(
            sem, ("tanh_ready", "ffh_ready", "ffhi_ready", "fflo_ready", "y_ps", "y_added"))
        dft1_ps, dft1_act, dft1_dve, dft2_ps, ft_hi, ft_lo = map(
            sem, ("dft1_ps", "dft1_act", "dft1_dve", "dft2_ps", "ft_hi", "ft_lo"))
        logit_ps, logit_sb, r_neg, r_exp, mask_ready, pos_ps, pos_sb, gate_ready = map(
            sem, ("logit_ps", "logit_sb", "r_neg", "r_exp", "mask_ready", "pos_ps", "pos_sb", "gate_ready"))
        tokT_ps, tok_hi_ready, tok_lo_ready, zeroed = map(sem, ("tokT_ps", "tok_hi_ready", "tok_lo_ready", "zeroed"))
        cols_ready, sel_ready, selT_ps, selT_sb, rows_ps, rows_sb, xe_ps, xe_hi_ready, xe_lo_ready = map(
            sem, ("cols_ready", "sel_ready", "selT_ps", "selT_sb", "rows_ps", "rows_sb", "xe_ps", "xe_hi_ready",
                  "xe_lo_ready"))
        et_ready, ea_ready, eh_ready, ehT_ps, eh_hi_ready, eh_lo_ready = map(
            sem, ("et_ready", "ea_ready", "eh_ready", "ehT_ps", "eh_hi_ready", "eh_lo_ready"))
        ey_hi_ready, ey_lo_ready, comb_ps, comb_sb, y_ready, y_stored, cnt_ready, xch = map(
            sem, ("ey_hi_ready", "ey_lo_ready", "comb_ps", "comb_sb", "y_ready", "y_stored", "cnt_ready", "xch"))

        meta_ready, x_sel, x_selT_ps, x_tok_ps, x_selT_sb, x_tok_sb, x_used = map(
            sem, ("meta_ready", "x_sel", "x_selT_ps", "x_tok_ps", "x_selT_sb", "x_tok_sb", "x_used"))
        x_tanh, x_h_half, x_h, x_hT_ps, x_hT_sb, x_y_sb, x_comb_ps, x_comb_sb = map(
            sem, ("x_tanh", "x_h_half", "x_h", "x_hT_ps", "x_hT_sb", "x_y_sb", "x_comb_ps", "x_comb_sb"))
        x_loaded_w = [sem(f"x_loaded_w{i}") for i in range(RING)]

        block = ctx.enter_context(nc.Block())

        w_rows = {
            "qkv": t["w_qkv_0"].rearrange("(k p) n -> p k n", p=P),
            "wo": t["w_o_0"].rearrange("(k p) n -> p k n", p=P),
            "wf": t["w_fourier_1"].rearrange("(k p) n -> p k n", p=P),
        }
        ada_rows = [t[f"ada_w_{l}"].rearrange("(k p) n -> p k n", p=P) for l in range(2)]

        def gu_source(w, c, kh):
            return w.rearrange("(k p) (u n) -> p k u n", p=P, u=2)[:, kh * 4:kh * 4 + 4, :, c * 256:c * 256 + 256]

        def down_source(w, c):
            return w.rearrange("(s p) n -> p s n", p=P)[:, 2 * c:2 * c + 2, :]

        def slot_view(slot, kind):
            s = raw[:, slot, :]
            if kind == "gu":
                return s.rearrange("p (k u n) -> p k u n", k=4, u=2)
            if kind == "down":
                return s.rearrange("p (s n) -> p s n", s=2)
            if kind == "ada":
                return s
            return s.rearrange("p (k n) -> p k n", k=4)

        def par(j, c):
            return (FFC * j + c) % 2

        def nth(i, j, c):
            return 2 * FFC * i + FFC * j + c


        def down_used(i, j, c):
            jj, cc = (j, c - 2) if c >= 2 else (j - 1, c - 2 + FFC)
            return MOE0 + NU * jj + FFN_UNITS.index(("down", cc, 0)) + 1 + PER_PAIR * i

        NORMS = ((0, 0, 0, 1, 16), (1, 1, 2, 0, 24), (3, 0, 3, 1, 32), (4, 1, 5, 0, 40))

        @block.sync
        def _(sp):
            def load(slot, kind, a, b, source=None, loaded=raw_loaded):
                dst = slot_view(slot, kind)
                if kind == "ada":
                    src = ada_rows[a // 3][:, b, (a % 3) * UNIT:(a % 3 + 1) * UNIT]
                elif kind == "gu":
                    src = gu_source(source[0], a, b)
                elif kind == "down":
                    src = down_source(source[1], a)
                else:
                    src = w_rows[kind][:, b * 4:b * 4 + 4, a * HALF:a * HALF + HALF]
                if kind == "gu":
                    for g in range(2):
                        sp.dma_start(dst[:, :, g, :], src[:, :, g, :]).then_inc(loaded[slot], 16)
                else:
                    sp.dma_start(dst, src).then_inc(loaded[slot], 16)

            for u, (kind, a, b) in enumerate(STREAM):
                if u >= RAW:
                    before = u - RAW
                    if STREAM[before][0] == "ada":
                        sp.wait_ge(ada_used, ADA_AT.index(before) + 1)
                    else:
                        sp.wait_ge(lo_ready, SPLIT_AT.index(before) + 1)
                load(u % RAW, kind, a, b, (t["w_gu_0"], t["w_down_0"]))
            with sp.Fori(0, PAIRS) as i:
                for m in range(PER_PAIR):
                    kind, c, kh = FFN_UNITS[m % NU]
                    e = 2 * i + m // NU
                    u = MOE_U0 + m
                    sp.wait_ge(lo_ready, MOE0 + m - RAW + 1 + PER_PAIR * i)
                    load(u % RAW, kind, c, kh, (t["w_gu_e_1"][e], t["w_down_e_1"][e]))
            for m in range(AHEAD):
                kind, c, kh = FFN_UNITS[m]
                sp.wait_ge(lo_ready, MOE0 + PER_PAIR * PAIRS + m - RAW + 1)
                load((MOE_U0 + m) % RAW, kind, c, kh, (t["w_gu_e_1"][N_EXP - 1], None))
            sp.wait_ge(meta_ready, 1)
            blocks = sp.value_load(meta[0:1, EXTRA:EXTRA + 1], min_val=0, max_val=EXTRA)
            sp.wait_ge(lo_ready, MOE0 + PER_PAIR * PAIRS + AHEAD)
            with sp.If(blocks > 0):
                with sp.Fori(0, EXTRA) as b:
                    e = sp.value_load(meta[0:1, bass.ds(b, 1)], min_val=0, max_val=N_EXP - 1)
                    for m, (kind, c, kh) in enumerate(FFN_UNITS):
                        if m < RING:
                            sp.wait_ge(x_sel, b + 1)
                        else:
                            sp.wait_ge(x_used, NU * b + m - RING + 1)
                        load(m % RING, kind, c, kh, (t["w_gu_e_1"][e], t["w_down_e_1"][e]), x_loaded_w)
            sp.end_ifs()
            sp.wait_ge(ctx_stored, 32)
            sp.wait_ge(y_stored, 48)

        x_unit_loaded, x_slot_total = [], [0] * RING
        for m in range(NU):
            x_slot_total[m % RING] += 32 if FFN_UNITS[m][0] == "gu" else 16
            x_unit_loaded.append(x_slot_total[m % RING])

        per_slot = [0] * RAW
        loaded_at = []
        for u, (kind, a, b) in enumerate(STREAM):
            per_slot[u % RAW] += 32 if kind == "gu" else 16
            loaded_at.append(per_slot[u % RAW])
        moe_loaded, moe_slot_total = [], [0] * RAW
        for m in range(PER_PAIR):
            s = (MOE_U0 + m) % RAW
            moe_slot_total[s] += 32 if FFN_UNITS[m % NU][0] == "gu" else 16
            moe_loaded.append(per_slot[s] + moe_slot_total[s])

        def wait_loaded(eng, u):
            eng.wait_ge(raw_loaded[u % RAW], loaded_at[u])

        def wait_moe_loaded(eng, i, m):
            s = (MOE_U0 + m) % RAW
            more = moe_slot_total[s] * (m // PER_PAIR)
            eng.wait_ge(raw_loaded[s], moe_loaded[m % PER_PAIR] + more + moe_slot_total[s] * i)

        @block.gpsimd
        def _(pool):
            def load_bias(g):
                b = t[f"ada_b_{g // 3}"]
                for j in range(4):
                    src = b[(g % 3) * UNIT + j * HALF:(g % 3) * UNIT + (j + 1) * HALF]
                    pool.dma_start(mrow[32 * j:32 * j + 32, g % 2, :],
                                   src.partition_broadcast(32)).then_inc(bias_loaded[g], 16)

            pool.memset(mhalf[:], -0.5).then_inc(const_ready, 1)
            pool.memset(ones[:], 1.0).then_inc(const_ready, 1)
            load_bias(0)
            for r, name in enumerate(("lambda_q1_0", "lambda_k1_0", "lambda_q2_0", "lambda_k2_0")):
                pool.dma_start(lamv[:, r, :], t[name].partition_broadcast(P)).then_inc(lam_loaded, 16)

            chain = [0]

            def link(ins):
                chain[0] += 1
                ins.then_inc(xch, 1)
                pool.wait_ge(xch, chain[0])

            def total(out, a):
                lead = (slice(None),) * (len(a.shape) - 1)
                for w in (4, 2, 1):
                    lower, upper = a[lead + (slice(0, w),)], a[lead + (slice(w, 2 * w),)]
                    dst = lower if w > 1 else (out.unsqueeze(2) if len(a.shape) == 3 else out)
                    link(pool.tensor_tensor(dst, lower, upper, ALU.add))

            def further_blocks():
                pool.wait_ge(cnt_ready, 1)
                pool.tensor_scalar(ext[:, 0, :], cnt[:], float(P), None, ALU.is_gt)
                link(pool.tensor_scalar(ext[:, 1, :], cnt[:], float(2 * P), None, ALU.is_gt))
                link(pool.tensor_tensor(ext[:, 0, :], ext[:, 0, :], ext[:, 1, :], ALU.add))
                link(pool.tensor_copy(cum[:, 0, :], ext[:, 0, :]))
                for e in range(1, N_EXP):
                    link(pool.tensor_tensor(cum[:, 0, e:e + 1], cum[:, 0, e:e + 1], cum[:, 0, e - 1:e], ALU.add))
                link(pool.tensor_tensor(cum[:, 1, :], cum[:, 0, :], ext[:, 0, :], ALU.subtract))
                for b in range(EXTRA):
                    pool.tensor_scalar(pick[:, b, 0, :], cum[:, 0, :], float(b), None, ALU.is_gt)
                    link(pool.tensor_scalar(pick[:, b, 1, :], cum[:, 1, :], float(b), None, ALU.is_le))
                    link(pool.tensor_tensor(pick[:, b, 0, :], pick[:, b, 0, :], pick[:, b, 1, :], ALU.mult))
                    link(pool.tensor_tensor(pick[:, b, 1, :], pick[:, b, 0, :], iota[:, 0:N_EXP], ALU.mult))
                    total(meta_f[:, b:b + 1], pick[:, b, 1, :])
                    link(pool.tensor_scalar(pick[:, b, 1, :], cum[:, 1, :], float(-P), float(P * (b + 1)), ALU.mult, ALU.add))
                    link(pool.tensor_tensor(pick[:, b, 1, :], pick[:, b, 0, :], pick[:, b, 1, :], ALU.mult))
                    total(start[:, b:b + 1], pick[:, b, 1, :])
                    chosen = pick[:, b, 0, :].unsqueeze(1).to_broadcast([P, TILES, N_EXP])
                    link(pool.tensor_scalar(x_tmp[:], posm[:, :, 0:N_EXP], 1.0, None, ALU.add))
                    link(pool.tensor_tensor(x_tmp[:], x_tmp[:], chosen, ALU.mult))
                    total(x_place[:, b, :], x_tmp[:])
                    link(pool.tensor_scalar(x_place[:, b, :], x_place[:, b, :], start[:, b:b + 1], -1.0,
                                           ALU.subtract, ALU.add))
                    link(pool.tensor_tensor(x_tmp[:], gate[:], chosen, ALU.mult))
                    total(x_gate[:, b, :], x_tmp[:])
                pool.memset(meta_f[:, EXTRA + 1:8], 0.0)
                link(pool.tensor_copy(meta_f[:, EXTRA:EXTRA + 1], cum[:, 0, N_EXP - 1:N_EXP]))
                pool.tensor_copy(meta[:], meta_f[:]).then_inc(meta_ready, 1)

            def norm_pool(n):
                for k in range(TILES):
                    pool.wait_ge(ssq_ready, 3 * n + k + 1)
                    pool.tensor_scalar(msq[:, n, k:k + 1], ssq[:, n, k:k + 1], 1.0 / D, EPS,
                                       ALU.mult, ALU.add).then_inc(msq_ready, 1)
                    pool.wait_ge(msq_ready, 3 * n + k + 1)
                    pool.tensor_tensor(rstd[:, n, k:k + 1], msq[:, n, k:k + 1], mhalf[:, 0:1],
                                       ALU.pow).then_inc(rstd_ready, 1)

            pool.wait_ge(const_ready, 2)
            norm_pool(0)
            load_bias(1)
            for c, name in enumerate(("rope_cos", "rope_sin")):
                pool.dma_start((cos, sin)[c][:], t[name].rearrange("(t p) n -> p t n", p=P)).then_inc(rope_loaded, 16)
            for c, name in enumerate(("cache_k_0", "cache_v_0")):
                pool.dma_start(gbc[:, c, :], t[name].rearrange("b p h d -> (b p) (h d)")).then_inc(cache_loaded, 16)
            pool.dma_start(lane[:], t["lane"]).then_inc(lane_loaded, 16)
            pool.dma_start(dft_ch[:], t["dft_ch"].rearrange("(k p) n -> p k n", p=P)).then_inc(dft_loaded, 16)
            pool.dma_start(dft_p[:], t["dft_p"].rearrange("p (k n) -> p k n", k=2)).then_inc(dft_loaded, 16)
            pool.dma_start(dft_s[:], t["dft_s"].rearrange("(k p) (c n) -> p k c n", p=P, c=2)).then_inc(dft_loaded, 16)
            pool.dma_start(iota[:], t["iota"]).then_inc(route_loaded, 16)
            pool.dma_start(tri[:], t["tri"]).then_inc(route_loaded, 16)
            pool.dma_start(wr[:], t["w_router_1"].rearrange("(k p) n -> p k n", p=P)).then_inc(route_loaded, 16)
            pool.wait_ge(modv_ready, 1)
            load_bias(2)
            pool.wait_ge(qkv_sb, 3 * 3 + 1)
            pool.dma_start(t["k_ctx"], kbuf[:, 0, :]).then_inc(ctx_stored, 16)
            pool.wait_ge(qkv_sb, 3 * 5 + 1)
            pool.dma_start(t["v_ctx"], v[:, 0, :]).then_inc(ctx_stored, 16)
            for g in range(3, 6):
                pool.wait_ge(modv_ready, g - 1)
                load_bias(g)
            for k in range(TILES):
                pool.wait_ge(o_sum, k + 1)
                pool.tensor_scalar(o_msq[:, k, :], o_ssq[:, k, :], 1.0 / P, SUBLN_EPS,
                                   ALU.mult, ALU.add).then_inc(o_ms, 1)
                pool.wait_ge(o_ms, k + 1)
                pool.tensor_tensor(o_rstd[:, k, :], o_msq[:, k, :], mhalf[:, 0:HEADS],
                                   ALU.pow).then_inc(o_rs, 1)
            norm_pool(1)
            pool.wait_ge(modv_ready, 6)
            pool.dma_start(final_g, t["final_norm_g"].partition_broadcast(P)).then_inc(final_g_loaded, 16)
            norm_pool(2)
            norm_pool(3)
            pool.wait_ge(tokT_ps, 2 * TILES)
            for buf in (acc[:], y_hi[:].bitcast(F32), y_lo[:].bitcast(F32), selT[:, 1, :].bitcast(F32), gate_col[:]):
                pool.memset(buf, 0.0).then_inc(zeroed, 1)
            further_blocks()
            norm_pool(4)

        @block.scalar
        def _(act):
            act.dma_start(ident[:], t["ident"]).then_inc(ident_loaded, 16)
            row = 0
            for name, n in (("c_ctx", 8), ("c", 8), ("norm1_g_0", 8), ("norm2_g_0", 8),
                            ("norm1_g_1", 8), ("norm2_g_1", 8), ("subln_g_0", 1)):
                src = t[name] if name != "c" else t[name].rearrange("b n -> (b n)")
                act.dma_start(vecs[row:row + n, :], src.rearrange("(k p) -> k p", p=P)).then_inc(vecs_loaded, 16)
                row += n
            act.dma_start(x[:, 0, :], t["x_prompt"].rearrange("b p n -> (b p) n")).then_inc(x_loaded, 16)
            act.dma_start(x[:, 1:3, :], t["x_sample"].rearrange("b (t p) n -> (b p) t n", p=P)).then_inc(x_loaded, 16)

            def split_hi(s):
                u = SPLIT_AT[s]
                wait_loaded(act, u)
                if s >= RING:
                    act.wait_ge(unit_used, s - RING + 1)
                act.activation(ring_hi[:, s % RING, :], raw[:, u % RAW, :], ACT.Copy).then_inc(hi_ready, 1)

            def x_ready(n, k):
                if n == 0:
                    act.wait_ge(x_loaded, 32)
                else:
                    act.wait_ge(x_upd, 6 * n - 3 + k + 1)

            def norm_act(n, turned, split, gate_no):
                for k in range(TILES):
                    x_ready(n, k)
                    act.activation(xn[:, k, :], x[:, k, :], ACT.Square,
                                   accum_out=ssq[:, n, k:k + 1]).then_inc(ssq_ready, 1)
                for k in range(TILES):
                    act.wait_ge(rstd_ready, 3 * n + k + 1)
                    act.activation(xn[:, k, :], x[:, k, :], ACT.Copy, scale=rstd[:, n, k:k + 1]).then_inc(xn_ready, 1)
                modulate(n, turned)
                if gate_no is not None:
                    spread_gate(gate_no)
                if split is not None:
                    high_parts(turned, split, n)

            def modulate(n, turned):
                gs, vs = NORMS[n][0:2]
                act.wait_ge(mod_a_ready, n + 1)
                for k in range(TILES):
                    act.wait_ge(xT_ps, 3 * turned + k + 1)
                    for q in range(4, KC):
                        ins = act.activation(h32[:, q, k * P:(k + 1) * P],
                                             ps[:, 2 * k + 1, (q - 4) * P:(q - 3) * P], ACT.Identity,
                                             scale=mod_a[:, n, q, COND[k]:COND[k] + 1],
                                             bias=modv[:, gs, vs, q, COND[k]:COND[k] + 1])
                    ins.then_inc(h32_upper, 1)

            def high_parts(turned, split, norm_no):
                for k in range(TILES):
                    act.wait_ge(h32_ready, 3 * turned + k + 1)
                    if norm_no is not None:
                        act.wait_ge(h32_upper, 3 * norm_no + k + 1)
                    act.activation(h_hi[:, :, k * P:(k + 1) * P], h32[:, :, k * P:(k + 1) * P],
                                   ACT.Copy).then_inc(hhi_ready, 1)

            def spread_gate(q):
                act.wait_ge(x_upd, 6 * q) if q else act.wait_ge(o_sb, 24)
                for j in range(4):
                    act.wait_ge(gbc_ps, 4 * q + j + 1)
                    act.activation(gbc[:, j // 2, (j % 2) * HALF:(j % 2 + 1) * HALF], ps[:, 6, :],
                                   ACT.Copy).then_inc(gbc_sb, 1)

            act.wait_ge(vecsT_sb, 1)
            act.activation(cond_t[:].rearrange("p c k -> p (c k)"), vecsT[:, 0:16], ACT.Tanh,
                           scale=0.5).then_inc(cond_tanh, 1)
            act.wait_ge(lam_sum, 2)
            act.activation(lams[:, 2:4], lams[:, 0:2], ACT.Exp).then_inc(lam_exp, 1)

            norm_act(0, 0, None, None)
            high_parts(0, 0, 0)

            split_hi(QKV0)
            split_hi(QKV0 + 1)
            for s in range(len(QKV_UNITS) + 1):
                if s + 2 < len(QKV_UNITS):
                    split_hi(QKV0 + s + 2)
                if s and QKV_UNITS[s - 1][2] == 1:
                    n = QKV_UNITS[s - 1][1]
                    dst = (qbuf, kbuf, v)[n // 2]
                    for k in range(TILES):
                        if k < 2:
                            act.wait_ge(qkv_acc, 2 * n + k + 1)
                        else:
                            act.wait_ge(unit_used, s)
                        act.activation(dst[:, k, (n % 2) * HALF:(n % 2 + 1) * HALF],
                                       ps[:, (n % 2) * 3 + k, :], ACT.Copy).then_inc(qkv_sb, 1)

            def keys_turned(h):
                act.wait_ge(qkT_ps, h + 1)
                if h >= 2:
                    act.wait_ge(score_ps, 3 * (h - 1))
                act.activation(kT[:, h % 2, :], ps[:, 6, :], ACT.Copy).then_inc(kT_sb, 1)

            def exps(i):
                n = P if i % 3 == 0 else TOK
                act.wait_ge(negmax, i + 1)
                if i >= 2:
                    act.wait_ge(a_ready, i - 1)
                for m in range(2):
                    ins = act.activation(prob[:, i % 2, m, 0:n], ps[:, 2 * (i % 2) + m, 0:n], ACT.Exp,
                                         bias=nmx[:, i % 2, m:m + 1], scale=SCALE,
                                         accum_out=sums[:, i % 2, m:m + 1])
                ins.then_inc(exp_done, 1)

            def map_turned(i):
                n = P if i % 3 == 0 else TOK
                act.wait_ge(aT_ps, i + 1)
                if i >= 2:
                    act.wait_ge(o_ps, i - 1)
                act.activation(aT[:, i % 2, 0:n], ps[:, 4, 0:n], ACT.Copy).then_inc(aT_sb, 1)

            keys_turned(0)
            exps(0)
            for i in range(ITEMS + 1):
                if 1 <= i:
                    map_turned(i - 1)
                if i + 1 < ITEMS:
                    exps(i + 1)
                if i % 3 == 1 and i // 3 + 1 < HEADS:
                    keys_turned(i // 3 + 1)
                if ITEMS - 2 <= i < ITEMS:
                    split_hi(WO0 + i - (ITEMS - 2))
            act.wait_ge(ctx_stored, 32)
            for k in range(TILES):
                act.wait_ge(o_sb, 24)
                act.activation(kbuf[:, k, :], obuf[:, k, :], ACT.Square).then_inc(o_sq, 1)
            spread_gate(0)
            high_parts(1, 1, None)
            for s in range(WO0 + 2, FFN0 + 2):
                split_hi(s)

            norm_act(1, 2, None, 1)
            high_parts(2, 2, 1)
            for s in range(NU + 1):
                if s and FFN_UNITS[s - 1][0] == "gu" and FFN_UNITS[s - 1][2] == 1:
                    c = FFN_UNITS[s - 1][1]
                    act.wait_ge(unit_used, FFN0 + s)
                    if c:
                        act.wait_ge(ffh_ready, 2 * c)
                    for j in range(2):
                        act.activation(tnh[:, j, :], ps[:, 2 * j, 0:TOK], ACT.Tanh, scale=0.5).then_inc(tanh_ready, 1)
                    if c >= 2:
                        act.wait_ge(unit_used, FFN0 + FFN_UNITS.index(("down", c - 2, 0)) + 1)
                    for j in range(2):
                        act.wait_ge(ffh_ready, 2 * c + j + 1)
                        act.activation(ff_hi[:, c % 2, j, :], hb[:, j, :], ACT.Copy).then_inc(ffhi_ready, 1)
                if s + 2 < NU:
                    split_hi(FFN0 + s + 2)
            split_hi(WF0)
            split_hi(WF0 + 1)
            norm_act(2, 3, None, 2)

            for n in range(0, 12, 2):
                k, g = n // 4, n % 4
                act.wait_ge(dft1_ps, n + 1)
                act.wait_ge(xT_ps, 3 * 3 + 3)
                act.activation(f_cos[:, k, g * 256:(g + 1) * 256], ps[:, n % 6, 0:256], ACT.Copy)
                act.activation(f_sin[:, k, g * 256:(g + 1) * 256], ps[:, n % 6, 256:512], ACT.Copy).then_inc(dft1_act, 1)
            for k in range(KC):
                act.wait_ge(dft2_ps, k + 1)
                act.activation(h_hi[:, k, :], ps[:, k % 6, 0:TOK], ACT.Copy).then_inc(ft_hi, 1)
            for s in range(2):
                split_hi(WF0 + s + 2)

            def hi(i, m):
                wait_moe_loaded(act, i, m)
                s = MOE0 + m
                act.wait_ge(unit_used, s - RING + 1 + PER_PAIR * i)
                act.activation(ring_hi[:, s % RING, :], raw[:, (MOE_U0 + m) % RAW, :], ACT.Copy).then_inc(hi_ready, 1)

            norm_act(3, 4, None, None)
            for m in range(AHEAD):
                hi(0, m)
            spread_gate(3)
            act.wait_ge(r_neg, 1)
            for k in range(TILES):
                act.activation(pr[:, k, :], lg[:, k, :], ACT.Exp, bias=lmax[:, k:k + 1],
                               accum_out=psumr[:, k:k + 1]).then_inc(r_exp, 1)
            for n in range(2 * TILES):
                act.wait_ge(tokT_ps, n + 1)
                act.activation(tok_hi[:, n // 2, (n % 2) * HALF:(n % 2 + 1) * HALF], ps[:, n, :],
                               ACT.Copy).then_inc(tok_hi_ready, 1)

            def keep_rows(e, half):
                act.wait_ge(rows_ps, 2 * e + half + 1)
                if half:
                    act.wait_ge(xe_ps, 2 * e + 1)
                act.activation(gathered[:], ps[:, 6, :], ACT.Copy).then_inc(rows_sb, 1)

            def high_xe(e, b, half):
                act.wait_ge(xe_ps, 2 * e + half + 1)
                act.activation(xe[:, b, 0, 4 * half:4 * half + 4, :], ps[:, 7, :].rearrange("p (k n) -> p k n", k=4),
                               ACT.Copy).then_inc(xe_hi_ready, 1)

            def keep_selT(e, b):
                act.wait_ge(selT_ps, e + 1)
                act.activation(selT[:, b, :], ps[:, 6, 0:TOK], ACT.Copy).then_inc(selT_sb, 1)

            for half in range(2):
                keep_rows(0, half)
                high_xe(0, 0, half)
            keep_selT(0, 0)
            act.wait_ge(zeroed, 5)

            with act.Fori(0, PAIRS) as i:
                def high_eh(j, c):
                    act.wait_ge(ehT_ps, nth(i, j, c) + 1)
                    act.wait_ge(unit_used, down_used(i, j, c))
                    act.activation(eh_hi[:, par(j, c), :, :],
                                   ps[:, 2 + par(j, c), 0:256].rearrange("p (s n) -> p s n", s=2),
                                   ACT.Copy).then_inc(eh_hi_ready, 1)

                for m in range(PER_PAIR + 1):
                    if m:
                        j, (kind, c, kh) = (m - 1) // NU, FFN_UNITS[(m - 1) % NU]
                        if kind == "gu" and kh == 1:
                            act.wait_ge(unit_used, MOE0 + m + PER_PAIR * i)
                            act.activation(et[:, par(j, c), :], ps[:, par(j, c), 0:256], ACT.Tanh,
                                           scale=0.5).then_inc(et_ready, 1)
                        if kind == "down" and c == FFC - 1:
                            act.wait_ge(unit_used, MOE0 + m + PER_PAIR * i)
                            act.wait_ge(comb_ps, 12 * i + 6 * j + 6)
                            act.activation(y_hi[:].rearrange("p (a n) -> p a n", a=2), ps[:, 4:6, :],
                                           ACT.Copy).then_inc(ey_hi_ready, 1)
                    if m == PER_PAIR:
                        break
                    j, (kind, c, kh) = m // NU, FFN_UNITS[m % NU]
                    if kind == "gu" and kh == 1 and c >= 1:
                        high_eh(j, c - 1)
                    if kind == "down" and c == FFC - 1:
                        high_eh(j, c)
                    hi(i, m + AHEAD)
                    e, b, at = 2 * i + j + 1, 1 - j, m % NU
                    if at in ROWS_AT:
                        keep_rows(e, ROWS_AT.index(at))
                    if at in TURN_AT:
                        high_xe(e, b, TURN_AT.index(at))
                    if at == SELT_AT:
                        keep_selT(e, b)

            act.wait_ge(meta_ready, 1)
            blocks = act.value_load(meta[0:1, EXTRA:EXTRA + 1], min_val=0, max_val=EXTRA)
            with act.If(blocks > 0):
                with act.Fori(0, EXTRA) as b:
                    act.wait_ge(x_selT_ps, b + 1)
                    act.activation(selT[:, 0, :], ps[:, 2, 0:TOK], ACT.Copy).then_inc(x_selT_sb, 1)
                    act.wait_ge(x_tok_ps, b + 1)
                    act.activation(x_tok[:].rearrange("p (a k) n -> p a (k n)", a=2), ps[:, 0:2, :],
                                   ACT.Copy).then_inc(x_tok_sb, 1)
                    for m, (kind, c, kh) in enumerate(FFN_UNITS):
                        if (kind == "gu" and kh == 1 and c) or (kind == "down" and c == FFC - 1):
                            cc = c - 1 if kind == "gu" else c
                            act.wait_ge(x_hT_ps, FFC * b + cc + 1)
                            act.activation(x_hT[:], ps[:, 0, 0:256].rearrange("p (s n) -> p s n", s=2),
                                           ACT.Copy).then_inc(x_hT_sb, 1)
                        if kind == "gu" and kh == 1:
                            act.wait_ge(x_used, NU * b + m + 1)
                            act.activation(et[:, 0, :], ps[:, 3, 0:256], ACT.Tanh, scale=0.5).then_inc(x_tanh, 1)
                    act.wait_ge(x_used, NU * b + NU)
                    act.activation(x_y[:].rearrange("p (a n) -> p a n", a=2), ps[:, 4:6, :],
                                   ACT.Copy).then_inc(x_y_sb, 1)
            act.end_ifs()

            for k in range(TILES):
                act.wait_ge(x_upd, 6 * 4 - 3 + k + 1)
                act.activation(acc[:, k, :], x[:, k, :], ACT.Square,
                               accum_out=ssq[:, 4, k:k + 1]).then_inc(ssq_ready, 1)
            yp = t["y_prompt"].rearrange("b p n -> (b p) n")
            ysm = t["y_sample"].rearrange("b (t p) n -> t (b p) n", p=P)
            for k in range(TILES):
                act.wait_ge(y_ready, k + 1)
                act.dma_start(yp if k == 0 else ysm[k - 1], acc[:, k, :]).then_inc(y_stored, 16)

        @block.vector
        def _(dve):
            chain = [0]

            def link(ins):
                chain[0] += 1
                ins.then_inc(vch, 1)
                dve.wait_ge(vch, chain[0])

            def split_lo(s):
                u = SPLIT_AT[s]
                dve.wait_ge(hi_ready, s + 1)
                dve.tensor_tensor(ring_lo[:, s % RING, :], raw[:, u % RAW, :],
                                  ring_hi[:, s % RING, :].bitcast(F32), ALU.subtract).then_inc(lo_ready, 1)

            dve.wait_ge(vecsT_ps, 1)
            dve.tensor_copy(vecsT[:], ps[:, 6, 0:49]).then_inc(vecsT_sb, 1)
            dve.wait_ge(cond_tanh, 1)
            link(dve.scalar_tensor_tensor(cond_t[:].rearrange("p c k -> p (c k)"),
                                          cond_t[:].rearrange("p c k -> p (c k)"), 1.0,
                                          vecsT[:, 0:16], ALU.add, ALU.mult))
            for r in range(16):
                ins = dve.tensor_scalar(cond[:, :, 2 * r:2 * r + 2], cond_t[:].rearrange("p c k -> p k c"),
                                        0.5, None, ALU.mult)
            ins.then_inc(cond_ready, 1)
            dve.tensor_scalar(sub_g[:], vecsT[:, 48:49], 1.0 - LAMBDA_INIT, None, ALU.mult)
            dve.wait_ge(lam_loaded, 64)
            for r in range(2):
                dve.tensor_tensor_reduce(junk[:], lamv[:, 2 * r, :], lamv[:, 2 * r + 1, :], 1.0, 0.0,
                                         ALU.mult, ALU.add, lams[:, r:r + 1]).then_inc(lam_sum, 1)
                dve.wait_ge(lam_sum, r + 1)
            dve.wait_ge(lam_exp, 1)
            link(dve.tensor_scalar(lam[:], lams[:, 2:3], lams[:, 3:4], LAMBDA_INIT, ALU.subtract, ALU.add))

            def ada_rows_out(g):
                dve.wait_ge(ada_used, KC * (g + 1))
                dve.wait_ge(bias_loaded[g], 64)
                dve.tensor_tensor(mrow[:, g % 2, :], ps[:, 7, :], mrow[:, g % 2, :], ALU.add).then_inc(mrow_ready, 1)
                if g in GATE_GROUPS:
                    n = GATE_GROUPS.index(g)
                    dve.wait_ge(mrow_ready, g + 1)
                    if n == 0:
                        dve.wait_ge(lane_loaded, 16)
                        ins = dve.tensor_scalar(gates[:], mrow[:, g % 2, :], lane[:, g:g + 1], None, ALU.mult)
                    else:
                        dve.wait_ge(gates_ready, n)
                        ins = dve.scalar_tensor_tensor(gates[:], mrow[:, g % 2, :], lane[:, g:g + 1], gates[:],
                                                       ALU.mult, ALU.add)
                    ins.then_inc(gates_ready, 1)

            def ada_cols_out(g):
                dve.wait_ge(modT_ps, g + 1)
                src = ps[:, 7, :].rearrange("p (q j r) -> p q j r", q=4, j=4)
                for c in range(2):
                    ins = dve.tensor_copy(
                        modv[:, g, :, :, c].rearrange("p v (h q) -> p (v h) q", h=2).rearrange("p j q -> p q j"),
                        src[:, :, :, c])
                ins.then_inc(modv_ready, 1)

            ada_rows_out(0)
            ada_cols_out(0)

            def low_parts(split):
                def low(k):
                    dve.wait_ge(hhi_ready, 3 * split + k + 1)
                    dve.tensor_tensor(h_lo[:, :, k * P:(k + 1) * P], h32[:, :, k * P:(k + 1) * P],
                                      h_hi[:, :, k * P:(k + 1) * P].bitcast(F32), ALU.subtract).then_inc(hlo_ready, 1)
                return low

            def norm_dve(n, turned, split):
                gs, vs, gc, vc, row = NORMS[n]
                dve.wait_ge(modv_ready, max(gs, gc) + 1)
                for c in range(2):
                    ins = dve.scalar_tensor_tensor(mod_a[:, n, :, c], modv[:, gc, vc, :, c], 1.0,
                                                   vecsT[:, row:row + KC], ALU.add, ALU.mult)
                ins.then_inc(mod_a_ready, 1)
                dve.wait_ge(mod_a_ready, n + 1)
                low = low_parts(split) if split is not None else (lambda k: None)
                for k in range(TILES):
                    dve.wait_ge(xT_ps, 3 * turned + k + 1)
                    for q in range(4):
                        ins = dve.tensor_scalar(h32[:, q, k * P:(k + 1) * P],
                                                ps[:, 2 * k, q * P:(q + 1) * P],
                                                mod_a[:, n, q, COND[k]:COND[k] + 1],
                                                modv[:, gs, vs, q, COND[k]:COND[k] + 1], ALU.mult, ALU.add)
                    ins.then_inc(h32_ready, 1)
                    if k:
                        low(k - 1)
                low(TILES - 1)

            norm_dve(0, 0, 0)

            def rope(n):
                buf = (qbuf, kbuf)[n // 2]
                for k in (1, 2):
                    xs = buf[:, k, (n % 2) * HALF:(n % 2 + 1) * HALF]
                    dve.wait_ge(qkv_sb, 3 * n + k + 1)
                    if n == 0 and k == 1:
                        dve.wait_ge(rope_loaded, 32)
                    g8 = lambda a: a.rearrange("p (g d) -> p g d", d=HD)
                    table = lambda a: a[:, k - 1, :].unsqueeze(1).to_broadcast([P, 8, HD])
                    dve.tensor_tensor(g8(rope_a[:]), g8(xs), table(cos), ALU.mult)
                    halves = lambda a: a.rearrange("p g (a f r) -> p g a f r", a=2, f=2)
                    for f in range(2):
                        for a in range(2):
                            ins = dve.tensor_tensor(halves(g8(rope_b[:]))[:, :, a, f, :], halves(g8(xs))[:, :, a, 1 - f, :],
                                                    halves(table(sin))[:, :, a, f, :], ALU.mult)
                    link(ins)
                    dve.tensor_tensor(xs, rope_a[:], rope_b[:], ALU.add).then_inc(rope_done, 1)
                    dve.wait_ge(rope_done, 2 * n + k)

            split_lo(QKV0)
            split_lo(QKV0 + 1)
            for s in range(len(QKV_UNITS) + 2):
                if s + 2 < len(QKV_UNITS):
                    split_lo(QKV0 + s + 2)
                if 2 <= s < 10 and s % 2 == 0:
                    rope(s // 2 - 1)

            def queries_turned(h):
                dve.wait_ge(qkT_ps, h + 1)
                if h >= 2:
                    dve.wait_ge(score_ps, 3 * (h - 1))
                dve.tensor_copy(qT[:, h % 2, :], ps[:, 5, 0:TOK]).then_inc(qT_sb, 1)

            def row_max(i):
                n = P if i % 3 == 0 else TOK
                dve.wait_ge(score_ps, i + 1)
                link(dve.tensor_reduce(mx[:, i % 2, :], ps[:, 2 * (i % 2):2 * (i % 2) + 2, 0:n], AX.X, ALU.max))
                dve.tensor_scalar(nmx[:, i % 2, :], mx[:, i % 2, :], -SCALE, None, ALU.mult).then_inc(negmax, 1)

            def difference(i):
                n = P if i % 3 == 0 else TOK
                dve.wait_ge(exp_done, i + 1)
                link(dve.reciprocal(rs[:, i % 2, :], sums[:, i % 2, :]))
                link(dve.tensor_scalar(l1[:, i % 2:i % 2 + 1], rs[:, i % 2, 1:2], lam[:, 0:1], None, ALU.mult))
                link(dve.tensor_scalar(prob[:, i % 2, 1, 0:n], prob[:, i % 2, 1, 0:n], l1[:, i % 2:i % 2 + 1], None, ALU.mult))
                if i >= 2:
                    dve.wait_ge(aT_ps, i - 1)
                dve.scalar_tensor_tensor(amap[:, i % 2, 0:n], prob[:, i % 2, 0, 0:n], rs[:, i % 2, 0:1],
                                         prob[:, i % 2, 1, 0:n], ALU.mult, ALU.subtract).then_inc(a_ready, 1)

            def out_rows(i):
                h, k = i // 3, i % 3
                dve.wait_ge(o_ps, i + 1)
                dve.tensor_copy(obuf[:, k, h * P:(h + 1) * P], ps[:, 5, TOK:HALF]).then_inc(o_sb, 1)

            queries_turned(0)
            row_max(0)
            for i in range(ITEMS + 3):
                if i < ITEMS:
                    difference(i)
                if i >= 3:
                    out_rows(i - 3)
                if i + 1 < ITEMS:
                    row_max(i + 1)
                group = ada_complete(i)
                if group is not None:
                    ada_rows_out(group)
                if i % 3 == 1 and i // 3 + 1 < HEADS:
                    queries_turned(i // 3 + 1)
                if group is not None:
                    ada_cols_out(group)
                if ITEMS - 2 <= i < ITEMS:
                    split_lo(WO0 + i - (ITEMS - 2))

            for k in range(TILES):
                dve.wait_ge(o_sq, k + 1)
                dve.tensor_reduce(o_ssq[:, k, :], kbuf[:, k, :].rearrange("p (h d) -> p h d", d=P), AX.X,
                                  ALU.add).then_inc(o_sum, 1)
            for k in range(TILES):
                dve.wait_ge(o_rs, k + 1)
                dve.tensor_tensor(obuf[:, k, :].rearrange("p (h d) -> p h d", d=P),
                                  obuf[:, k, :].rearrange("p (h d) -> p h d", d=P),
                                  o_rstd[:, k, :].unsqueeze(2).to_broadcast([P, HEADS, P]),
                                  ALU.mult).then_inc(on_ready, 1)
            low = low_parts(1)
            for k in range(TILES):
                dve.wait_ge(xT_ps, 3 + k + 1)
                dve.wait_ge(o_sum, TILES)
                for q in range(2):
                    ins = dve.tensor_scalar(h32[:, 4 * q:4 * q + 4, k * P:(k + 1) * P],
                                            ps[:, 2 * k + q, :].rearrange("p (q n) -> p q n", q=4),
                                            sub_g[:, 0:1], None, ALU.mult)
                ins.then_inc(h32_ready, 1)
            for k in range(TILES):
                low(k)

            def add_projection(w, n, first):
                for k in range(TILES):
                    if k < 2:
                        dve.wait_ge(proj_acc, 4 * w + 2 * n + k + 1)
                    else:
                        dve.wait_ge(unit_used, first + 2 * n + 2)
                    if n == 0 and k == 0:
                        dve.wait_ge(gbc_sb, 4 * (2 * w + 1))
                    cols = slice(n * HALF, (n + 1) * HALF)
                    link(dve.tensor_tensor(xn[:, k, cols], ps[:, n * 3 + k, :], gbc[:, COND[k], cols], ALU.mult))
                    dve.tensor_tensor(x[:, k, cols], x[:, k, cols], xn[:, k, cols], ALU.add).then_inc(x_upd, 1)

            split_lo(WO0 + 2)
            split_lo(WO0 + 3)
            add_projection(0, 0, WO0)
            split_lo(FFN0)
            split_lo(FFN0 + 1)
            add_projection(0, 1, WO0)

            norm_dve(1, 2, 2)

            def low_hidden(c):
                for j in range(2):
                    dve.wait_ge(ffhi_ready, 2 * c + j + 1)
                    dve.tensor_tensor(ff_lo[:, c % 2, j, :], hb[:, j, :], ff_hi[:, c % 2, j, :].bitcast(F32),
                                      ALU.subtract).then_inc(fflo_ready, 1)

            def add_y(c, n):
                k, half = n // 2, n % 2
                if n < 5:
                    dve.wait_ge(y_ps, 5 * c + n + 1)
                else:
                    dve.wait_ge(unit_used, FFN0 + FFN_UNITS.index(("down", c, 0)) + 1)
                dst = yacc[:, k, half * HALF:(half + 1) * HALF]
                if c == 0:
                    dve.tensor_copy(dst, ps[:, 4 + n % 3, :]).then_inc(y_added, 1)
                else:
                    dve.wait_ge(y_added, 6 * (c - 1) + n + 1)
                    dve.tensor_tensor(dst, ps[:, 4 + n % 3, :], dst, ALU.add).then_inc(y_added, 1)

            for s in range(NU + 1):
                prev = FFN_UNITS[s - 1] if s else None
                if prev is not None and prev[0] == "gu" and prev[2] == 1:
                    c = prev[1]
                    for j in range(2):
                        dve.wait_ge(tanh_ready, 2 * c + j + 1)
                        if c:
                            dve.wait_ge(fflo_ready, 2 * (c - 1) + j + 1)
                        link(dve.scalar_tensor_tensor(hb[:, j, :], tnh[:, j, :], 1.0, ps[:, 2 * j, 0:TOK],
                                                      ALU.add, ALU.mult))
                        dve.scalar_tensor_tensor(hb[:, j, :], hb[:, j, :], 0.5, ps[:, 2 * j + 1, 0:TOK],
                                                 ALU.mult, ALU.mult).then_inc(ffh_ready, 1)
                    for n in range(6 if c else 0):
                        if n == 3:
                            low_hidden(c)
                        add_y(c - 1, n)
                    if c == 0:
                        low_hidden(c)
                if s + 2 < NU:
                    split_lo(FFN0 + s + 2)
            for n in range(6):
                add_y(FFC - 1, n)
            dve.wait_ge(y_added, 6 * FFC)
            dve.wait_ge(gbc_sb, 8)

            def add_gated(buf):
                for n in range(2):
                    for k in range(TILES):
                        cols = slice(n * HALF, (n + 1) * HALF)
                        link(dve.tensor_tensor(buf[:, k, cols], buf[:, k, cols], gbc[:, COND[k], cols], ALU.mult))
                        dve.tensor_tensor(x[:, k, cols], x[:, k, cols], buf[:, k, cols], ALU.add).then_inc(x_upd, 1)

            add_gated(yacc)
            norm_dve(2, 3, None)

            for n in range(1, 12, 2):
                k, g = n // 4, n % 4
                dve.wait_ge(dft1_ps, n + 1)
                dve.tensor_copy(f_cos[:, k, g * 256:(g + 1) * 256], ps[:, n % 6, 0:256])
                dve.tensor_copy(f_sin[:, k, g * 256:(g + 1) * 256], ps[:, n % 6, 256:512]).then_inc(dft1_dve, 1)
            split_lo(WF0)
            split_lo(WF0 + 1)
            for k in range(KC):
                dve.wait_ge(ft_hi, k + 1)
                dve.tensor_tensor(h_lo[:, k, :], ps[:, k % 6, 0:TOK], h_hi[:, k, :].bitcast(F32),
                                  ALU.subtract).then_inc(ft_lo, 1)
            split_lo(WF0 + 2)
            split_lo(WF0 + 3)
            add_projection(1, 0, WF0)
            add_projection(1, 1, WF0)
            norm_dve(3, 4, None)

            dve.wait_ge(logit_ps, 1)
            dve.wait_ge(route_loaded, 48)
            link(dve.tensor_copy(lg[:], ps[:, 6, 0:24].rearrange("p (t e) -> p t e", t=TILES)))
            link(dve.tensor_reduce(lmax[:], lg[:], AX.X, ALU.max))
            dve.tensor_scalar(lmax[:], lmax[:], -1.0, None, ALU.mult).then_inc(r_neg, 1)

            def lo(i, m):
                s = MOE0 + m
                dve.wait_ge(hi_ready, s + 1 + PER_PAIR * i)
                dve.tensor_tensor(ring_lo[:, s % RING, :], raw[:, (MOE_U0 + m) % RAW, :],
                                  ring_hi[:, s % RING, :].bitcast(F32), ALU.subtract).then_inc(lo_ready, 1)

            lo(0, 0)
            dve.wait_ge(r_exp, TILES)
            link(dve.reciprocal(prec[:], psumr[:]))
            for k in range(TILES):
                link(dve.tensor_scalar(pr[:, k, :], pr[:, k, :], prec[:, k:k + 1], None, ALU.mult))
                link(dve.max(top[:, k, :], pr[:, k, :]))
                link(dve.max_index(topi[:, k, :], top[:, k, :], pr[:, k, :]))
            link(dve.tensor_copy(topf[:], topi[:]))
            link(dve.tensor_tensor(tsum[:], top[:, :, 0], top[:, :, 1], ALU.add))
            link(dve.reciprocal(trec[:], tsum[:]))
            for k in range(TILES):
                dve.tensor_scalar(tg[:, k, :], top[:, k, 0:2], trec[:, k:k + 1], None, ALU.mult)
                dve.tensor_scalar(oh1[:, k, :], iota[:, 0:N_EXP], topf[:, k, 0:1], None, ALU.is_equal)
                link(dve.tensor_scalar(oh2[:, k, :], iota[:, 0:N_EXP], topf[:, k, 1:2], None, ALU.is_equal))
            dve.tensor_tensor(mask[:], oh1[:], oh2[:], ALU.add).then_inc(mask_ready, 1)
            for k in range(TILES):
                link(dve.tensor_scalar(gate[:, k, :], oh1[:, k, :], tg[:, k, 0:1], None, ALU.mult))
                link(dve.scalar_tensor_tensor(gate[:, k, :], oh2[:, k, :], tg[:, k, 1:2], gate[:, k, :],
                                              ALU.mult, ALU.add))
            lo(0, 1)
            dve.wait_ge(mask_ready, 1)
            dve.wait_ge(pos_ps, 1)
            link(dve.scalar_tensor_tensor(posm[:, :, 0:N_EXP], ps[:, 6, 0:24].rearrange("p (t e) -> p t e", t=TILES), 1.0,
                                          mask[:], ALU.add, ALU.mult))
            dve.tensor_scalar(posm[:, :, 0:N_EXP], posm[:, :, 0:N_EXP], -1.0, None, ALU.add)
            link(dve.memset(posm[:, :, N_EXP:], -1.0))
            dve.tensor_copy(cnt[:], ps[:, 6, 24:32]).then_inc(cnt_ready, 1)

            def select(e, b):
                dve.tensor_copy(pos_col[:], posm[:, :, bass.ds(e, 1)].rearrange("p t e -> p (t e)")).then_inc(cols_ready, 1)
                dve.wait_ge(cols_ready, e + 1)
                for k in range(TILES):
                    ins = dve.tensor_scalar(sel[:, b, k, :], iota[:], pos_col[:, k:k + 1], None, ALU.is_equal)
                ins.then_inc(sel_ready, 1)

            def low_xe(e, b, half):
                dve.wait_ge(xe_hi_ready, 2 * e + half + 1)
                ks = slice(4 * half, 4 * half + 4)
                dve.tensor_tensor(xe[:, b, 1, ks, :], ps[:, 7, :].rearrange("p (k n) -> p k n", k=4),
                                  xe[:, b, 0, ks, :].bitcast(F32), ALU.subtract).then_inc(xe_lo_ready, 1)

            dve.wait_ge(tokT_ps, 2 * TILES)
            select(0, 0)
            for n in range(2 * TILES):
                dve.wait_ge(tok_hi_ready, n + 1)
                cols = slice((n % 2) * HALF, (n % 2 + 1) * HALF)
                dve.tensor_tensor(tok_lo[:, n // 2, cols], ps[:, n, :], tok_hi[:, n // 2, cols].bitcast(F32),
                                  ALU.subtract).then_inc(tok_lo_ready, 1)
            for half in range(2):
                low_xe(0, 0, half)
            dve.wait_ge(zeroed, 5)

            def combine(e, k):
                for half in range(2):
                    n = 2 * k + half
                    cols = slice(half * HALF, (half + 1) * HALF)
                    dve.wait_ge(comb_ps, 6 * e + n + 1)
                    dve.scalar_tensor_tensor(acc[:, k, cols], ps[:, 6 + half, :], gate_col[:, k:k + 1],
                                             acc[:, k, cols], ALU.mult, ALU.add).then_inc(comb_sb, 1)

            with dve.Fori(0, PAIRS) as i:
                def low_eh(j, c):
                    dve.wait_ge(eh_hi_ready, nth(i, j, c) + 1)
                    b = par(j, c)
                    dve.tensor_tensor(eh_lo[:, b, :, :], ps[:, 2 + b, 0:256].rearrange("p (s n) -> p s n", s=2),
                                      eh_hi[:, b, :, :].bitcast(F32), ALU.subtract).then_inc(eh_lo_ready, 1)

                for m in range(PER_PAIR + 1):
                    if m:
                        j, (kind, c, kh) = (m - 1) // NU, FFN_UNITS[(m - 1) % NU]
                        n, b = nth(i, j, c), par(j, c)
                        if kind == "gu" and kh == 1:
                            dve.wait_ge(et_ready, n + 1)
                            dve.scalar_tensor_tensor(eh[:, b, :], et[:, b, :], 1.0, ps[:, b, 0:256],
                                                     ALU.add, ALU.mult).then_inc(ea_ready, 1)
                            dve.wait_ge(ea_ready, n + 1)
                            dve.scalar_tensor_tensor(eh[:, b, :], eh[:, b, :], 0.5, ps[:, b, 256:512],
                                                     ALU.mult, ALU.mult).then_inc(eh_ready, 1)
                        if kind == "down" and c == FFC - 1:
                            dve.wait_ge(ey_hi_ready, 2 * i + j + 1)
                            dve.tensor_tensor(y_lo[:].rearrange("p (a n) -> p a n", a=2), ps[:, 4:6, :],
                                              y_hi[:].rearrange("p (a n) -> p a n", a=2).bitcast(F32),
                                              ALU.subtract).then_inc(ey_lo_ready, 1)
                    if m == PER_PAIR:
                        break
                    j, (kind, c, kh) = m // NU, FFN_UNITS[m % NU]
                    if kind == "gu" and kh == 1 and c >= 1:
                        low_eh(j, c - 1)
                    if kind == "down" and c == FFC - 1:
                        low_eh(j, c)
                    lo(i, m + AHEAD)
                    e, b, at = 2 * i + j + 1, 1 - j, m % NU
                    if at in COMBINE_AT:
                        combine(e - 1, COMBINE_AT.index(at))
                    if at == NEXT_SEL_AT:
                        dve.wait_ge(comb_sb, 6 * e)
                        dve.wait_ge(selT_ps, e)
                        dve.tensor_copy(gate_col[:], gate[:, :, bass.ds(e - 1, 1)].rearrange("p t e -> p (t e)"))
                        select(e, b)
                    if at in TURN_AT:
                        low_xe(e, b, TURN_AT.index(at))

            for k in range(TILES):
                combine(N_EXP, k)
            dve.wait_ge(comb_sb, 6 * N_EXP + 6)
            dve.wait_ge(meta_ready, 1)
            blocks = dve.value_load(meta[0:1, EXTRA:EXTRA + 1], min_val=0, max_val=EXTRA)
            with dve.If(blocks > 0):
                with dve.Fori(0, EXTRA) as b:
                    dve.tensor_copy(pos_col[:], x_place[:, bass.ds(b, 1), :].rearrange("p b t -> p (b t)"))
                    dve.tensor_copy(gate_col[:],
                                    x_gate[:, bass.ds(b, 1), :].rearrange("p b t -> p (b t)")).then_inc(cols_ready, 1)
                    dve.wait_ge(cols_ready, N_EXP + 1 + b + 1)
                    for k in range(TILES):
                        ins = dve.tensor_scalar(sel[:, 0, k, :], iota[:], pos_col[:, k:k + 1], None, ALU.is_equal)
                    ins.then_inc(x_sel, 1)
                    for c in range(FFC):
                        dve.wait_ge(x_tanh, FFC * b + c + 1)
                        if c:
                            dve.wait_ge(x_hT_ps, FFC * b + c)
                        dve.scalar_tensor_tensor(eh[:, 0, :], et[:, 0, :], 1.0, ps[:, 3, 0:256],
                                                 ALU.add, ALU.mult).then_inc(x_h_half, 1)
                        dve.wait_ge(x_h_half, FFC * b + c + 1)
                        dve.scalar_tensor_tensor(eh[:, 0, :], eh[:, 0, :], 0.5, ps[:, 3, 256:512],
                                                 ALU.mult, ALU.mult).then_inc(x_h, 1)
                    for n in range(6):
                        k, half = n // 2, n % 2
                        cols = slice(half * HALF, (half + 1) * HALF)
                        dve.wait_ge(x_comb_ps, 6 * b + n + 1)
                        dve.scalar_tensor_tensor(acc[:, k, cols], ps[:, 6 + n % 2, :], gate_col[:, k:k + 1],
                                                 acc[:, k, cols], ALU.mult, ALU.add).then_inc(x_comb_sb, 1)
                    dve.wait_ge(x_comb_sb, 6 * b + 6)
            dve.end_ifs()
            dve.wait_ge(gbc_sb, 16)
            dve.wait_ge(final_g_loaded, 16)
            add_gated(acc)
            for k in range(TILES):
                dve.wait_ge(rstd_ready, 12 + k + 1)
                dve.scalar_tensor_tensor(acc[:, k, :], x[:, k, :], rstd[:, 4, k:k + 1], final_g,
                                         ALU.mult, ALU.mult).then_inc(y_ready, 1)

        @block.tensor
        def _(pe):
            def mm3(out, l_hi, l_lo, r_hi, r_lo, first, last):
                pe.matmul(out, l_hi, r_hi, start=first, stop=False)
                pe.matmul(out, l_lo, r_hi, start=False, stop=False)
                return pe.matmul(out, l_hi, r_lo, start=False, stop=last)

            def ada_unit(g, k):
                n = KC * g + k
                u = ADA_AT[n]
                wait_loaded(pe, u)
                if k == 0 and g:
                    pe.wait_ge(modv_ready, g)
                for j in range(4):
                    ins = pe.matmul(ps[32 * j:32 * j + 32, 7, :], cond[:, k, :],
                                    raw[:, u % RAW, j * HALF:(j + 1) * HALF], start=(k == 0), stop=(k == KC - 1))
                ins.then_inc(ada_used, 1)

            def ada_turn(g):
                pe.wait_ge(mrow_ready, g + 1)
                for q in range(4):
                    ins = pe.transpose(ps[:, 7, q * P:(q + 1) * P], mrow[:, g % 2, q * P:(q + 1) * P], ident[:])
                ins.then_inc(modT_ps, 1)

            pe.wait_ge(ident_loaded, 16)
            pe.wait_ge(vecs_loaded, 7 * 16)
            pe.transpose(ps[:, 6, 0:49], vecs[:], ident[0:49, 0:49]).then_inc(vecsT_ps, 1)
            pe.wait_ge(cond_ready, 1)
            for k in range(KC):
                ada_unit(0, k)
            ada_turn(0)

            def turn_rows(ordinal, ready, base):
                for k in range(TILES):
                    pe.wait_ge(ready, base + k + 1)
                    for q in range(KC):
                        ins = pe.transpose(ps[:, 2 * k + q // 4, (q % 4) * P:(q % 4 + 1) * P],
                                           xn[:, k, q * P:(q + 1) * P], ident[:])
                    ins.then_inc(xT_ps, 1)

            def spread_gate(q):
                layer, second = q // 2, q % 2
                g = 3 * layer + 1 + second
                pe.wait_ge(gates_ready, GATE_GROUPS.index(g) + 1)
                for n in range(4):
                    if n or q:
                        pe.wait_ge(gbc_sb, 4 * q + n)
                    c, half = n // 2, n % 2
                    row = 32 * (2 * second + half) + 2 * g + c
                    pe.matmul(ps[:, 6, :], ident[:, row:row + 1].to_broadcast([P, P]), gates[:],
                              start=True, stop=True).then_inc(gbc_ps, 1)

            turn_rows(0, xn_ready, 0)

            def project(first, n, kh, s, banks, acc_sem, acc_base, hsem, hbase):
                pe.wait_ge(lo_ready, first + s + 1)
                slot = (first + s) % RING
                for k in range(TILES):
                    if hsem is not None:
                        pe.wait_ge(hsem, hbase + k + 1)
                    for q in range(4):
                        kc = kh * 4 + q
                        cols = slice(k * P, (k + 1) * P)
                        ins = mm3(ps[:, banks + k, :], h_hi[:, kc, cols], h_lo[:, kc, cols],
                                  ring_hi[:, slot, q * HALF:(q + 1) * HALF], ring_lo[:, slot, q * HALF:(q + 1) * HALF],
                                  kh == 0 and q == 0, kh == 1 and q == 3)
                    if kh == 1 and k < 2:
                        ins.then_inc(acc_sem, 1)
                ins.then_inc(unit_used, 1)

            for s, (_, n, kh) in enumerate(QKV_UNITS):
                if kh == 0 and n >= 2:
                    pe.wait_ge(qkv_sb, 3 * (n - 1))
                project(QKV0, n, kh, s, (n % 2) * 3, qkv_acc, 2 * n, hlo_ready if s == 0 else None, 0)

            def turn_heads(h):
                if h:
                    pe.wait_ge(qT_sb, h)
                    pe.wait_ge(kT_sb, h)
                else:
                    pe.wait_ge(qkv_sb, 18)
                    pe.wait_ge(rope_done, 8)
                    pe.wait_ge(cache_loaded, 32)
                if h > 1:
                    pe.wait_ge(o_sb, 3 * h - 4)
                cols = slice(h * P, (h + 1) * P)
                for k in range(TILES):
                    pe.transpose(ps[:, 5, k * P:(k + 1) * P], qbuf[:, k, cols], ident[:])
                    pe.transpose(ps[:, 6, k * P:(k + 1) * P], kbuf[:, k, cols], ident[:])
                pe.transpose(ps[:, 6, TOK:HALF], gbc[:, 0, cols], ident[:]).then_inc(qkT_ps, 1)

            def scores(i):
                h, k = i // 3, i % 3
                pe.wait_ge(qT_sb, h + 1)
                pe.wait_ge(kT_sb, h + 1)
                if i >= 2:
                    pe.wait_ge(exp_done, i - 1)
                keys = slice(0, P) if k == 0 else slice(P, HALF)
                for m in range(2):
                    rows = slice(HD * m, HD * m + HD)
                    ins = pe.matmul(ps[:, 2 * (i % 2) + m, 0:(P if k == 0 else TOK)],
                                    qT[rows, h % 2, k * P:(k + 1) * P], kT[rows, h % 2, keys], start=True, stop=True)
                ins.then_inc(score_ps, 1)

            def turn_map(i):
                pe.wait_ge(a_ready, i + 1)
                if i:
                    pe.wait_ge(aT_sb, i)
                for b in range(1 if i % 3 == 0 else 3):
                    ins = pe.transpose(ps[:, 4, b * P:(b + 1) * P], amap[:, i % 2, b * P:(b + 1) * P], ident[:])
                ins.then_inc(aT_ps, 1)

            def values(i):
                h, k = i // 3, i % 3
                cols = slice(h * P, (h + 1) * P)
                pe.wait_ge(aT_sb, i + 1)
                if i:
                    pe.wait_ge(o_sb, i)
                pe.wait_ge(qT_sb, min((i + 4) // 3, HEADS - 1) + 1)
                vs = [v[:, 0, cols]] if k == 0 else [v[:, 1, cols], v[:, 2, cols], gbc[:, 1, cols]]
                for b, vb in enumerate(vs):
                    ins = pe.matmul(ps[:, 5, TOK:HALF], aT[:, i % 2, b * P:(b + 1) * P], vb,
                                    start=(b == 0), stop=(b == len(vs) - 1))
                ins.then_inc(o_ps, 1)

            turn_heads(0)
            scores(0)
            for i in range(ITEMS + 2):
                if i + 1 < ITEMS:
                    scores(i + 1)
                if 1 <= i <= ITEMS:
                    turn_map(i - 1)
                if ada_complete(i) is not None:
                    ada_turn(ada_complete(i))
                if i % 3 == 1 and i // 3 + 1 < HEADS:
                    turn_heads(i // 3 + 1)
                for g, k in ada_at(i):
                    ada_unit(g, k)
                if i >= 2:
                    values(i - 2)
            pe.wait_ge(o_sb, 24)
            turn_rows(1, on_ready, 0)
            spread_gate(0)

            def projection(first, w, hsem, hbase):
                for s in range(4):
                    n, kh = s // 2, s % 2
                    project(first, n, kh, s, 3 * n, proj_acc, 4 * w + 2 * n, hsem if s == 0 else None, hbase)

            pe.wait_ge(h32_ready, 6)
            projection(WO0, 0, hlo_ready, 3)
            turn_rows(2, xn_ready, 3)
            spread_gate(1)

            pe.wait_ge(hlo_ready, 9)
            for s, (kind, c, kh) in enumerate(FFN_UNITS):
                pe.wait_ge(lo_ready, FFN0 + s + 1)
                slot = (FFN0 + s) % RING
                if kind == "gu":
                    if kh == 0 and c:
                        pe.wait_ge(ffh_ready, 2 * c)
                    for q in range(4):
                        for b in range(4):
                            w = q * HALF + (b % 2) * 256 + (b // 2) * P
                            cols = slice(w, w + P)
                            kc = kh * 4 + q
                            ins = mm3(ps[:, b, 0:TOK], ring_hi[:, slot, cols], ring_lo[:, slot, cols],
                                      h_hi[:, kc, :], h_lo[:, kc, :], kh == 0 and q == 0, kh == 1 and q == 3)
                else:
                    pe.wait_ge(fflo_ready, 2 * c + 2)
                    if c == 0:
                        pe.wait_ge(gbc_sb, 8)
                    for n in range(6):
                        k, half = n // 2, n % 2
                        if 6 * c + n >= 3:
                            pe.wait_ge(y_added, 6 * c + n - 2)
                        for j in range(2):
                            cols = slice(k * P, (k + 1) * P)
                            w = slice(j * D + half * HALF, j * D + (half + 1) * HALF)
                            ins = mm3(ps[:, 4 + n % 3, :], ff_hi[:, c % 2, j, cols], ff_lo[:, c % 2, j, cols],
                                      ring_hi[:, slot, w], ring_lo[:, slot, w], j == 0, j == 1)
                        if n < 5:
                            ins.then_inc(y_ps, 1)
                ins.then_inc(unit_used, 1)

            turn_rows(3, xn_ready, 6)
            spread_gate(2)
            pe.wait_ge(h32_ready, 12)
            pe.wait_ge(h32_upper, 9)
            pe.wait_ge(dft_loaded, 48)
            for n in range(12):
                k, g = n // 4, n % 4
                if n >= 6:
                    pe.wait_ge(dft1_act if n % 2 == 0 else dft1_dve, (n - 6) // 2 + 1)
                for q in range(2):
                    ins = pe.matmul(ps[:, n % 6, :], h32[:, 2 * g + q, k * P:(k + 1) * P], dft_ch[:, q, :],
                                    start=(q == 0), stop=(q == 1))
                ins.then_inc(dft1_ps, 1)
            pe.wait_ge(dft1_act, 6)
            pe.wait_ge(dft1_dve, 6)
            for q in range(KC):
                cols = slice(q * P, (q + 1) * P)
                if q >= 6:
                    pe.wait_ge(ft_lo, q - 5)
                pe.matmul(ps[:, q % 6, 0:P], f_cos[:, 0, cols], dft_p[:, 0, :], start=True, stop=False)
                pe.matmul(ps[:, q % 6, 0:P], f_sin[:, 0, cols], dft_p[:, 1, :], start=False, stop=True)
                for k in range(2):
                    pe.matmul(ps[:, q % 6, P:TOK], f_cos[:, 1 + k, cols], dft_s[:, k, 0, :], start=(k == 0), stop=False)
                    ins = pe.matmul(ps[:, q % 6, P:TOK], f_sin[:, 1 + k, cols], dft_s[:, k, 1, :],
                                    start=False, stop=(k == 1))
                ins.then_inc(dft2_ps, 1)
            pe.wait_ge(ft_lo, KC)
            projection(WF0, 1, None, 0)
            turn_rows(4, xn_ready, 9)
            spread_gate(3)

            pe.wait_ge(h32_ready, 15)
            pe.wait_ge(h32_upper, 12)
            pe.wait_ge(gbc_sb, 16)
            pe.wait_ge(route_loaded, 48)
            for k in range(TILES):
                for q in range(KC):
                    ins = pe.matmul(ps[:, 6, k * N_EXP:(k + 1) * N_EXP], h32[:, q, k * P:(k + 1) * P], wr[:, q, :],
                                    start=(q == 0), stop=(q == KC - 1))
            ins.then_inc(logit_ps, 1)
            for n in range(2 * TILES):
                for q in range(4):
                    ins = pe.transpose(ps[:, n, q * P:(q + 1) * P],
                                       h32[:, 4 * (n % 2) + q, (n // 2) * P:(n // 2 + 1) * P], ident[:])
                ins.then_inc(tokT_ps, 1)
            pe.wait_ge(mask_ready, 1)
            pe.wait_ge(const_ready, 2)
            for k in range(TILES):
                out = ps[:, 6, k * N_EXP:(k + 1) * N_EXP]
                for b in range(k):
                    pe.matmul(out, ones[:].to_broadcast([P, P]), mask[:, b, :], start=(b == 0), stop=False)
                pe.matmul(out, tri[:], mask[:, k, :], start=(k == 0), stop=True)
            for k in range(TILES):
                ins = pe.matmul(ps[:, 6, 24:32], ones[:].to_broadcast([P, P]), mask[:, k, :],
                                start=(k == 0), stop=(k == TILES - 1))
            ins.then_inc(pos_ps, 1)
            pe.wait_ge(tok_lo_ready, 6)

            def gather_rows(e, b, half):
                if half:
                    pe.wait_ge(rows_sb, 2 * e + 1)
                else:
                    pe.wait_ge(sel_ready, e + 1)
                for r, part in enumerate((tok_hi, tok_lo)):
                    for k in range(TILES):
                        ins = pe.matmul(ps[:, 6, :], sel[:, b, k, :], part[:, k, half * HALF:(half + 1) * HALF],
                                        start=(r == 0 and k == 0), stop=(r == 1 and k == TILES - 1))
                ins.then_inc(rows_ps, 1)

            def turn_gathered(e, half):
                pe.wait_ge(rows_sb, 2 * e + half + 1)
                if half:
                    pe.wait_ge(xe_lo_ready, 2 * e + 1)
                for q in range(4):
                    ins = pe.transpose(ps[:, 7, q * P:(q + 1) * P], gathered[:, q * P:(q + 1) * P], ident[:])
                ins.then_inc(xe_ps, 1)

            def turn_selection(e, b):
                for k in range(TILES):
                    ins = pe.transpose(ps[:, 6, k * P:(k + 1) * P], sel[:, b, k, :].bitcast(F32), ident[:])
                ins.then_inc(selT_ps, 1)

            def bring_back(e, b, k):
                for half in range(2):
                    if k:
                        pe.wait_ge(comb_sb, 6 * e + 2 * k + half - 1)
                    for r, part in enumerate((y_hi, y_lo)):
                        ins = pe.matmul(ps[:, 6 + half, :], selT[:, b, k * P:(k + 1) * P],
                                        part[:, half * HALF:(half + 1) * HALF], start=(r == 0), stop=(r == 1))
                    ins.then_inc(comb_ps, 1)

            for half in range(2):
                gather_rows(0, 0, half)
                turn_gathered(0, half)
            turn_selection(0, 0)
            pe.wait_ge(xe_lo_ready, 2)
            pe.wait_ge(selT_sb, 1)
            pe.wait_ge(zeroed, 5)

            with pe.Fori(0, PAIRS) as i:
                def turn_hidden(j, c):
                    b = par(j, c)
                    pe.wait_ge(eh_ready, nth(i, j, c) + 1)
                    for s in range(2):
                        ins = pe.transpose(ps[:, 2 + b, s * P:(s + 1) * P], eh[:, b, s * P:(s + 1) * P], ident[:])
                    ins.then_inc(ehT_ps, 1)

                for m in range(PER_PAIR):
                    j, at = m // NU, m % NU
                    kind, c, kh = FFN_UNITS[at]
                    n, b, e = nth(i, j, c), par(j, c), 2 * i + j
                    if kind == "gu" and kh == 1 and c >= 1:
                        turn_hidden(j, c - 1)
                    if kind == "down" and c == FFC - 1:
                        turn_hidden(j, c)
                    if at in COMBINE_AT:
                        if at == COMBINE_AT[0]:
                            pe.wait_ge(selT_sb, e + 1)
                            if j:
                                pe.wait_ge(ey_lo_ready, 2 * i + 1)
                            else:
                                pe.wait_ge(lo_ready, MOE0 + m + 1 + PER_PAIR * i)
                        bring_back(e, 1 - j, COMBINE_AT.index(at))
                    if at in ROWS_AT:
                        gather_rows(e + 1, 1 - j, ROWS_AT.index(at))
                    if at in TURN_AT:
                        turn_gathered(e + 1, TURN_AT.index(at))
                    if at == SELT_AT:
                        turn_selection(e + 1, 1 - j)
                    pe.wait_ge(lo_ready, MOE0 + m + 1 + PER_PAIR * i)
                    slot = (MOE0 + m) % RING
                    if kind == "gu":
                        if c == 0 and kh == 0:
                            pe.wait_ge(xe_lo_ready, 2 * e + 2)
                        for q in range(4):
                            kc = kh * 4 + q
                            ins = mm3(ps[:, b, :], xe[:, j, 0, kc, :], xe[:, j, 1, kc, :],
                                      ring_hi[:, slot, q * HALF:(q + 1) * HALF], ring_lo[:, slot, q * HALF:(q + 1) * HALF],
                                      kh == 0 and q == 0, kh == 1 and q == 3)
                    else:
                        pe.wait_ge(eh_lo_ready, n + 1)
                        for s in range(2):
                            for half in range(2):
                                w = slice(s * D + half * HALF, s * D + (half + 1) * HALF)
                                ins = mm3(ps[:, 4 + half, :], eh_hi[:, b, s, :], eh_lo[:, b, s, :],
                                          ring_hi[:, slot, w], ring_lo[:, slot, w],
                                          c == 0 and s == 0, c == FFC - 1 and s == 1)
                    ins.then_inc(unit_used, 1)

            pe.wait_ge(ey_lo_ready, N_EXP)
            for k in range(TILES):
                bring_back(N_EXP, 1, k)
            pe.wait_ge(meta_ready, 1)
            blocks = pe.value_load(meta[0:1, EXTRA:EXTRA + 1], min_val=0, max_val=EXTRA)
            pe.wait_ge(comb_sb, 6 * N_EXP + 6)
            with pe.If(blocks > 0):
                with pe.Fori(0, EXTRA) as b:
                    pe.wait_ge(x_sel, b + 1)
                    for k in range(TILES):
                        ins = pe.transpose(ps[:, 2, k * P:(k + 1) * P], sel[:, 0, k, :].bitcast(F32), ident[:])
                    ins.then_inc(x_selT_ps, 1)
                    for q in range(KC):
                        for r, part in enumerate((tok_hi, tok_lo)):
                            for k in range(TILES):
                                ins = pe.matmul(ps[:, q // 4, (q % 4) * P:(q % 4 + 1) * P],
                                                part[:, k, q * P:(q + 1) * P], sel[:, 0, k, :],
                                                start=(r == 0 and k == 0), stop=(r == 1 and k == TILES - 1))
                    ins.then_inc(x_tok_ps, 1)
                    pe.wait_ge(x_tok_sb, b + 1)
                    pe.wait_ge(x_selT_sb, b + 1)

                    def turn_extra(c):
                        pe.wait_ge(x_h, FFC * b + c + 1)
                        for s in range(2):
                            ins = pe.transpose(ps[:, 0, s * P:(s + 1) * P], eh[:, 0, s * P:(s + 1) * P], ident[:])
                        ins.then_inc(x_hT_ps, 1)

                    for m, (kind, c, kh) in enumerate(FFN_UNITS):
                        if kind == "gu" and kh == 0 and c:
                            turn_extra(c - 1)
                        if kind == "down" and c == FFC - 1:
                            turn_extra(c)
                        slot = m % RING
                        pe.wait_ge(x_loaded_w[slot], x_unit_loaded[m] + x_slot_total[slot] * b)
                        if kind == "gu":
                            for q in range(4):
                                ins = pe.matmul(ps[:, 3, :], x_tok[:, kh * 4 + q, :],
                                                raw[:, slot, q * HALF:(q + 1) * HALF],
                                                start=(kh == 0 and q == 0), stop=(kh == 1 and q == 3))
                        else:
                            pe.wait_ge(x_hT_sb, FFC * b + c + 1)
                            for s in range(2):
                                for half in range(2):
                                    w = slice(s * D + half * HALF, s * D + (half + 1) * HALF)
                                    ins = pe.matmul(ps[:, 4 + half, :], x_hT[:, s, :], raw[:, slot, w],
                                                    start=(c == 0 and s == 0), stop=(c == FFC - 1 and s == 1))
                        ins.then_inc(x_used, 1)
                    pe.wait_ge(x_y_sb, b + 1)
                    for n in range(6):
                        k, half = n // 2, n % 2
                        if n >= 2:
                            pe.wait_ge(x_comb_sb, 6 * b + n - 1)
                        pe.matmul(ps[:, 6 + n % 2, :], selT[:, 0, k * P:(k + 1) * P].bitcast(F32),
                                  x_y[:, half * HALF:(half + 1) * HALF], start=True, stop=True).then_inc(x_comb_ps, 1)
            pe.end_ifs()


_INS = ["x_prompt", "x_sample", "c", "cache_k_0", "cache_v_0", "c_ctx",
        "ada_w_0", "ada_b_0", "norm1_g_0", "norm2_g_0", "w_qkv_0",
        "lambda_q1_0", "lambda_k1_0", "lambda_q2_0", "lambda_k2_0", "subln_g_0", "w_o_0",
        "w_gu_0", "w_down_0", "ada_w_1", "ada_b_1", "norm1_g_1", "norm2_g_1", "w_fourier_1",
        "w_router_1", "w_gu_e_1", "w_down_e_1", "final_norm_g"]
_OUTS = [("y_prompt", (1, 128, 1024)), ("y_sample", (1, 256, 1024)),
         ("k_ctx", (1, 128, 8, 128)), ("v_ctx", (1, 128, 8, 128))]


def shape_constants():
    f = np.float32
    rows = 256 // 64
    row = np.repeat(np.arange(rows), 64).astype(f)
    col = np.tile(np.arange(64), rows).astype(f)
    inv = (f(1.0) / (f(10000.0) ** (np.arange(0, 32, 2, dtype=f) / f(32)))).astype(f)
    ar, ac = row[:, None] * inv[None, :], col[:, None] * inv[None, :]
    ang = np.concatenate([ar, ar, ac, ac], axis=-1).astype(np.float64)
    sign = np.tile(np.repeat([-1.0, 1.0], 16), 2)

    def wave(n):
        a = 2 * np.pi * (np.outer(np.arange(n), np.arange(n)) % n) / n
        return np.cos(a), np.sin(a)

    c256, s256 = wave(256)
    c128, s128 = wave(128)
    return {
        "ident": np.eye(128, dtype=f),
        "lane": (np.arange(128)[:, None] % 32 // 2 == np.arange(6)[None, :]).astype(f),
        "iota": np.tile(np.arange(128, dtype=f), (128, 1)),
        "tri": np.triu(np.ones((128, 128), f), 1),
        "rope_cos": np.cos(ang).astype(f),
        "rope_sin": (np.sin(ang) * sign).astype(f),
        "dft_ch": (np.concatenate([c256, s256], axis=1) / 16).astype(f),
        "dft_p": (np.concatenate([c128, -s128], axis=1) / np.sqrt(128)).astype(f),
        "dft_s": (np.concatenate([c256, -s256], axis=1) / 16).astype(f),
    }


def kernel(**inputs):
    import concourse.bacc as bacc
    from concourse.bass_utils import run_bass_kernel_spmd

    nc = bacc.Bacc("TRN2", target_bir_lowering=False, num_devices=1)
    arrays, args = {}, {}
    for name, a in list((n, inputs[n]) for n in _INS) + list(shape_constants().items()):
        a = np.ascontiguousarray(a)
        arrays[f"in_{name}"] = a
        args[name] = nc.dram_tensor(f"in_{name}", a.shape, mybir.dt.from_np(a.dtype), kind="ExternalInput").ap()
    for name, shape in _OUTS:
        out = nc.dram_tensor(f"out_{name}", shape, F32, kind="ExternalOutput").ap()
        args[name] = out.rearrange("b p h d -> (b p) (h d)") if len(shape) == 4 else out
    build(nc, args)
    r = run_bass_kernel_spmd(nc, [arrays], core_ids=[0])
    return tuple(np.asarray(r.results[0][f"out_{name}"]) for name, _ in _OUTS)
```

```python
from contextlib import ExitStack

import numpy as np

import concourse.bass as bass
from concourse import mybir

F32 = mybir.dt.float32
F32R = mybir.dt.float32r
I32 = mybir.dt.int32
U32 = mybir.dt.uint32
ALU = mybir.AluOpType
ACT = mybir.ActivationFunctionType
AX = mybir.AxisListType

P = 128
D = 1024
KC = D // P
TILES = 3
TOK = TILES * P
GATE_GROUPS = (1, 2, 4, 5)
COND = (0, 1, 1)
HEADS = 8
HD = 64
D_FF = 2816
N_EXP = 8
FFC = D_FF // 256
EPS = 1e-6
SUBLN_EPS = 1e-5
LAMBDA_INIT = 0.2
SCALE = HD ** -0.5
HALF = 512

UNIT = 2048
RAW = 6
RING = 3


def ffn_units():
    out = []
    for c in range(FFC):
        out += [("gu", c, 0), ("gu", c, 1)]
        if c:
            out.append(("down", c - 1, 0))
    return out + [("down", FFC - 1, 0)]


FFN_UNITS = ffn_units()
NU = len(FFN_UNITS)


QKV_UNITS = [("qkv", n, kh) for n in range(6) for kh in range(2)]
ADA_FROM = len(QKV_UNITS) - KC
ITEMS = HEADS * TILES

SPLIT_WO_AT = (17, 19, 21)


def ada_at(item):
    if not 0 <= item < ITEMS:
        return []
    first = item * 4 // 3 + (item % 3 > 0)
    return [(2 + m // KC, m % KC) for m in range(first, first + (2 if item % 3 == 0 else 1))]


def ada_complete(item):
    before = ada_at(item - 1)
    return before[-1][0] if before and before[-1][1] == KC - 1 else None


def stream_before_experts():
    s = [("ada", 0, k) for k in range(KC)]
    for i, u in enumerate(QKV_UNITS):
        s.append(u)
        if i >= ADA_FROM:
            s.append(("ada", 1, i - ADA_FROM))
    wo = [("wo", n, kh) for n in range(2) for kh in range(2)]
    for i in range(ITEMS):
        if i in SPLIT_WO_AT:
            s.append(wo[SPLIT_WO_AT.index(i)])
        s += [("ada", g, k) for g, k in ada_at(i)]
    s += wo[len(SPLIT_WO_AT):]
    s += FFN_UNITS
    s += [("wf", n, kh) for n in range(2) for kh in range(2)]
    return s


STREAM = stream_before_experts()
SPLIT_AT = [u for u, it in enumerate(STREAM) if it[0] != "ada"]
ADA_AT = [u for u, it in enumerate(STREAM) if it[0] == "ada"]
QKV0, WO0 = 0, len(QKV_UNITS)
FFN0 = WO0 + 4
WF0 = FFN0 + NU
MOE0 = WF0 + 4
MOE_U0 = len(STREAM)
PAIRS = N_EXP // 2
EXTRA = (2 * TOK) // (P + 1)
PER_PAIR = 2 * NU
AHEAD = 2
COMBINE_AT = (8, 11, 14, 17, 18, 20)
NEXT_SEL_AT = 21
ROWS_AT = (24, 27)
TURN_AT = (26, 29)
SELT_AT = 30


def build(nc, t):
    with ExitStack() as ctx:
        def sb(name, shape, dt=F32, stack=ctx):
            return stack.enter_context(nc.sbuf_tensor(name, shape, dt))

        def sem(name):
            return ctx.enter_context(nc.semaphore(name))

        ps = ctx.enter_context(nc.psum_tensor("ps", [P, 8, HALF], F32))

        raw = sb("raw", [P, RAW, UNIT])
        ring_hi = sb("ring_hi", [P, RING, UNIT], F32R)
        ring_lo = sb("ring_lo", [P, RING, UNIT], F32R)
        x = sb("x", [P, TILES, D])
        mrow = sb("mrow", [P, 2, HALF])
        gates = sb("gates", [P, HALF])
        lane = sb("lane", [P, 6])
        gbc = sb("gbc", [P, 2, D])
        ident = sb("ident", [P, P])
        iota = sb("iota", [P, P])
        tri = sb("tri", [P, P])
        ones = sb("ones", [P, 1])
        wr = sb("wr", [P, KC, N_EXP])
        cvecs = sb("cvecs", [16, P])
        gvecs = sb("gvecs", [33, P])
        vecsT = sb("vecsT", [P, 49])
        cond_t = sb("cond_t", [P, 2, KC])
        cond = sb("cond", [P, KC, 32])
        modv = sb("modv", [P, 6, 2, KC, 2])
        mod_a = sb("mod_a", [P, 4, KC, 2])
        sub_g = sb("sub_g", [P, 1])
        lamv = sb("lamv", [P, 4, HD])
        lams = sb("lams", [P, 4])
        junk = sb("junk", [P, HD])
        o_junk = sb("o_junk", [P, P])
        lam = sb("lam", [P, 1])
        ssq = sb("ssq", [P, 5, TILES])
        msq = sb("msq", [P, 5, TILES])
        rstd = sb("rstd", [P, 5, TILES])
        mhalf = sb("mhalf", [P, 24])
        o_ssq = sb("o_ssq", [P, TILES, HEADS])
        o_msq = sb("o_msq", [P, TILES, HEADS])
        o_rstd = sb("o_rstd", [P, TILES, HEADS])
        mx = sb("mx", [P, 2, 2])
        nmx = sb("nmx", [P, 2, 2])
        sums = sb("sums", [P, 2, 2])
        rs = sb("rs", [P, 2, 2])
        l1 = sb("l1", [P, 2])
        lmax = sb("lmax", [P, TILES])
        pr = sb("pr", [P, TILES, N_EXP])
        psumr = sb("psumr", [P, TILES])
        prec = sb("prec", [P, TILES])
        top = sb("top", [P, TILES, 8])
        topi = sb("topi", [P, TILES, 8], U32)
        topf = sb("topf", [P, TILES, 8])
        tsum = sb("tsum", [P, TILES])
        trec = sb("trec", [P, TILES])
        tg = sb("tg", [P, TILES, 2])
        oh1 = sb("oh1", [P, TILES, N_EXP])
        oh2 = sb("oh2", [P, TILES, N_EXP])
        mask = sb("mask", [P, TILES, N_EXP])
        gate = sb("gate", [P, TILES, N_EXP])
        posm = sb("posm", [P, TILES, N_EXP + 1])
        pos_col = sb("pos_col", [P, TILES])
        gate_col = sb("gate_col", [P, TILES])
        cnt = sb("cnt", [P, N_EXP])
        ext = sb("ext", [P, 2, N_EXP])
        cum = sb("cum", [P, 2, N_EXP])
        pick = sb("pick", [P, EXTRA, 2, N_EXP])
        meta_f = sb("meta_f", [P, 8])
        meta = sb("meta", [P, 8], I32)
        start = sb("start", [P, EXTRA])
        x_place = sb("x_place", [P, EXTRA, TILES])
        x_gate = sb("x_gate", [P, EXTRA, TILES])
        x_tmp = sb("x_tmp", [P, TILES, N_EXP])

        def over(stack_fn):
            with ExitStack() as s:
                return stack_fn(s)

        def phase_h(s):
            return (sb("h_hi", [P, KC, TOK], F32R, s), sb("h_lo", [P, KC, TOK], F32R, s))

        def phase_attn(s):
            return (sb("qT", [P, 2, TOK], F32, s), sb("kT", [P, 2, HALF], F32, s),
                    sb("prob", [P, 2, 2, TOK], F32, s), sb("amap", [P, 2, TOK], F32, s),
                    sb("aT", [P, 2, TOK], F32, s))

        h_hi, h_lo = over(phase_h)
        qT, kT, prob, amap, aT = over(phase_attn)

        def dense(s):
            sb("skip_h", [P, 2, KC, TOK], F32, s)
            h32 = sb("h32", [P, KC, TOK], F32, s)
            xn = sb("xn", [P, TILES, D], F32, s)
            dft_ch = sb("dft_ch", [P, 2, HALF], F32, s)
            dft_p = sb("dft_p", [P, 2, P], F32, s)
            dft_s = sb("dft_s", [P, 2, 2, 256], F32, s)
            with ExitStack() as q:
                v = sb("v", [P, TILES, D], F32, q)
                cos = sb("cos", [P, 2, HD], F32, q)
                sin = sb("sin", [P, 2, HD], F32, q)
                rope_a = sb("rope_a", [P, HALF], F32, q)
                rope_b = sb("rope_b", [P, HALF], F32, q)
            with ExitStack() as q:
                ff_hi = sb("ff_hi", [P, 2, 2, TOK], F32R, q)
                ff_lo = sb("ff_lo", [P, 2, 2, TOK], F32R, q)
                tnh = sb("tnh", [P, 2, TOK], F32, q)
                hb = sb("hb", [P, 2, TOK], F32, q)
            with ExitStack() as q:
                f_sin = sb("f_sin", [P, TILES, D], F32, q)
            return h32, xn, dft_ch, dft_p, dft_s, v, cos, sin, rope_a, rope_b, ff_hi, ff_lo, tnh, hb, f_sin

        (h32, xn, dft_ch, dft_p, dft_s, v, cos, sin, rope_a, rope_b,
         ff_hi, ff_lo, tnh, hb, f_sin) = over(dense)

        def one_or_other(s):
            with ExitStack() as q:
                xe = sb("xe", [P, 2, 2, KC, P], F32R, q)
            with ExitStack() as q:
                more = (sb("x_tok", [P, KC, P], F32, q), sb("x_hT", [P, 2, P], F32, q), sb("x_y", [P, D], F32, q))
            sb("xe_space", [P, 2, 2, KC, P], F32, s)
            return xe, more

        def experts(s):
            return (sb("tok_hi", [P, TILES, D], F32R, s), sb("tok_lo", [P, TILES, D], F32R, s),
                    sb("acc", [P, TILES, D], F32, s),
                    one_or_other(s),
                    sb("sel", [P, 2, TILES, P], F32R, s), sb("selT", [P, 2, TOK], F32R, s),
                    sb("y_hi", [P, D], F32R, s), sb("y_lo", [P, D], F32R, s),
                    sb("eh_hi", [P, 2, 2, P], F32R, s), sb("eh_lo", [P, 2, 2, P], F32R, s),
                    sb("et", [P, 2, 256], F32, s), sb("eh", [P, 2, 256], F32, s),
                    sb("gathered", [P, HALF], F32, s))

        (tok_hi, tok_lo, acc, (xe, (x_tok, x_hT, x_y)), sel, selT, y_hi, y_lo, eh_hi, eh_lo, et, eh, gathered) = over(experts)

        kbuf = h32[:].rearrange("p k m -> p (k m)").rearrange("p (t n) -> p t n", t=TILES)
        qbuf = xn
        obuf = xn
        yacc = xn
        f_cos = xn
        final_g = mrow[:, 0:2, :].rearrange("p a n -> p (a n)")

        raw_loaded = [sem(f"raw_loaded{i}") for i in range(RAW)]
        hi_ready, lo_ready, unit_used, ada_used = map(sem, ("hi_ready", "lo_ready", "unit_used", "ada_used"))
        x_loaded, cvecs_loaded, ident_loaded, lam_loaded = map(sem, ("x_loaded", "cvecs_loaded", "ident_loaded", "lam_loaded"))
        rope_loaded, cache_loaded, dft_loaded, route_loaded, final_g_loaded = map(
            sem, ("rope_loaded", "cache_loaded", "dft_loaded", "route_loaded", "final_g_loaded"))
        lane_loaded, gates_ready, gvecs_loaded, xn_last, cnt_ps, x_folded, x_scaled = map(
            sem, ("lane_loaded", "gates_ready", "gvecs_loaded", "xn_last", "cnt_ps", "x_folded", "x_scaled"))
        bias_loaded = [sem(f"bias_loaded{g}") for g in range(6)]
        const_ready, vecsT_ps, vecsT_sb, cond_tanh, cond_ready, vch, lam_exp, lam_sum = map(
            sem, ("const_ready", "vecsT_ps", "vecsT_sb", "cond_tanh", "cond_ready", "vch", "lam_exp", "lam_sum"))
        mrow_ready, modT_ps, modv_ready, mod_a_ready = map(
            sem, ("mrow_ready", "modT_ps", "modv_ready", "mod_a_ready"))
        ssq_ready, msq_ready, rstd_ready, xn_ready, xT_ps, h32_ready, h32_upper, hhi_ready, hlo_ready, x_upd = map(
            sem, ("ssq_ready", "msq_ready", "rstd_ready", "xn_ready", "xT_ps", "h32_ready", "h32_upper", "hhi_ready", "hlo_ready", "x_upd"))
        qkv_acc, qkv_sb, rope_done, ctx_stored = map(sem, ("qkv_acc", "qkv_sb", "rope_done", "ctx_stored"))
        qkT_ps, qT_sb, kT_sb, score_ps, negmax, exp_done, a_ready, aT_ps, aT_sb, o_ps, o_sb = map(
            sem, ("qkT_ps", "qT_sb", "kT_sb", "score_ps", "negmax", "exp_done", "a_ready", "aT_ps", "aT_sb", "o_ps", "o_sb"))
        o_sum, o_ms, o_rs, on_ready = map(sem, ("o_sum", "o_ms", "o_rs", "on_ready"))
        gbc_ps, gbc_sb, proj_acc = map(sem, ("gbc_ps", "gbc_sb", "proj_acc"))
        tanh_ready, ffh_ready, ffhi_ready, fflo_ready, y_ps, y_added = map(
            sem, ("tanh_ready", "ffh_ready", "ffhi_ready", "fflo_ready", "y_ps", "y_added"))
        dft1_ps, dft1_act, dft1_dve, dft2_ps, ft_hi, ft_lo = map(
            sem, ("dft1_ps", "dft1_act", "dft1_dve", "dft2_ps", "ft_hi", "ft_lo"))
        logit_ps, r_neg, r_exp, mask_ready, pos_ps = map(
            sem, ("logit_ps", "r_neg", "r_exp", "mask_ready", "pos_ps"))
        tokT_ps, tok_hi_ready, tok_lo_ready, zeroed = map(sem, ("tokT_ps", "tok_hi_ready", "tok_lo_ready", "zeroed"))
        cols_ready, sel_ready, selT_ps, selT_sb, rows_ps, rows_sb, xe_ps, xe_hi_ready, xe_lo_ready = map(
            sem, ("cols_ready", "sel_ready", "selT_ps", "selT_sb", "rows_ps", "rows_sb", "xe_ps", "xe_hi_ready",
                  "xe_lo_ready"))
        et_ready, ea_ready, eh_ready, ehT_ps, eh_hi_ready, eh_lo_ready = map(
            sem, ("et_ready", "ea_ready", "eh_ready", "ehT_ps", "eh_hi_ready", "eh_lo_ready"))
        ey_hi_ready, ey_lo_ready, comb_ps, comb_sb, y_ready, y_stored, cnt_ready, xch = map(
            sem, ("ey_hi_ready", "ey_lo_ready", "comb_ps", "comb_sb", "y_ready", "y_stored", "cnt_ready", "xch"))

        meta_ready, x_sel, x_selT_ps, x_tok_ps, x_selT_sb, x_tok_sb, x_used = map(
            sem, ("meta_ready", "x_sel", "x_selT_ps", "x_tok_ps", "x_selT_sb", "x_tok_sb", "x_used"))
        x_tanh, x_h_half, x_h, x_hT_ps, x_hT_sb, x_y_sb, x_comb_ps, x_comb_sb = map(
            sem, ("x_tanh", "x_h_half", "x_h", "x_hT_ps", "x_hT_sb", "x_y_sb", "x_comb_ps", "x_comb_sb"))
        x_loaded_w = [sem(f"x_loaded_w{i}") for i in range(RING)]

        block = ctx.enter_context(nc.Block())

        w_rows = {
            "qkv": t["w_qkv_0"].rearrange("(k p) n -> p k n", p=P),
            "wo": t["w_o_0"].rearrange("(k p) n -> p k n", p=P),
            "wf": t["w_fourier_1"].rearrange("(k p) n -> p k n", p=P),
        }
        ada_rows = [t[f"ada_w_{l}"].rearrange("(k p) n -> p k n", p=P) for l in range(2)]

        def gu_source(w, c, kh):
            return w.rearrange("(k p) (u n) -> p k u n", p=P, u=2)[:, kh * 4:kh * 4 + 4, :, c * 256:c * 256 + 256]

        def down_source(w, c):
            return w.rearrange("(s p) n -> p s n", p=P)[:, 2 * c:2 * c + 2, :]

        def slot_view(slot, kind):
            s = raw[:, slot, :]
            if kind == "gu":
                return s.rearrange("p (k u n) -> p k u n", k=4, u=2)
            if kind == "down":
                return s.rearrange("p (s n) -> p s n", s=2)
            if kind == "ada":
                return s
            return s.rearrange("p (k n) -> p k n", k=4)

        def par(j, c):
            return (FFC * j + c) % 2

        def nth(i, j, c):
            return 2 * FFC * i + FFC * j + c


        def down_used(i, j, c):
            jj, cc = (j, c - 2) if c >= 2 else (j - 1, c - 2 + FFC)
            return MOE0 + NU * jj + FFN_UNITS.index(("down", cc, 0)) + 1 + PER_PAIR * i

        GATE_BANKS = (7, 3, 4, 5)
        NORMS = ((0, 0, 0, 1, 16), (1, 1, 2, 0, 24), (3, 0, 3, 1, 32), (4, 1, 5, 0, 40))

        @block.sync
        def _(sp):
            def load(slot, kind, a, b, source=None, loaded=raw_loaded):
                dst = slot_view(slot, kind)
                if kind == "ada":
                    src = ada_rows[a // 3][:, b, (a % 3) * UNIT:(a % 3 + 1) * UNIT]
                elif kind == "gu":
                    src = gu_source(source[0], a, b)
                elif kind == "down":
                    src = down_source(source[1], a)
                else:
                    src = w_rows[kind][:, b * 4:b * 4 + 4, a * HALF:a * HALF + HALF]
                if kind == "gu":
                    for g in range(2):
                        sp.dma_start(dst[:, :, g, :], src[:, :, g, :]).then_inc(loaded[slot], 16)
                else:
                    sp.dma_start(dst, src).then_inc(loaded[slot], 16)

            for r, src in enumerate((t["c_ctx"], t["c"].rearrange("b n -> (b n)"))):
                sp.dma_start(cvecs[8 * r:8 * r + 8, :], src.rearrange("(k p) -> k p", p=P)).then_inc(cvecs_loaded, 16)
            for u, (kind, a, b) in enumerate(STREAM):
                if u >= RAW:
                    before = u - RAW
                    if STREAM[before][0] == "ada":
                        sp.wait_ge(ada_used, ADA_AT.index(before) + 1)
                    else:
                        sp.wait_ge(lo_ready, SPLIT_AT.index(before) + 1)
                load(u % RAW, kind, a, b, (t["w_gu_0"], t["w_down_0"]))
                if u == 3:
                    sp.dma_start(x[:, 0, :], t["x_prompt"].rearrange("b p n -> (b p) n")).then_inc(x_loaded, 16)
                    sp.dma_start(x[:, 1:3, :], t["x_sample"].rearrange("b (t p) n -> (b p) t n", p=P)).then_inc(x_loaded, 16)
            with sp.Fori(0, PAIRS) as i:
                for m in range(PER_PAIR):
                    kind, c, kh = FFN_UNITS[m % NU]
                    e = 2 * i + m // NU
                    u = MOE_U0 + m
                    sp.wait_ge(lo_ready, MOE0 + m - RAW + 1 + PER_PAIR * i)
                    load(u % RAW, kind, c, kh, (t["w_gu_e_1"][e], t["w_down_e_1"][e]))
            for m in range(AHEAD):
                kind, c, kh = FFN_UNITS[m]
                sp.wait_ge(lo_ready, MOE0 + PER_PAIR * PAIRS + m - RAW + 1)
                load((MOE_U0 + m) % RAW, kind, c, kh, (t["w_gu_e_1"][N_EXP - 1], None))
            sp.wait_ge(meta_ready, 1)
            blocks = sp.value_load(meta[0:1, EXTRA:EXTRA + 1], min_val=0, max_val=EXTRA)
            sp.wait_ge(lo_ready, MOE0 + PER_PAIR * PAIRS + AHEAD)
            with sp.If(blocks > 0):
                with sp.Fori(0, EXTRA) as b:
                    e = sp.value_load(meta[0:1, bass.ds(b, 1)], min_val=0, max_val=N_EXP - 1)
                    for m, (kind, c, kh) in enumerate(FFN_UNITS):
                        if m < RING:
                            sp.wait_ge(x_sel, b + 1)
                        else:
                            sp.wait_ge(x_used, NU * b + m - RING + 1)
                        load(m % RING, kind, c, kh, (t["w_gu_e_1"][e], t["w_down_e_1"][e]), x_loaded_w)
            sp.end_ifs()
            sp.wait_ge(ctx_stored, 32)
            sp.wait_ge(y_stored, 48)

        x_unit_loaded, x_slot_total = [], [0] * RING
        for m in range(NU):
            x_slot_total[m % RING] += 32 if FFN_UNITS[m][0] == "gu" else 16
            x_unit_loaded.append(x_slot_total[m % RING])

        per_slot = [0] * RAW
        loaded_at = []
        for u, (kind, a, b) in enumerate(STREAM):
            per_slot[u % RAW] += 32 if kind == "gu" else 16
            loaded_at.append(per_slot[u % RAW])
        moe_loaded, moe_slot_total = [], [0] * RAW
        for m in range(PER_PAIR):
            s = (MOE_U0 + m) % RAW
            moe_slot_total[s] += 32 if FFN_UNITS[m % NU][0] == "gu" else 16
            moe_loaded.append(per_slot[s] + moe_slot_total[s])

        def wait_loaded(eng, u):
            eng.wait_ge(raw_loaded[u % RAW], loaded_at[u])

        def wait_moe_loaded(eng, i, m):
            s = (MOE_U0 + m) % RAW
            more = moe_slot_total[s] * (m // PER_PAIR)
            eng.wait_ge(raw_loaded[s], moe_loaded[m % PER_PAIR] + more + moe_slot_total[s] * i)

        @block.gpsimd
        def _(pool):
            def load_bias(g):
                b = t[f"ada_b_{g // 3}"]
                for j in range(4):
                    src = b[(g % 3) * UNIT + j * HALF:(g % 3) * UNIT + (j + 1) * HALF]
                    pool.dma_start(mrow[32 * j:32 * j + 32, g % 2, :],
                                   src.partition_broadcast(32)).then_inc(bias_loaded[g], 16)

            pool.memset(mhalf[:], -0.5).then_inc(const_ready, 1)
            pool.memset(ones[:], 1.0).then_inc(const_ready, 1)
            load_bias(0)
            for r, name in enumerate(("lambda_q1_0", "lambda_k1_0", "lambda_q2_0", "lambda_k2_0")):
                pool.dma_start(lamv[:, r, :], t[name].partition_broadcast(P)).then_inc(lam_loaded, 16)

            chain = [0]

            def link(ins):
                chain[0] += 1
                ins.then_inc(xch, 1)
                pool.wait_ge(xch, chain[0])

            def total(out, a):
                lead = (slice(None),) * (len(a.shape) - 1)
                for w in (4, 2, 1):
                    lower, upper = a[lead + (slice(0, w),)], a[lead + (slice(w, 2 * w),)]
                    dst = lower if w > 1 else (out.unsqueeze(2) if len(a.shape) == 3 else out)
                    link(pool.tensor_tensor(dst, lower, upper, ALU.add))

            def further_blocks():
                pool.wait_ge(cnt_ready, 1)
                pool.tensor_scalar(ext[:, 0, :], cnt[:], float(P), None, ALU.is_gt)
                link(pool.tensor_scalar(ext[:, 1, :], cnt[:], float(2 * P), None, ALU.is_gt))
                link(pool.tensor_tensor(ext[:, 0, :], ext[:, 0, :], ext[:, 1, :], ALU.add))
                link(pool.tensor_copy(cum[:, 0, :], ext[:, 0, :]))
                for e in range(1, N_EXP):
                    link(pool.tensor_tensor(cum[:, 0, e:e + 1], cum[:, 0, e:e + 1], cum[:, 0, e - 1:e], ALU.add))
                link(pool.tensor_tensor(cum[:, 1, :], cum[:, 0, :], ext[:, 0, :], ALU.subtract))
                for b in range(EXTRA):
                    pool.tensor_scalar(pick[:, b, 0, :], cum[:, 0, :], float(b), None, ALU.is_gt)
                    link(pool.tensor_scalar(pick[:, b, 1, :], cum[:, 1, :], float(b), None, ALU.is_le))
                    link(pool.tensor_tensor(pick[:, b, 0, :], pick[:, b, 0, :], pick[:, b, 1, :], ALU.mult))
                    link(pool.tensor_tensor(pick[:, b, 1, :], pick[:, b, 0, :], iota[:, 0:N_EXP], ALU.mult))
                    total(meta_f[:, b:b + 1], pick[:, b, 1, :])
                    link(pool.tensor_scalar(pick[:, b, 1, :], cum[:, 1, :], float(-P), float(P * (b + 1)), ALU.mult, ALU.add))
                    link(pool.tensor_tensor(pick[:, b, 1, :], pick[:, b, 0, :], pick[:, b, 1, :], ALU.mult))
                    total(start[:, b:b + 1], pick[:, b, 1, :])
                    chosen = pick[:, b, 0, :].unsqueeze(1).to_broadcast([P, TILES, N_EXP])
                    link(pool.tensor_scalar(x_tmp[:], posm[:, :, 0:N_EXP], 1.0, None, ALU.add))
                    link(pool.tensor_tensor(x_tmp[:], x_tmp[:], chosen, ALU.mult))
                    total(x_place[:, b, :], x_tmp[:])
                    link(pool.tensor_scalar(x_place[:, b, :], x_place[:, b, :], start[:, b:b + 1], -1.0,
                                           ALU.subtract, ALU.add))
                    link(pool.tensor_tensor(x_tmp[:], gate[:], chosen, ALU.mult))
                    total(x_gate[:, b, :], x_tmp[:])
                pool.memset(meta_f[:, EXTRA + 1:8], 0.0)
                link(pool.tensor_copy(meta_f[:, EXTRA:EXTRA + 1], cum[:, 0, N_EXP - 1:N_EXP]))
                pool.tensor_copy(meta[:], meta_f[:]).then_inc(meta_ready, 1)

            def norm_pool(n):
                for k in range(TILES):
                    pool.wait_ge(ssq_ready, 3 * n + k + 1)
                    pool.tensor_scalar(msq[:, n, k:k + 1], ssq[:, n, k:k + 1], 1.0 / D, EPS,
                                       ALU.mult, ALU.add).then_inc(msq_ready, 1)
                    pool.wait_ge(msq_ready, 3 * n + k + 1)
                    pool.tensor_tensor(rstd[:, n, k:k + 1], msq[:, n, k:k + 1], mhalf[:, 0:1],
                                       ALU.pow).then_inc(rstd_ready, 1)

            pool.wait_ge(const_ready, 2)
            norm_pool(0)
            load_bias(1)
            for c, name in enumerate(("rope_cos", "rope_sin")):
                pool.dma_start((cos, sin)[c][:], t[name].rearrange("(t p) n -> p t n", p=P)).then_inc(rope_loaded, 16)
            for c, name in enumerate(("cache_k_0", "cache_v_0")):
                pool.dma_start(gbc[:, c, :], t[name].rearrange("b p h d -> (b p) (h d)")).then_inc(cache_loaded, 16)
            pool.dma_start(lane[:], t["lane"]).then_inc(lane_loaded, 16)
            pool.dma_start(dft_ch[:], t["dft_ch"].rearrange("(k p) n -> p k n", p=P)).then_inc(dft_loaded, 16)
            pool.dma_start(dft_p[:], t["dft_p"].rearrange("p (k n) -> p k n", k=2)).then_inc(dft_loaded, 16)
            pool.dma_start(dft_s[:], t["dft_s"].rearrange("(k p) (c n) -> p k c n", p=P, c=2)).then_inc(dft_loaded, 16)
            pool.dma_start(iota[:], t["iota"]).then_inc(route_loaded, 16)
            pool.dma_start(tri[:], t["tri"]).then_inc(route_loaded, 16)
            pool.dma_start(wr[:], t["w_router_1"].rearrange("(k p) n -> p k n", p=P)).then_inc(route_loaded, 16)
            pool.wait_ge(modv_ready, 1)
            load_bias(2)
            pool.wait_ge(qkv_sb, 3 * 3 + 1)
            pool.dma_start(t["k_ctx"], kbuf[:, 0, :]).then_inc(ctx_stored, 16)
            pool.wait_ge(qkv_sb, 3 * 5 + 1)
            pool.dma_start(t["v_ctx"], v[:, 0, :]).then_inc(ctx_stored, 16)
            for i in range(ITEMS):
                if i in (1, 4, 10):
                    g = 3 + (1, 4, 10).index(i)
                    pool.wait_ge(modv_ready, g - 1)
                    load_bias(g)
                h, k = i // TILES, i % TILES
                pool.wait_ge(o_sum, i + 1)
                pool.tensor_scalar(o_msq[:, k, h:h + 1], o_ssq[:, k, h:h + 1], 1.0 / P, SUBLN_EPS,
                                   ALU.mult, ALU.add).then_inc(o_ms, 1)
                pool.wait_ge(o_ms, i + 1)
                pool.tensor_tensor(o_rstd[:, k, h:h + 1], o_msq[:, k, h:h + 1], mhalf[:, 0:1],
                                   ALU.pow).then_inc(o_rs, 1)
                pool.wait_ge(o_rs, i + 1)
                rows = obuf[:, k, h * P:(h + 1) * P]
                pool.tensor_scalar(rows, rows, o_rstd[:, k, h:h + 1], None, ALU.mult).then_inc(on_ready, 1)
            norm_pool(1)
            pool.wait_ge(modv_ready, 6)
            pool.dma_start(final_g, t["final_norm_g"].partition_broadcast(P)).then_inc(final_g_loaded, 16)
            norm_pool(2)
            norm_pool(3)
            pool.wait_ge(tokT_ps, 2 * TILES)
            for buf in (acc[:], y_hi[:].bitcast(F32), y_lo[:].bitcast(F32), selT[:, 1, :].bitcast(F32), gate_col[:]):
                pool.memset(buf, 0.0).then_inc(zeroed, 1)
            further_blocks()
            pool.wait_ge(gbc_sb, 16)
            pool.wait_ge(comb_sb, 6 * N_EXP)
            for n in range(6):
                k, cols = n // 2, slice((n % 2) * HALF, (n % 2 + 1) * HALF)
                link(pool.tensor_tensor(acc[:, k, cols], acc[:, k, cols], gbc[:, COND[k], cols], ALU.mult))
                pool.tensor_tensor(x[:, k, cols], x[:, k, cols], acc[:, k, cols], ALU.add).then_inc(x_folded, 1)
            norm_pool(4)

        @block.scalar
        def _(act):
            act.dma_start(ident[:], t["ident"]).then_inc(ident_loaded, 16)
            row = 0
            for name, n in (("norm1_g_0", 8), ("norm2_g_0", 8), ("norm1_g_1", 8), ("norm2_g_1", 8), ("subln_g_0", 1)):
                act.dma_start(gvecs[row:row + n, :], t[name].rearrange("(k p) -> k p", p=P)).then_inc(gvecs_loaded, 16)
                row += n

            def split_hi(s):
                u = SPLIT_AT[s]
                wait_loaded(act, u)
                if s >= RING:
                    act.wait_ge(unit_used, s - RING + 1)
                act.activation(ring_hi[:, s % RING, :], raw[:, u % RAW, :], ACT.Copy).then_inc(hi_ready, 1)

            def x_ready(n, k):
                if n == 0:
                    act.wait_ge(x_loaded, 32)
                else:
                    act.wait_ge(x_upd, 6 * (n - 1) + (3 + k + 1 if n % 2 else 2 * k + 2))

            def norm_rows(n):
                def square(k):
                    x_ready(n, k)
                    act.activation(xn[:, k, :], x[:, k, :], ACT.Square,
                                   accum_out=ssq[:, n, k:k + 1]).then_inc(ssq_ready, 1)

                def scaled(k):
                    act.wait_ge(rstd_ready, 3 * n + k + 1)
                    act.activation(xn[:, k, :], x[:, k, :], ACT.Copy, scale=rstd[:, n, k:k + 1]).then_inc(xn_ready, 1)

                square(0)
                square(1)
                scaled(0)
                square(2)
                scaled(1)

            def modulate(n, turned, split, behind=1):
                gs, vs = NORMS[n][0:2]
                act.wait_ge(mod_a_ready, n + 1)
                for k in range(TILES):
                    act.wait_ge(xT_ps, 3 * turned + k + 1)
                    for q in range(4, KC):
                        ins = act.activation(h32[:, q, k * P:(k + 1) * P],
                                             ps[:, 2 * k + 1, (q - 4) * P:(q - 3) * P], ACT.Identity,
                                             scale=mod_a[:, n, q, COND[k]:COND[k] + 1],
                                             bias=modv[:, gs, vs, q, COND[k]:COND[k] + 1])
                    ins.then_inc(h32_upper, 1)
                    if split is not None and k >= behind:
                        high_part(n, split, k - behind)
                if split is not None and behind:
                    high_part(n, split, TILES - 1)

            def high_part(n, split, k):
                act.wait_ge(h32_ready, 3 * n + k + 1)
                act.wait_ge(h32_upper, 3 * n + k + 1)
                act.activation(h_hi[:, :, k * P:(k + 1) * P], h32[:, :, k * P:(k + 1) * P],
                               ACT.Copy).then_inc(hhi_ready, 1)

            def keep_gate(q, j, bank=7):
                act.wait_ge(x_upd, 6 * q) if q else act.wait_ge(o_sb, 24)
                act.wait_ge(gbc_ps, 4 * q + j + 1)
                act.activation(gbc[:, j // 2, (j % 2) * HALF:(j % 2 + 1) * HALF], ps[:, bank, :],
                               ACT.Copy).then_inc(gbc_sb, 1)

            act.wait_ge(vecsT_sb, 1)
            act.activation(cond_t[:].rearrange("p c k -> p (c k)"), vecsT[:, 0:16], ACT.Tanh,
                           scale=0.5).then_inc(cond_tanh, 1)
            act.wait_ge(lam_sum, 2)
            act.activation(lams[:, 2:4], lams[:, 0:2], ACT.Exp).then_inc(lam_exp, 1)

            norm_rows(0)
            split_hi(QKV0)
            modulate(0, 0, 0, behind=0)

            split_hi(QKV0 + 1)
            for s in range(len(QKV_UNITS) + 1):
                if s + 2 < len(QKV_UNITS):
                    split_hi(QKV0 + s + 2)
                if s and QKV_UNITS[s - 1][2] == 1:
                    n = QKV_UNITS[s - 1][1]
                    dst = (qbuf, kbuf, v)[n // 2]
                    for k in range(TILES):
                        if k < 2:
                            act.wait_ge(qkv_acc, 2 * n + k + 1)
                        else:
                            act.wait_ge(unit_used, s)
                        act.activation(dst[:, k, (n % 2) * HALF:(n % 2 + 1) * HALF],
                                       ps[:, (n % 2) * 3 + k, :], ACT.Copy).then_inc(qkv_sb, 1)

            def keys_turned(h):
                act.wait_ge(qkT_ps, h + 1)
                if h >= 2:
                    act.wait_ge(score_ps, 3 * (h - 1))
                act.activation(kT[:, h % 2, :], ps[:, 6, :], ACT.Copy).then_inc(kT_sb, 1)

            def exps(i):
                n = P if i % 3 == 0 else TOK
                act.wait_ge(negmax, i + 1)
                if i >= 2:
                    act.wait_ge(a_ready, i - 1)
                for m in range(2):
                    ins = act.activation(prob[:, i % 2, m, 0:n], ps[:, 2 * (i % 2) + m, 0:n], ACT.Exp,
                                         bias=nmx[:, i % 2, m:m + 1], scale=SCALE,
                                         accum_out=sums[:, i % 2, m:m + 1])
                ins.then_inc(exp_done, 1)

            def map_turned(i):
                n = P if i % 3 == 0 else TOK
                act.wait_ge(aT_ps, i + 1)
                if i >= 2:
                    act.wait_ge(o_ps, i - 1)
                act.activation(aT[:, i % 2, 0:n], ps[:, 4, 0:n], ACT.Copy).then_inc(aT_sb, 1)

            keys_turned(0)
            exps(0)
            for i in range(ITEMS + 3):
                if 1 <= i <= ITEMS:
                    map_turned(i - 1)
                if i + 1 < ITEMS:
                    exps(i + 1)
                if i % 3 == 0 and i // 3 + 1 < HEADS:
                    keys_turned(i // 3 + 1)
                if i >= 3:
                    h, k = (i - 3) // TILES, (i - 3) % TILES
                    act.wait_ge(o_sb, i - 2)
                    if i > 3:
                        act.wait_ge(o_sum, i - 3)
                    act.activation(o_junk[:], obuf[:, k, h * P:(h + 1) * P], ACT.Square,
                                   accum_out=o_ssq[:, k, h:h + 1]).then_inc(o_sum, 1)
                if i in SPLIT_WO_AT:
                    split_hi(WO0 + SPLIT_WO_AT.index(i))
            for k in range(TILES):
                act.wait_ge(xT_ps, 3 + k + 1)
                for q in range(2):
                    ins = act.activation(h_hi[:, 4 * q:4 * q + 4, k * P:(k + 1) * P],
                                         ps[:, 2 * k + q, :].rearrange("p (q n) -> p q n", q=4), ACT.Copy,
                                         scale=sub_g[:, 0:1])
                ins.then_inc(hhi_ready, 1)
            for j in range(4):
                keep_gate(0, j)
            for s in range(WO0 + 3, FFN0 + 2):
                split_hi(s)

            act.wait_ge(ctx_stored, 32)
            norm_rows(1)
            modulate(1, 2, 2)
            for s in range(NU + 1):
                if s and FFN_UNITS[s - 1][0] == "gu" and FFN_UNITS[s - 1][2] == 1:
                    c = FFN_UNITS[s - 1][1]
                    act.wait_ge(unit_used, FFN0 + s)
                    if c:
                        act.wait_ge(ffh_ready, 2 * c)
                    for j in range(2):
                        act.activation(tnh[:, j, :], ps[:, 2 * j, 0:TOK], ACT.Tanh, scale=0.5).then_inc(tanh_ready, 1)
                    if c >= 2:
                        act.wait_ge(unit_used, FFN0 + FFN_UNITS.index(("down", c - 2, 0)) + 1)
                    for j in range(2):
                        act.wait_ge(ffh_ready, 2 * c + j + 1)
                        act.activation(ff_hi[:, c % 2, j, :], hb[:, j, :], ACT.Copy).then_inc(ffhi_ready, 1)
                if s + 2 < NU:
                    split_hi(FFN0 + s + 2)
                if 2 <= s < 6:
                    keep_gate(1, s - 2)
            norm_rows(2)
            modulate(2, 3, None)
            split_hi(WF0)
            split_hi(WF0 + 1)

            for n in range(0, 12, 2):
                k, g = n // 4, n % 4
                act.wait_ge(dft1_ps, n + 1)
                act.wait_ge(xT_ps, 3 * 3 + 3)
                act.activation(f_cos[:, k, g * 256:(g + 1) * 256], ps[:, n % 6, 0:256], ACT.Copy)
                act.activation(f_sin[:, k, g * 256:(g + 1) * 256], ps[:, n % 6, 256:512], ACT.Copy).then_inc(dft1_act, 1)
            for k in range(KC):
                act.wait_ge(dft2_ps, k + 1)
                act.activation(h_hi[:, k, :], ps[:, k % 6, 0:TOK], ACT.Copy).then_inc(ft_hi, 1)
            split_hi(WF0 + 2)
            for j in range(4):
                keep_gate(2, j)
            split_hi(WF0 + 3)

            def hi(i, m):
                wait_moe_loaded(act, i, m)
                s = MOE0 + m
                act.wait_ge(unit_used, s - RING + 1 + PER_PAIR * i)
                act.activation(ring_hi[:, s % RING, :], raw[:, (MOE_U0 + m) % RAW, :], ACT.Copy).then_inc(hi_ready, 1)

            norm_rows(3)
            modulate(3, 4, None)
            for m in range(AHEAD):
                hi(0, m)
            act.wait_ge(r_neg, 1)
            for k in range(TILES):
                act.activation(pr[:, k, :], ps[:, 6, k * N_EXP:(k + 1) * N_EXP], ACT.Exp, bias=lmax[:, k:k + 1],
                               accum_out=psumr[:, k:k + 1]).then_inc(r_exp, 1)
            for n in range(2 * TILES):
                act.wait_ge(tokT_ps, n + 1)
                act.activation(tok_hi[:, n // 2, (n % 2) * HALF:(n % 2 + 1) * HALF], ps[:, n, :],
                               ACT.Copy).then_inc(tok_hi_ready, 1)

            keep_gate(3, 0, GATE_BANKS[0])

            def keep_rows(e, half):
                act.wait_ge(rows_ps, 2 * e + half + 1)
                if half:
                    act.wait_ge(xe_ps, 2 * e + 1)
                act.activation(gathered[:], ps[:, 6, :], ACT.Copy).then_inc(rows_sb, 1)

            def high_xe(e, b, half):
                act.wait_ge(xe_ps, 2 * e + half + 1)
                act.activation(xe[:, b, 0, 4 * half:4 * half + 4, :], ps[:, 7, :].rearrange("p (k n) -> p k n", k=4),
                               ACT.Copy).then_inc(xe_hi_ready, 1)

            def keep_selT(e, b):
                act.wait_ge(selT_ps, e + 1)
                act.activation(selT[:, b, :], ps[:, 6, 0:TOK], ACT.Copy).then_inc(selT_sb, 1)

            for half in range(2):
                keep_rows(0, half)
                high_xe(0, 0, half)
            keep_selT(0, 0)
            for j in range(1, 4):
                keep_gate(3, j, GATE_BANKS[j])
            act.wait_ge(zeroed, 5)

            with act.Fori(0, PAIRS) as i:
                def high_eh(j, c):
                    act.wait_ge(ehT_ps, nth(i, j, c) + 1)
                    act.wait_ge(unit_used, down_used(i, j, c))
                    act.activation(eh_hi[:, par(j, c), :, :],
                                   ps[:, 2 + par(j, c), 0:256].rearrange("p (s n) -> p s n", s=2),
                                   ACT.Copy).then_inc(eh_hi_ready, 1)

                for m in range(PER_PAIR + 1):
                    if m:
                        j, (kind, c, kh) = (m - 1) // NU, FFN_UNITS[(m - 1) % NU]
                        if kind == "gu" and kh == 1:
                            act.wait_ge(unit_used, MOE0 + m + PER_PAIR * i)
                            act.activation(et[:, par(j, c), :], ps[:, par(j, c), 0:256], ACT.Tanh,
                                           scale=0.5).then_inc(et_ready, 1)
                        if kind == "down" and c == FFC - 1:
                            act.wait_ge(unit_used, MOE0 + m + PER_PAIR * i)
                            act.wait_ge(comb_ps, 12 * i + 6 * j + 6)
                            act.activation(y_hi[:].rearrange("p (a n) -> p a n", a=2), ps[:, 4:6, :],
                                           ACT.Copy).then_inc(ey_hi_ready, 1)
                    if m == PER_PAIR:
                        break
                    j, (kind, c, kh) = m // NU, FFN_UNITS[m % NU]
                    if kind == "gu" and kh == 1 and c >= 1:
                        high_eh(j, c - 1)
                    if kind == "down" and c == FFC - 1:
                        high_eh(j, c)
                    hi(i, m + AHEAD)
                    e, b, at = 2 * i + j + 1, 1 - j, m % NU
                    if at in ROWS_AT:
                        keep_rows(e, ROWS_AT.index(at))
                    if at in TURN_AT:
                        high_xe(e, b, TURN_AT.index(at))
                    if at == SELT_AT:
                        keep_selT(e, b)

            act.wait_ge(meta_ready, 1)
            blocks = act.value_load(meta[0:1, EXTRA:EXTRA + 1], min_val=0, max_val=EXTRA)
            with act.If(blocks > 0):
                with act.Fori(0, EXTRA) as b:
                    act.wait_ge(x_selT_ps, b + 1)
                    act.activation(selT[:, 0, :], ps[:, 2, 0:TOK], ACT.Copy).then_inc(x_selT_sb, 1)
                    act.wait_ge(x_tok_ps, b + 1)
                    act.activation(x_tok[:].rearrange("p (a k) n -> p a (k n)", a=2), ps[:, 0:2, :],
                                   ACT.Copy).then_inc(x_tok_sb, 1)
                    for m, (kind, c, kh) in enumerate(FFN_UNITS):
                        if (kind == "gu" and kh == 1 and c) or (kind == "down" and c == FFC - 1):
                            cc = c - 1 if kind == "gu" else c
                            act.wait_ge(x_hT_ps, FFC * b + cc + 1)
                            act.activation(x_hT[:], ps[:, 0, 0:256].rearrange("p (s n) -> p s n", s=2),
                                           ACT.Copy).then_inc(x_hT_sb, 1)
                        if kind == "gu" and kh == 1:
                            act.wait_ge(x_used, NU * b + m + 1)
                            act.activation(et[:, 0, :], ps[:, 3, 0:256], ACT.Tanh, scale=0.5).then_inc(x_tanh, 1)
                    act.wait_ge(x_used, NU * b + NU)
                    act.activation(x_y[:].rearrange("p (a n) -> p a n", a=2), ps[:, 4:6, :],
                                   ACT.Copy).then_inc(x_y_sb, 1)
                act.wait_ge(x_comb_sb, 6 * EXTRA)
            act.end_ifs()

            for k in range(TILES):
                act.wait_ge(comb_sb, 6 * N_EXP + 2 * k + 2)
                act.activation(acc[:, k, :], x[:, k, :], ACT.Square,
                               accum_out=ssq[:, 4, k:k + 1]).then_inc(ssq_ready, 1)
            yp = t["y_prompt"].rearrange("b p n -> (b p) n")
            ysm = t["y_sample"].rearrange("b (t p) n -> t (b p) n", p=P)
            for k in range(TILES):
                act.wait_ge(y_ready, k + 1)
                act.dma_start(yp if k == 0 else ysm[k - 1], acc[:, k, :]).then_inc(y_stored, 16)

        @block.vector
        def _(dve):
            chain = [0]

            def link(ins):
                chain[0] += 1
                ins.then_inc(vch, 1)
                dve.wait_ge(vch, chain[0])

            def split_lo(s):
                u = SPLIT_AT[s]
                dve.wait_ge(hi_ready, s + 1)
                dve.tensor_tensor(ring_lo[:, s % RING, :], raw[:, u % RAW, :],
                                  ring_hi[:, s % RING, :].bitcast(F32), ALU.subtract).then_inc(lo_ready, 1)

            dve.wait_ge(vecsT_ps, 1)
            dve.tensor_copy(vecsT[:, 0:16], ps[:, 6, 0:16]).then_inc(vecsT_sb, 1)
            dve.wait_ge(cond_tanh, 1)
            link(dve.scalar_tensor_tensor(cond_t[:].rearrange("p c k -> p (c k)"),
                                          cond_t[:].rearrange("p c k -> p (c k)"), 1.0,
                                          vecsT[:, 0:16], ALU.add, ALU.mult))
            dve.tensor_scalar(cond[:].rearrange("p k (r c) -> p k r c", c=2),
                              cond_t[:].rearrange("p c k -> p k c").unsqueeze(2).to_broadcast([P, KC, 16, 2]),
                              0.5, None, ALU.mult).then_inc(cond_ready, 1)
            dve.wait_ge(vecsT_ps, 2)
            link(dve.tensor_copy(vecsT[:, 16:49], ps[:, 6, 16:49]))
            dve.tensor_scalar(sub_g[:], vecsT[:, 48:49], 1.0 - LAMBDA_INIT, None, ALU.mult)
            dve.wait_ge(lam_loaded, 64)
            for r in range(2):
                dve.tensor_tensor_reduce(junk[:], lamv[:, 2 * r, :], lamv[:, 2 * r + 1, :], 1.0, 0.0,
                                         ALU.mult, ALU.add, lams[:, r:r + 1]).then_inc(lam_sum, 1)
                dve.wait_ge(lam_sum, r + 1)
            dve.wait_ge(lam_exp, 1)
            link(dve.tensor_scalar(lam[:], lams[:, 2:3], lams[:, 3:4], LAMBDA_INIT, ALU.subtract, ALU.add))

            def ada_rows_out(g):
                dve.wait_ge(ada_used, KC * (g + 1))
                dve.wait_ge(bias_loaded[g], 64)
                dve.tensor_tensor(mrow[:, g % 2, :], ps[:, 7, :], mrow[:, g % 2, :], ALU.add).then_inc(mrow_ready, 1)
                if g in GATE_GROUPS:
                    n = GATE_GROUPS.index(g)
                    dve.wait_ge(mrow_ready, g + 1)
                    if n == 0:
                        dve.wait_ge(lane_loaded, 16)
                        ins = dve.tensor_scalar(gates[:], mrow[:, g % 2, :], lane[:, g:g + 1], None, ALU.mult)
                    else:
                        dve.wait_ge(gates_ready, n)
                        ins = dve.scalar_tensor_tensor(gates[:], mrow[:, g % 2, :], lane[:, g:g + 1], gates[:],
                                                       ALU.mult, ALU.add)
                    ins.then_inc(gates_ready, 1)

            def ada_cols_out(g):
                dve.wait_ge(modT_ps, g + 1)
                src = ps[:, 7, :].rearrange("p (q j r) -> p q j r", q=4, j=4)
                for c in range(2):
                    ins = dve.tensor_copy(
                        modv[:, g, :, :, c].rearrange("p v (h q) -> p (v h) q", h=2).rearrange("p j q -> p q j"),
                        src[:, :, :, c])
                ins.then_inc(modv_ready, 1)

            def scale_last(n):
                dve.wait_ge(rstd_ready, 3 * n + 3)
                dve.tensor_scalar(xn[:, 2, :], x[:, 2, :], rstd[:, n, 2:3], None, ALU.mult).then_inc(xn_last, 1)

            scale_last(0)
            ada_rows_out(0)
            ada_cols_out(0)

            def low_parts(split):
                def low(k):
                    dve.wait_ge(hhi_ready, 3 * split + k + 1)
                    dve.tensor_tensor(h_lo[:, :, k * P:(k + 1) * P], h32[:, :, k * P:(k + 1) * P],
                                      h_hi[:, :, k * P:(k + 1) * P].bitcast(F32), ALU.subtract).then_inc(hlo_ready, 1)
                return low

            def norm_dve(n, turned, split, meanwhile=None):
                gs, vs, gc, vc, row = NORMS[n]
                dve.wait_ge(modv_ready, max(gs, gc) + 1)
                for c in range(2):
                    ins = dve.scalar_tensor_tensor(mod_a[:, n, :, c], modv[:, gc, vc, :, c], 1.0,
                                                   vecsT[:, row:row + KC], ALU.add, ALU.mult)
                ins.then_inc(mod_a_ready, 1)
                dve.wait_ge(mod_a_ready, n + 1)
                low = low_parts(split) if split is not None else (lambda k: None)
                for k in range(TILES):
                    dve.wait_ge(xT_ps, 3 * turned + k + 1)
                    for q in range(4):
                        ins = dve.tensor_scalar(h32[:, q, k * P:(k + 1) * P],
                                                ps[:, 2 * k, q * P:(q + 1) * P],
                                                mod_a[:, n, q, COND[k]:COND[k] + 1],
                                                modv[:, gs, vs, q, COND[k]:COND[k] + 1], ALU.mult, ALU.add)
                    ins.then_inc(h32_ready, 1)
                    if n and k == 0:
                        scale_last(n)
                    if meanwhile:
                        if k == 0:
                            meanwhile()
                        low(k)
                    elif k:
                        low(k - 1)
                if not meanwhile:
                    low(TILES - 1)

            norm_dve(0, 0, 0, lambda: split_lo(QKV0))

            def rope(n):
                buf = (qbuf, kbuf)[n // 2]
                for k in (1, 2):
                    xs = buf[:, k, (n % 2) * HALF:(n % 2 + 1) * HALF]
                    dve.wait_ge(qkv_sb, 3 * n + k + 1)
                    if n == 0 and k == 1:
                        dve.wait_ge(rope_loaded, 32)
                    g8 = lambda a: a.rearrange("p (g d) -> p g d", d=HD)
                    table = lambda a: a[:, k - 1, :].unsqueeze(1).to_broadcast([P, 8, HD])
                    dve.tensor_tensor(g8(rope_a[:]), g8(xs), table(cos), ALU.mult)
                    halves = lambda a: a.rearrange("p g (a f r) -> p g a f r", a=2, f=2)
                    for f in range(2):
                        for a in range(2):
                            ins = dve.tensor_tensor(halves(g8(rope_b[:]))[:, :, a, f, :], halves(g8(xs))[:, :, a, 1 - f, :],
                                                    halves(table(sin))[:, :, a, f, :], ALU.mult)
                    link(ins)
                    dve.tensor_tensor(xs, rope_a[:], rope_b[:], ALU.add).then_inc(rope_done, 1)
                    dve.wait_ge(rope_done, 2 * n + k)

            split_lo(QKV0 + 1)
            for s in range(len(QKV_UNITS) + 2):
                if s + 2 < len(QKV_UNITS):
                    split_lo(QKV0 + s + 2)
                if 2 <= s < 10 and s % 2 == 0:
                    rope(s // 2 - 1)

            def queries_turned(h):
                dve.wait_ge(qkT_ps, h + 1)
                if h >= 2:
                    dve.wait_ge(score_ps, 3 * (h - 1))
                dve.tensor_copy(qT[:, h % 2, :], ps[:, 5, 0:TOK]).then_inc(qT_sb, 1)

            def row_max(i):
                n = P if i % 3 == 0 else TOK
                dve.wait_ge(score_ps, i + 1)
                link(dve.tensor_reduce(mx[:, i % 2, :], ps[:, 2 * (i % 2):2 * (i % 2) + 2, 0:n], AX.X, ALU.max))
                dve.tensor_scalar(nmx[:, i % 2, :], mx[:, i % 2, :], -SCALE, None, ALU.mult).then_inc(negmax, 1)

            def difference(i):
                n = P if i % 3 == 0 else TOK
                dve.wait_ge(exp_done, i + 1)
                link(dve.reciprocal(rs[:, i % 2, :], sums[:, i % 2, :]))
                link(dve.tensor_scalar(l1[:, i % 2:i % 2 + 1], rs[:, i % 2, 1:2], lam[:, 0:1], None, ALU.mult))
                link(dve.tensor_scalar(prob[:, i % 2, 1, 0:n], prob[:, i % 2, 1, 0:n], l1[:, i % 2:i % 2 + 1], None, ALU.mult))
                if i >= 2:
                    dve.wait_ge(aT_ps, i - 1)
                dve.scalar_tensor_tensor(amap[:, i % 2, 0:n], prob[:, i % 2, 0, 0:n], rs[:, i % 2, 0:1],
                                         prob[:, i % 2, 1, 0:n], ALU.mult, ALU.subtract).then_inc(a_ready, 1)

            def out_rows(i):
                h, k = i // 3, i % 3
                dve.wait_ge(o_ps, i + 1)
                dve.tensor_copy(obuf[:, k, h * P:(h + 1) * P], ps[:, 5, TOK:HALF]).then_inc(o_sb, 1)

            ada_rows_out(1)
            ada_cols_out(1)
            queries_turned(0)
            row_max(0)
            for i in range(ITEMS + 3):
                if i + 1 < ITEMS:
                    row_max(i + 1)
                if i < ITEMS:
                    difference(i)
                if i >= 3:
                    out_rows(i - 3)
                group = ada_complete(i)
                if group is not None:
                    ada_rows_out(group)
                if i % 3 == 0 and i // 3 + 1 < HEADS:
                    queries_turned(i // 3 + 1)
                if group is not None:
                    ada_cols_out(group)
                if i in SPLIT_WO_AT:
                    split_lo(WO0 + SPLIT_WO_AT.index(i))

            for k in range(TILES):
                dve.wait_ge(hhi_ready, 3 + k + 1)
                for q in range(2):
                    part = (slice(None), slice(4 * q, 4 * q + 4), slice(k * P, (k + 1) * P))
                    ins = dve.scalar_tensor_tensor(h_lo[part], ps[:, 2 * k + q, :].rearrange("p (q n) -> p q n", q=4),
                                                   sub_g[:, 0:1], h_hi[part].bitcast(F32), ALU.mult, ALU.subtract)
                ins.then_inc(hlo_ready, 1)

            def add_projection(w, n, first):
                for k in range(TILES):
                    if k < 2:
                        dve.wait_ge(proj_acc, 4 * w + 2 * n + k + 1)
                    else:
                        dve.wait_ge(unit_used, first + 2 * n + 2)
                    if n == 0 and k == 0:
                        dve.wait_ge(gbc_sb, 4 * (2 * w + 1))
                    cols = slice(n * HALF, (n + 1) * HALF)
                    link(dve.tensor_tensor(xn[:, k, cols], ps[:, n * 3 + k, :], gbc[:, COND[k], cols], ALU.mult))
                    dve.tensor_tensor(x[:, k, cols], x[:, k, cols], xn[:, k, cols], ALU.add).then_inc(x_upd, 1)

            split_lo(WO0 + 3)
            add_projection(0, 0, WO0)
            split_lo(FFN0)
            split_lo(FFN0 + 1)
            add_projection(0, 1, WO0)

            dve.wait_ge(ctx_stored, 32)
            norm_dve(1, 2, 2)

            def low_hidden(c):
                for j in range(2):
                    dve.wait_ge(ffhi_ready, 2 * c + j + 1)
                    dve.tensor_tensor(ff_lo[:, c % 2, j, :], hb[:, j, :], ff_hi[:, c % 2, j, :].bitcast(F32),
                                      ALU.subtract).then_inc(fflo_ready, 1)

            def add_y(c, n):
                k, half = n // 2, n % 2
                if n < 5:
                    dve.wait_ge(y_ps, 5 * c + n + 1)
                else:
                    dve.wait_ge(unit_used, FFN0 + FFN_UNITS.index(("down", c, 0)) + 1)
                dst = yacc[:, k, half * HALF:(half + 1) * HALF]
                if c == 0:
                    dve.tensor_copy(dst, ps[:, 4 + n % 3, :]).then_inc(y_added, 1)
                else:
                    dve.wait_ge(y_added, 6 * (c - 1) + n + 1)
                    dve.tensor_tensor(dst, ps[:, 4 + n % 3, :], dst, ALU.add).then_inc(y_added, 1)

            for s in range(NU + 1):
                prev = FFN_UNITS[s - 1] if s else None
                if prev is not None and prev[0] == "gu" and prev[2] == 1:
                    c = prev[1]
                    for j in range(2):
                        dve.wait_ge(tanh_ready, 2 * c + j + 1)
                        if c:
                            dve.wait_ge(fflo_ready, 2 * (c - 1) + j + 1)
                        link(dve.scalar_tensor_tensor(hb[:, j, :], tnh[:, j, :], 1.0, ps[:, 2 * j, 0:TOK],
                                                      ALU.add, ALU.mult))
                        dve.scalar_tensor_tensor(hb[:, j, :], hb[:, j, :], 0.5, ps[:, 2 * j + 1, 0:TOK],
                                                 ALU.mult, ALU.mult).then_inc(ffh_ready, 1)
                    for n in range(6 if c else 0):
                        if n == 3:
                            low_hidden(c)
                        add_y(c - 1, n)
                    if c == 0:
                        low_hidden(c)
                if s + 2 < NU:
                    split_lo(FFN0 + s + 2)
            def add_gated(buf, n):
                k, cols = n // 2, slice((n % 2) * HALF, (n % 2 + 1) * HALF)
                link(dve.tensor_tensor(buf[:, k, cols], buf[:, k, cols], gbc[:, COND[k], cols], ALU.mult))
                dve.tensor_tensor(x[:, k, cols], x[:, k, cols], buf[:, k, cols], ALU.add).then_inc(x_upd, 1)

            dve.wait_ge(gbc_sb, 8)
            for n in range(6):
                add_y(FFC - 1, n)
                dve.wait_ge(y_added, 6 * (FFC - 1) + n + 1)
                add_gated(yacc, n)

            norm_dve(2, 3, None)

            for n in range(1, 12, 2):
                k, g = n // 4, n % 4
                dve.wait_ge(dft1_ps, n + 1)
                dve.tensor_copy(f_cos[:, k, g * 256:(g + 1) * 256], ps[:, n % 6, 0:256])
                dve.tensor_copy(f_sin[:, k, g * 256:(g + 1) * 256], ps[:, n % 6, 256:512]).then_inc(dft1_dve, 1)
            split_lo(WF0)
            split_lo(WF0 + 1)
            for k in range(KC):
                dve.wait_ge(ft_hi, k + 1)
                dve.tensor_tensor(h_lo[:, k, :], ps[:, k % 6, 0:TOK], h_hi[:, k, :].bitcast(F32),
                                  ALU.subtract).then_inc(ft_lo, 1)
            split_lo(WF0 + 2)
            split_lo(WF0 + 3)
            add_projection(1, 0, WF0)
            add_projection(1, 1, WF0)
            norm_dve(3, 4, None)

            def lo(i, m):
                s = MOE0 + m
                dve.wait_ge(hi_ready, s + 1 + PER_PAIR * i)
                dve.tensor_tensor(ring_lo[:, s % RING, :], raw[:, (MOE_U0 + m) % RAW, :],
                                  ring_hi[:, s % RING, :].bitcast(F32), ALU.subtract).then_inc(lo_ready, 1)

            for m in range(AHEAD):
                lo(0, m)

            dve.wait_ge(logit_ps, 1)
            dve.wait_ge(route_loaded, 48)
            link(dve.tensor_reduce(lmax[:], ps[:, 6, 0:24].rearrange("p (t e) -> p t e", t=TILES), AX.X, ALU.max))
            dve.tensor_scalar(lmax[:], lmax[:], -1.0, None, ALU.mult).then_inc(r_neg, 1)
            dve.wait_ge(r_exp, TILES)
            link(dve.reciprocal(prec[:], psumr[:]))
            per_expert = lambda a: a.unsqueeze(2).to_broadcast([P, TILES, N_EXP])
            link(dve.tensor_tensor(pr[:], pr[:], per_expert(prec[:]), ALU.mult))
            for k in range(TILES):
                ins = dve.max(top[:, k, :], pr[:, k, :])
            link(ins)
            for k in range(TILES):
                dve.max_index(topi[:, k, :], top[:, k, :], pr[:, k, :])
            link(dve.tensor_tensor(tsum[:], top[:, :, 0], top[:, :, 1], ALU.add))
            dve.reciprocal(trec[:], tsum[:])
            link(dve.tensor_copy(topf[:], topi[:]))
            numbers = iota[:, 0:N_EXP].unsqueeze(1).to_broadcast([P, TILES, N_EXP])
            dve.tensor_tensor(oh1[:], numbers, per_expert(topf[:, :, 0]), ALU.is_equal)
            link(dve.tensor_tensor(oh2[:], numbers, per_expert(topf[:, :, 1]), ALU.is_equal))
            dve.tensor_tensor(mask[:], oh1[:], oh2[:], ALU.add).then_inc(mask_ready, 1)
            link(dve.tensor_tensor(tg[:], top[:, :, 0:2], trec[:].unsqueeze(2).to_broadcast([P, TILES, 2]), ALU.mult))
            dve.tensor_tensor(oh1[:], oh1[:], per_expert(tg[:, :, 0]), ALU.mult)
            link(dve.tensor_tensor(oh2[:], oh2[:], per_expert(tg[:, :, 1]), ALU.mult))
            dve.tensor_tensor(gate[:], oh1[:], oh2[:], ALU.add)
            def low_tokens(n):
                dve.wait_ge(tok_hi_ready, n + 1)
                cols = slice((n % 2) * HALF, (n % 2 + 1) * HALF)
                dve.tensor_tensor(tok_lo[:, n // 2, cols], ps[:, n, :], tok_hi[:, n // 2, cols].bitcast(F32),
                                  ALU.subtract).then_inc(tok_lo_ready, 1)

            for n in range(3):
                low_tokens(n)
            link(dve.memset(posm[:, :, N_EXP:], -1.0))
            dve.wait_ge(mask_ready, 1)
            dve.wait_ge(pos_ps, 1)
            link(dve.scalar_tensor_tensor(posm[:, :, 0:N_EXP], ps[:, 6, 0:24].rearrange("p (t e) -> p t e", t=TILES), 1.0,
                                          mask[:], ALU.add, ALU.mult))
            link(dve.tensor_scalar(posm[:, :, 0:N_EXP], posm[:, :, 0:N_EXP], -1.0, None, ALU.add))

            def select(e, b):
                dve.tensor_copy(pos_col[:], posm[:, :, bass.ds(e, 1)].rearrange("p t e -> p (t e)")).then_inc(cols_ready, 1)
                dve.wait_ge(cols_ready, e + 1)
                for k in range(TILES):
                    ins = dve.tensor_scalar(sel[:, b, k, :], iota[:], pos_col[:, k:k + 1], None, ALU.is_equal)
                ins.then_inc(sel_ready, 1)

            def low_xe(e, b, half):
                dve.wait_ge(xe_hi_ready, 2 * e + half + 1)
                ks = slice(4 * half, 4 * half + 4)
                dve.tensor_tensor(xe[:, b, 1, ks, :], ps[:, 7, :].rearrange("p (k n) -> p k n", k=4),
                                  xe[:, b, 0, ks, :].bitcast(F32), ALU.subtract).then_inc(xe_lo_ready, 1)

            dve.wait_ge(tokT_ps, 2 * TILES)
            select(0, 0)
            for n in range(3, 2 * TILES):
                low_tokens(n)
            low_xe(0, 0, 0)
            low_xe(0, 0, 1)
            dve.wait_ge(cnt_ps, 1)
            dve.tensor_copy(cnt[:], ps[:, 2, 0:N_EXP]).then_inc(cnt_ready, 1)
            dve.wait_ge(zeroed, 5)

            def combine(e, n):
                k, half = n // 2, n % 2
                cols = slice(half * HALF, (half + 1) * HALF)
                dve.wait_ge(comb_ps, 6 * e + n + 1)
                dve.scalar_tensor_tensor(acc[:, k, cols], ps[:, 6 + half, :], gate_col[:, k:k + 1],
                                         acc[:, k, cols], ALU.mult, ALU.add).then_inc(comb_sb, 1)

            with dve.Fori(0, PAIRS) as i:
                def low_eh(j, c):
                    dve.wait_ge(eh_hi_ready, nth(i, j, c) + 1)
                    b = par(j, c)
                    dve.tensor_tensor(eh_lo[:, b, :, :], ps[:, 2 + b, 0:256].rearrange("p (s n) -> p s n", s=2),
                                      eh_hi[:, b, :, :].bitcast(F32), ALU.subtract).then_inc(eh_lo_ready, 1)

                for m in range(PER_PAIR + 1):
                    if m:
                        j, (kind, c, kh) = (m - 1) // NU, FFN_UNITS[(m - 1) % NU]
                        n, b = nth(i, j, c), par(j, c)
                        if kind == "gu" and kh == 1:
                            dve.wait_ge(et_ready, n + 1)
                            dve.scalar_tensor_tensor(eh[:, b, :], et[:, b, :], 1.0, ps[:, b, 0:256],
                                                     ALU.add, ALU.mult).then_inc(ea_ready, 1)
                            dve.wait_ge(ea_ready, n + 1)
                            dve.scalar_tensor_tensor(eh[:, b, :], eh[:, b, :], 0.5, ps[:, b, 256:512],
                                                     ALU.mult, ALU.mult).then_inc(eh_ready, 1)
                        if kind == "down" and c == FFC - 1:
                            dve.wait_ge(ey_hi_ready, 2 * i + j + 1)
                            dve.tensor_tensor(y_lo[:].rearrange("p (a n) -> p a n", a=2), ps[:, 4:6, :],
                                              y_hi[:].rearrange("p (a n) -> p a n", a=2).bitcast(F32),
                                              ALU.subtract).then_inc(ey_lo_ready, 1)
                    if m == PER_PAIR:
                        break
                    j, (kind, c, kh) = m // NU, FFN_UNITS[m % NU]
                    if kind == "gu" and kh == 1 and c >= 1:
                        low_eh(j, c - 1)
                    if kind == "down" and c == FFC - 1:
                        low_eh(j, c)
                    if m % NU != NU - 2:
                        if m % NU == NU - 1:
                            lo(i, m - 1 + AHEAD)
                        lo(i, m + AHEAD)
                    e, b, at = 2 * i + j + 1, 1 - j, m % NU
                    if at in COMBINE_AT:
                        combine(e - 1, COMBINE_AT.index(at))
                    if at == NEXT_SEL_AT:
                        dve.wait_ge(comb_sb, 6 * e)
                        dve.wait_ge(selT_ps, e)
                        dve.tensor_copy(gate_col[:], gate[:, :, bass.ds(e - 1, 1)].rearrange("p t e -> p (t e)"))
                        select(e, b)
                    if at in TURN_AT:
                        low_xe(e, b, TURN_AT.index(at))

            def add_to_x(n, count, added):
                k, half = n // 2, n % 2
                cols = slice(half * HALF, (half + 1) * HALF)
                dve.scalar_tensor_tensor(acc[:, k, cols], ps[:, 6 + half, :], gate_col[:, k:k + 1],
                                         gbc[:, COND[k], cols], ALU.mult, ALU.mult).then_inc(x_scaled, 1)
                dve.wait_ge(x_scaled, count)
                dve.tensor_tensor(x[:, k, cols], x[:, k, cols], acc[:, k, cols], ALU.add).then_inc(added, 1)

            dve.wait_ge(x_folded, 6)
            for n in range(6):
                dve.wait_ge(comb_ps, 6 * N_EXP + n + 1)
                add_to_x(n, n + 1, comb_sb)
            dve.wait_ge(comb_sb, 6 * N_EXP + 6)
            dve.wait_ge(meta_ready, 1)
            blocks = dve.value_load(meta[0:1, EXTRA:EXTRA + 1], min_val=0, max_val=EXTRA)
            with dve.If(blocks > 0):
                with dve.Fori(0, EXTRA) as b:
                    dve.tensor_copy(pos_col[:], x_place[:, bass.ds(b, 1), :].rearrange("p b t -> p (b t)"))
                    dve.tensor_copy(gate_col[:],
                                    x_gate[:, bass.ds(b, 1), :].rearrange("p b t -> p (b t)")).then_inc(cols_ready, 1)
                    dve.wait_ge(cols_ready, N_EXP + 1 + b + 1)
                    for k in range(TILES):
                        ins = dve.tensor_scalar(sel[:, 0, k, :], iota[:], pos_col[:, k:k + 1], None, ALU.is_equal)
                    ins.then_inc(x_sel, 1)
                    for c in range(FFC):
                        dve.wait_ge(x_tanh, FFC * b + c + 1)
                        if c:
                            dve.wait_ge(x_hT_ps, FFC * b + c)
                        dve.scalar_tensor_tensor(eh[:, 0, :], et[:, 0, :], 1.0, ps[:, 3, 0:256],
                                                 ALU.add, ALU.mult).then_inc(x_h_half, 1)
                        dve.wait_ge(x_h_half, FFC * b + c + 1)
                        dve.scalar_tensor_tensor(eh[:, 0, :], eh[:, 0, :], 0.5, ps[:, 3, 256:512],
                                                 ALU.mult, ALU.mult).then_inc(x_h, 1)
                    for n in range(6):
                        dve.wait_ge(x_comb_ps, 6 * b + n + 1)
                        add_to_x(n, 6 * b + n + 7, x_comb_sb)
                    dve.wait_ge(x_comb_sb, 6 * b + 6)
            dve.end_ifs()
            dve.wait_ge(final_g_loaded, 16)
            for k in range(TILES):
                dve.wait_ge(rstd_ready, 12 + k + 1)
                dve.scalar_tensor_tensor(acc[:, k, :], x[:, k, :], rstd[:, 4, k:k + 1], final_g,
                                         ALU.mult, ALU.mult).then_inc(y_ready, 1)

        @block.tensor
        def _(pe):
            def mm3(out, l_hi, l_lo, r_hi, r_lo, first, last):
                pe.matmul(out, l_hi, r_hi, start=first, stop=False)
                pe.matmul(out, l_lo, r_hi, start=False, stop=False)
                return pe.matmul(out, l_hi, r_lo, start=False, stop=last)

            def ada_unit(g, k):
                n = KC * g + k
                u = ADA_AT[n]
                wait_loaded(pe, u)
                if k == 0 and g:
                    pe.wait_ge(modv_ready, g)
                for j in range(4):
                    ins = pe.matmul(ps[32 * j:32 * j + 32, 7, :], cond[:, k, :],
                                    raw[:, u % RAW, j * HALF:(j + 1) * HALF], start=(k == 0), stop=(k == KC - 1))
                ins.then_inc(ada_used, 1)

            def ada_turn(g):
                pe.wait_ge(mrow_ready, g + 1)
                for q in range(4):
                    ins = pe.transpose(ps[:, 7, q * P:(q + 1) * P], mrow[:, g % 2, q * P:(q + 1) * P], ident[:])
                ins.then_inc(modT_ps, 1)

            pe.wait_ge(ident_loaded, 16)
            pe.wait_ge(cvecs_loaded, 2 * 16)
            pe.transpose(ps[:, 6, 0:16], cvecs[:], ident[0:16, 0:16]).then_inc(vecsT_ps, 1)
            pe.wait_ge(cond_ready, 1)
            for k in range(KC):
                ada_unit(0, k)
                if k == 2:
                    pe.wait_ge(gvecs_loaded, 5 * 16)
                    pe.transpose(ps[:, 6, 16:49], gvecs[:], ident[0:33, 0:33]).then_inc(vecsT_ps, 1)

            def turn_rows(wait):
                for k in range(TILES):
                    wait(k)
                    for q in range(KC):
                        ins = pe.transpose(ps[:, 2 * k + q // 4, (q % 4) * P:(q % 4 + 1) * P],
                                           xn[:, k, q * P:(q + 1) * P], ident[:])
                    ins.then_inc(xT_ps, 1)

            def turn_normed(n):
                turn_rows(lambda k: pe.wait_ge(xn_ready, 2 * n + k + 1) if k < 2 else pe.wait_ge(xn_last, n + 1))

            def spread_gate(q, j, bank=7):
                layer, second = q // 2, q % 2
                g = 3 * layer + 1 + second
                pe.wait_ge(gates_ready, GATE_GROUPS.index(g) + 1)
                if bank == 7 and (q or j):
                    pe.wait_ge(gbc_sb, 4 * q + j)
                elif bank == 7:
                    pe.wait_ge(modv_ready, 6)
                c, half = j // 2, j % 2
                row = 32 * (2 * second + half) + 2 * g + c
                pe.matmul(ps[:, bank, :], ident[:, row:row + 1].to_broadcast([P, P]), gates[:],
                          start=True, stop=True).then_inc(gbc_ps, 1)

            turn_normed(0)
            ada_turn(0)

            def project(first, n, kh, s, banks, acc_sem, acc_base, hsem, hbase, after_tile=None):
                pe.wait_ge(lo_ready, first + s + 1)
                slot = (first + s) % RING
                for k in range(TILES):
                    if hsem is not None:
                        pe.wait_ge(hsem, hbase + k + 1)
                    for q in range(4):
                        kc = kh * 4 + q
                        cols = slice(k * P, (k + 1) * P)
                        ins = mm3(ps[:, banks + k, :], h_hi[:, kc, cols], h_lo[:, kc, cols],
                                  ring_hi[:, slot, q * HALF:(q + 1) * HALF], ring_lo[:, slot, q * HALF:(q + 1) * HALF],
                                  kh == 0 and q == 0, kh == 1 and q == 3)
                    if kh == 1 and k < 2:
                        ins.then_inc(acc_sem, 1)
                    if k == TILES - 1:
                        ins.then_inc(unit_used, 1)
                    if after_tile:
                        after_tile(k)

            for s, (_, n, kh) in enumerate(QKV_UNITS):
                if kh == 0 and n >= 2:
                    pe.wait_ge(qkv_sb, 3 * (n - 1))
                project(QKV0, n, kh, s, (n % 2) * 3, qkv_acc, 2 * n, hlo_ready if s == 0 else None, 0)
                if s >= ADA_FROM:
                    ada_unit(1, s - ADA_FROM)

            def turn_heads(h):
                if h:
                    pe.wait_ge(qT_sb, h)
                    pe.wait_ge(kT_sb, h)
                else:
                    pe.wait_ge(qkv_sb, 18)
                    pe.wait_ge(rope_done, 8)
                    pe.wait_ge(cache_loaded, 32)
                if h > 1:
                    pe.wait_ge(o_sb, 3 * h - 5)
                cols = slice(h * P, (h + 1) * P)
                for k in range(TILES):
                    pe.transpose(ps[:, 5, k * P:(k + 1) * P], qbuf[:, k, cols], ident[:])
                    pe.transpose(ps[:, 6, k * P:(k + 1) * P], kbuf[:, k, cols], ident[:])
                pe.transpose(ps[:, 6, TOK:HALF], gbc[:, 0, cols], ident[:]).then_inc(qkT_ps, 1)

            def scores(i):
                h, k = i // 3, i % 3
                pe.wait_ge(qT_sb, h + 1)
                pe.wait_ge(kT_sb, h + 1)
                if i >= 2:
                    pe.wait_ge(exp_done, i - 1)
                keys = slice(0, P) if k == 0 else slice(P, HALF)
                for m in range(2):
                    rows = slice(HD * m, HD * m + HD)
                    ins = pe.matmul(ps[:, 2 * (i % 2) + m, 0:(P if k == 0 else TOK)],
                                    qT[rows, h % 2, k * P:(k + 1) * P], kT[rows, h % 2, keys], start=True, stop=True)
                ins.then_inc(score_ps, 1)

            def turn_map(i):
                pe.wait_ge(a_ready, i + 1)
                if i:
                    pe.wait_ge(aT_sb, i)
                for b in range(1 if i % 3 == 0 else 3):
                    ins = pe.transpose(ps[:, 4, b * P:(b + 1) * P], amap[:, i % 2, b * P:(b + 1) * P], ident[:])
                ins.then_inc(aT_ps, 1)

            def values(i):
                h, k = i // 3, i % 3
                cols = slice(h * P, (h + 1) * P)
                pe.wait_ge(aT_sb, i + 1)
                if i:
                    pe.wait_ge(o_sb, i)
                pe.wait_ge(qT_sb, min((i + 5) // 3, HEADS - 1) + 1)
                vs = [v[:, 0, cols]] if k == 0 else [v[:, 1, cols], v[:, 2, cols], gbc[:, 1, cols]]
                for b, vb in enumerate(vs):
                    ins = pe.matmul(ps[:, 5, TOK:HALF], aT[:, i % 2, b * P:(b + 1) * P], vb,
                                    start=(b == 0), stop=(b == len(vs) - 1))
                ins.then_inc(o_ps, 1)

            ada_turn(1)
            turn_heads(0)
            scores(0)
            scores(1)
            for i in range(ITEMS + 2):
                if 1 <= i <= ITEMS:
                    turn_map(i - 1)
                if i + 2 < ITEMS:
                    scores(i + 2)
                if ada_complete(i) is not None:
                    ada_turn(ada_complete(i))
                if i % 3 == 0 and i // 3 + 1 < HEADS:
                    turn_heads(i // 3 + 1)
                for g, k in ada_at(i):
                    ada_unit(g, k)
                if i >= 2:
                    values(i - 2)
            turn_rows(lambda k: pe.wait_ge(on_ready, ITEMS - TILES + k + 1))
            spread_gate(0, 0)

            def projection(first, w, hsem, hbase):
                for s in range(4):
                    n, kh = s // 2, s % 2
                    project(first, n, kh, s, 3 * n, proj_acc, 4 * w + 2 * n, hsem if s == 0 else None, hbase,
                            None if s else (lambda k: spread_gate(2 * w, k + 1)))

            projection(WO0, 0, hlo_ready, 3)
            turn_normed(1)

            pe.wait_ge(hhi_ready, 9)
            pe.wait_ge(lo_ready, FFN0 + 1)
            for part, weights in ((h_hi, (ring_hi, ring_lo)), (h_lo, (ring_hi,))):
                if part is h_lo:
                    pe.wait_ge(hlo_ready, 9)
                for q in range(4):
                    for b in range(4):
                        w = q * HALF + (b % 2) * 256 + (b // 2) * P
                        for weight in weights:
                            ins = pe.matmul(ps[:, b, 0:TOK], weight[:, FFN0 % RING, w:w + P], part[:, q, :],
                                            start=(q == 0 and part is h_hi and weight is ring_hi), stop=False)
            ins.then_inc(unit_used, 1)

            for s, (kind, c, kh) in enumerate(FFN_UNITS):
                if s == 0:
                    continue
                pe.wait_ge(lo_ready, FFN0 + s + 1)
                slot = (FFN0 + s) % RING
                if kind == "gu":
                    if kh == 0 and c:
                        pe.wait_ge(ffh_ready, 2 * c)
                    for q in range(4):
                        for b in range(4):
                            w = q * HALF + (b % 2) * 256 + (b // 2) * P
                            cols = slice(w, w + P)
                            kc = kh * 4 + q
                            ins = mm3(ps[:, b, 0:TOK], ring_hi[:, slot, cols], ring_lo[:, slot, cols],
                                      h_hi[:, kc, :], h_lo[:, kc, :], kh == 0 and q == 0, kh == 1 and q == 3)
                else:
                    pe.wait_ge(fflo_ready, 2 * c + 2)
                    for n in range(6):
                        k, half = n // 2, n % 2
                        if 6 * c + n >= 3:
                            pe.wait_ge(y_added, 6 * c + n - 2)
                        for j in range(2):
                            cols = slice(k * P, (k + 1) * P)
                            w = slice(j * D + half * HALF, j * D + (half + 1) * HALF)
                            ins = mm3(ps[:, 4 + n % 3, :], ff_hi[:, c % 2, j, cols], ff_lo[:, c % 2, j, cols],
                                      ring_hi[:, slot, w], ring_lo[:, slot, w], j == 0, j == 1)
                        if n < 5:
                            ins.then_inc(y_ps, 1)
                ins.then_inc(unit_used, 1)
                if 1 <= s < 5:
                    spread_gate(1, s - 1)

            turn_normed(2)
            pe.wait_ge(h32_ready, 9)
            pe.wait_ge(h32_upper, 9)
            pe.wait_ge(dft_loaded, 48)
            for n in range(12):
                k, g = n // 4, n % 4
                if n >= 6:
                    pe.wait_ge(dft1_act if n % 2 == 0 else dft1_dve, (n - 6) // 2 + 1)
                for q in range(2):
                    ins = pe.matmul(ps[:, n % 6, :], h32[:, 2 * g + q, k * P:(k + 1) * P], dft_ch[:, q, :],
                                    start=(q == 0), stop=(q == 1))
                ins.then_inc(dft1_ps, 1)
            pe.wait_ge(dft1_act, 6)
            pe.wait_ge(dft1_dve, 6)
            for q in range(KC):
                cols = slice(q * P, (q + 1) * P)
                if q >= 6:
                    pe.wait_ge(ft_lo, q - 5)
                pe.matmul(ps[:, q % 6, 0:P], f_cos[:, 0, cols], dft_p[:, 0, :], start=True, stop=False)
                pe.matmul(ps[:, q % 6, 0:P], f_sin[:, 0, cols], dft_p[:, 1, :], start=False, stop=True)
                for k in range(2):
                    pe.matmul(ps[:, q % 6, P:TOK], f_cos[:, 1 + k, cols], dft_s[:, k, 0, :], start=(k == 0), stop=False)
                    ins = pe.matmul(ps[:, q % 6, P:TOK], f_sin[:, 1 + k, cols], dft_s[:, k, 1, :],
                                    start=False, stop=(k == 1))
                ins.then_inc(dft2_ps, 1)
            pe.wait_ge(ft_lo, KC)
            spread_gate(2, 0)
            projection(WF0, 1, None, 0)
            turn_normed(3)

            pe.wait_ge(route_loaded, 48)
            for k in range(TILES):
                pe.wait_ge(h32_ready, 9 + k + 1)
                pe.wait_ge(h32_upper, 9 + k + 1)
                for q in range(KC):
                    ins = pe.matmul(ps[:, 6, k * N_EXP:(k + 1) * N_EXP], h32[:, q, k * P:(k + 1) * P], wr[:, q, :],
                                    start=(q == 0), stop=(q == KC - 1))
            ins.then_inc(logit_ps, 1)

            def turn_back(n):
                for q in range(4):
                    ins = pe.transpose(ps[:, n, q * P:(q + 1) * P],
                                       h32[:, 4 * (n % 2) + q, (n // 2) * P:(n // 2 + 1) * P], ident[:])
                ins.then_inc(tokT_ps, 1)

            for n in range(4):
                turn_back(n)
            pe.wait_ge(mask_ready, 1)
            pe.wait_ge(const_ready, 2)
            for k in range(TILES):
                out = ps[:, 6, k * N_EXP:(k + 1) * N_EXP]
                for b in range(k):
                    pe.matmul(out, ones[:].to_broadcast([P, P]), mask[:, b, :], start=(b == 0), stop=False)
                ins = pe.matmul(out, tri[:], mask[:, k, :], start=(k == 0), stop=True)
            ins.then_inc(pos_ps, 1)
            for n in range(4, 2 * TILES):
                turn_back(n)
            spread_gate(3, 0, GATE_BANKS[0])

            def gather_rows(e, b, half):
                if half:
                    pe.wait_ge(rows_sb, 2 * e + 1)
                else:
                    pe.wait_ge(sel_ready, e + 1)
                for r, part in enumerate((tok_hi, tok_lo)):
                    pe.wait_ge(tok_lo_ready if r else tok_hi_ready, 6)
                    for k in range(TILES):
                        ins = pe.matmul(ps[:, 6, :], sel[:, b, k, :], part[:, k, half * HALF:(half + 1) * HALF],
                                        start=(r == 0 and k == 0), stop=(r == 1 and k == TILES - 1))
                ins.then_inc(rows_ps, 1)

            def turn_gathered(e, half):
                pe.wait_ge(rows_sb, 2 * e + half + 1)
                if half:
                    pe.wait_ge(xe_lo_ready, 2 * e + 1)
                for q in range(4):
                    ins = pe.transpose(ps[:, 7, q * P:(q + 1) * P], gathered[:, q * P:(q + 1) * P], ident[:])
                ins.then_inc(xe_ps, 1)

            def turn_selection(e, b):
                for k in range(TILES):
                    ins = pe.transpose(ps[:, 6, k * P:(k + 1) * P], sel[:, b, k, :].bitcast(F32), ident[:])
                ins.then_inc(selT_ps, 1)

            def bring_back(e, b, n):
                k, half = n // 2, n % 2
                if k:
                    pe.wait_ge(comb_sb, 6 * e + n - 1)
                for r, part in enumerate((y_hi, y_lo)):
                    ins = pe.matmul(ps[:, 6 + half, :], selT[:, b, k * P:(k + 1) * P],
                                    part[:, half * HALF:(half + 1) * HALF], start=(r == 0), stop=(r == 1))
                ins.then_inc(comb_ps, 1)

            gather_rows(0, 0, 0)
            pe.wait_ge(gbc_sb, 13)
            turn_gathered(0, 0)
            gather_rows(0, 0, 1)
            turn_gathered(0, 1)
            turn_selection(0, 0)
            for j in range(1, 4):
                spread_gate(3, j, GATE_BANKS[j])
            for k in range(TILES):
                ins = pe.matmul(ps[:, 2, 0:N_EXP], ones[:].to_broadcast([P, P]), mask[:, k, :],
                                start=(k == 0), stop=(k == TILES - 1))
            ins.then_inc(cnt_ps, 1)
            pe.wait_ge(xe_lo_ready, 2)
            pe.wait_ge(selT_sb, 1)
            pe.wait_ge(zeroed, 5)

            with pe.Fori(0, PAIRS) as i:
                def turn_hidden(j, c):
                    b = par(j, c)
                    pe.wait_ge(eh_ready, nth(i, j, c) + 1)
                    for s in range(2):
                        ins = pe.transpose(ps[:, 2 + b, s * P:(s + 1) * P], eh[:, b, s * P:(s + 1) * P], ident[:])
                    ins.then_inc(ehT_ps, 1)

                for m in range(PER_PAIR):
                    j, at = m // NU, m % NU
                    kind, c, kh = FFN_UNITS[at]
                    n, b, e = nth(i, j, c), par(j, c), 2 * i + j
                    if m == 2:
                        pe.wait_ge(gbc_sb, 16)
                    if kind == "gu" and kh == 1 and c >= 1:
                        turn_hidden(j, c - 1)
                    if kind == "down" and c == FFC - 1:
                        turn_hidden(j, c)
                    if at in COMBINE_AT:
                        if at == COMBINE_AT[0]:
                            pe.wait_ge(selT_sb, e + 1)
                        bring_back(e, 1 - j, COMBINE_AT.index(at))
                    if at in ROWS_AT:
                        gather_rows(e + 1, 1 - j, ROWS_AT.index(at))
                    if at in TURN_AT:
                        turn_gathered(e + 1, TURN_AT.index(at))
                    if at == SELT_AT:
                        turn_selection(e + 1, 1 - j)
                    pe.wait_ge(lo_ready, MOE0 + m + 1 + PER_PAIR * i)
                    slot = (MOE0 + m) % RING
                    if kind == "gu":
                        if c == 0 and kh == 0:
                            pe.wait_ge(xe_lo_ready, 2 * e + 2)
                        for q in range(4):
                            kc = kh * 4 + q
                            ins = mm3(ps[:, b, :], xe[:, j, 0, kc, :], xe[:, j, 1, kc, :],
                                      ring_hi[:, slot, q * HALF:(q + 1) * HALF], ring_lo[:, slot, q * HALF:(q + 1) * HALF],
                                      kh == 0 and q == 0, kh == 1 and q == 3)
                    else:
                        pe.wait_ge(eh_lo_ready, n + 1)
                        for s in range(2):
                            for half in range(2):
                                w = slice(s * D + half * HALF, s * D + (half + 1) * HALF)
                                ins = mm3(ps[:, 4 + half, :], eh_hi[:, b, s, :], eh_lo[:, b, s, :],
                                          ring_hi[:, slot, w], ring_lo[:, slot, w],
                                          c == 0 and s == 0, c == FFC - 1 and s == 1)
                    ins.then_inc(unit_used, 1)

            pe.wait_ge(ey_lo_ready, N_EXP)
            for n in range(6):
                bring_back(N_EXP, 1, n)
            pe.wait_ge(meta_ready, 1)
            blocks = pe.value_load(meta[0:1, EXTRA:EXTRA + 1], min_val=0, max_val=EXTRA)
            pe.wait_ge(comb_sb, 6 * N_EXP + 6)
            with pe.If(blocks > 0):
                with pe.Fori(0, EXTRA) as b:
                    pe.wait_ge(x_sel, b + 1)
                    for k in range(TILES):
                        ins = pe.transpose(ps[:, 2, k * P:(k + 1) * P], sel[:, 0, k, :].bitcast(F32), ident[:])
                    ins.then_inc(x_selT_ps, 1)
                    for q in range(KC):
                        for r, part in enumerate((tok_hi, tok_lo)):
                            for k in range(TILES):
                                ins = pe.matmul(ps[:, q // 4, (q % 4) * P:(q % 4 + 1) * P],
                                                part[:, k, q * P:(q + 1) * P], sel[:, 0, k, :],
                                                start=(r == 0 and k == 0), stop=(r == 1 and k == TILES - 1))
                    ins.then_inc(x_tok_ps, 1)
                    pe.wait_ge(x_tok_sb, b + 1)
                    pe.wait_ge(x_selT_sb, b + 1)

                    def turn_extra(c):
                        pe.wait_ge(x_h, FFC * b + c + 1)
                        for s in range(2):
                            ins = pe.transpose(ps[:, 0, s * P:(s + 1) * P], eh[:, 0, s * P:(s + 1) * P], ident[:])
                        ins.then_inc(x_hT_ps, 1)

                    for m, (kind, c, kh) in enumerate(FFN_UNITS):
                        if kind == "gu" and kh == 0 and c:
                            turn_extra(c - 1)
                        if kind == "down" and c == FFC - 1:
                            turn_extra(c)
                        slot = m % RING
                        pe.wait_ge(x_loaded_w[slot], x_unit_loaded[m] + x_slot_total[slot] * b)
                        if kind == "gu":
                            for q in range(4):
                                ins = pe.matmul(ps[:, 3, :], x_tok[:, kh * 4 + q, :],
                                                raw[:, slot, q * HALF:(q + 1) * HALF],
                                                start=(kh == 0 and q == 0), stop=(kh == 1 and q == 3))
                        else:
                            pe.wait_ge(x_hT_sb, FFC * b + c + 1)
                            for s in range(2):
                                for half in range(2):
                                    w = slice(s * D + half * HALF, s * D + (half + 1) * HALF)
                                    ins = pe.matmul(ps[:, 4 + half, :], x_hT[:, s, :], raw[:, slot, w],
                                                    start=(c == 0 and s == 0), stop=(c == FFC - 1 and s == 1))
                        ins.then_inc(x_used, 1)
                    pe.wait_ge(x_y_sb, b + 1)
                    for n in range(6):
                        k, half = n // 2, n % 2
                        if n >= 2:
                            pe.wait_ge(x_comb_sb, 6 * b + n - 1)
                        pe.matmul(ps[:, 6 + n % 2, :], selT[:, 0, k * P:(k + 1) * P].bitcast(F32),
                                  x_y[:, half * HALF:(half + 1) * HALF], start=True, stop=True).then_inc(x_comb_ps, 1)
            pe.end_ifs()


_INS = ["x_prompt", "x_sample", "c", "cache_k_0", "cache_v_0", "c_ctx",
        "ada_w_0", "ada_b_0", "norm1_g_0", "norm2_g_0", "w_qkv_0",
        "lambda_q1_0", "lambda_k1_0", "lambda_q2_0", "lambda_k2_0", "subln_g_0", "w_o_0",
        "w_gu_0", "w_down_0", "ada_w_1", "ada_b_1", "norm1_g_1", "norm2_g_1", "w_fourier_1",
        "w_router_1", "w_gu_e_1", "w_down_e_1", "final_norm_g"]
_OUTS = [("y_prompt", (1, 128, 1024)), ("y_sample", (1, 256, 1024)),
         ("k_ctx", (1, 128, 8, 128)), ("v_ctx", (1, 128, 8, 128))]


def shape_constants():
    f = np.float32
    rows = 256 // 64
    row = np.repeat(np.arange(rows), 64).astype(f)
    col = np.tile(np.arange(64), rows).astype(f)
    inv = (f(1.0) / (f(10000.0) ** (np.arange(0, 32, 2, dtype=f) / f(32)))).astype(f)
    ar, ac = row[:, None] * inv[None, :], col[:, None] * inv[None, :]
    ang = np.concatenate([ar, ar, ac, ac], axis=-1).astype(np.float64)
    sign = np.tile(np.repeat([-1.0, 1.0], 16), 2)

    def wave(n):
        a = 2 * np.pi * (np.outer(np.arange(n), np.arange(n)) % n) / n
        return np.cos(a), np.sin(a)

    c256, s256 = wave(256)
    c128, s128 = wave(128)
    return {
        "ident": np.eye(128, dtype=f),
        "lane": (np.arange(128)[:, None] % 32 // 2 == np.arange(6)[None, :]).astype(f),
        "iota": np.tile(np.arange(128, dtype=f), (128, 1)),
        "tri": np.triu(np.ones((128, 128), f), 1),
        "rope_cos": np.cos(ang).astype(f),
        "rope_sin": (np.sin(ang) * sign).astype(f),
        "dft_ch": (np.concatenate([c256, s256], axis=1) / 16).astype(f),
        "dft_p": (np.concatenate([c128, -s128], axis=1) / np.sqrt(128)).astype(f),
        "dft_s": (np.concatenate([c256, -s256], axis=1) / 16).astype(f),
    }


def kernel(**inputs):
    import concourse.bacc as bacc
    from concourse.bass_utils import run_bass_kernel_spmd

    nc = bacc.Bacc("TRN2", target_bir_lowering=False, num_devices=1)
    arrays, args = {}, {}
    for name, a in list((n, inputs[n]) for n in _INS) + list(shape_constants().items()):
        a = np.ascontiguousarray(a)
        arrays[f"in_{name}"] = a
        args[name] = nc.dram_tensor(f"in_{name}", a.shape, mybir.dt.from_np(a.dtype), kind="ExternalInput").ap()
    for name, shape in _OUTS:
        out = nc.dram_tensor(f"out_{name}", shape, F32, kind="ExternalOutput").ap()
        args[name] = out.rearrange("b p h d -> (b p) (h d)") if len(shape) == 4 else out
    build(nc, args)
    r = run_bass_kernel_spmd(nc, [arrays], core_ids=[0])
    return tuple(np.asarray(r.results[0][f"out_{name}"]) for name, _ in _OUTS)
```
